# Optimizing a Trainium2 kernel written in Bass

```python
import jax, jax.numpy as jnp
from jax import lax
import numpy as np

D_MODEL = 1024
BATCH = 1
SEQ = 512
DEPTH = 1

GLA_HEADS = 4
GLA_DK = 128
GLA_DV = 256
GLA_GATE_RANK = 16
GLA_GATE_NORM = 16.0
GLA_CHUNK = 64
SWA_HEADS = 16
SWA_KV_HEADS = 4
SWA_HEAD_DIM = 64
SWA_WINDOW = 128
SWA_BLOCK = 128
ROPE_THETA = 500000.0
ROPE_DIM = SWA_HEAD_DIM // 4
PEER_HEADS = 8
PEER_NKEYS = 128
PEER_EXPERTS = PEER_NKEYS * PEER_NKEYS
PEER_QDIM = 256
PEER_TOPK = 16
PEER_TOKEN_BLOCK = 128
NORM_EPS = 1e-6

GLA_KW = GLA_HEADS * GLA_DK
GLA_VW = GLA_HEADS * GLA_DV
SWA_QW = SWA_HEADS * SWA_HEAD_DIM
SWA_KVW = SWA_KV_HEADS * SWA_HEAD_DIM
IN_SPLITS = (GLA_KW, GLA_KW, GLA_VW, GLA_VW, GLA_GATE_RANK, SWA_QW, SWA_KVW, SWA_KVW, D_MODEL, D_MODEL)
IN_WIDTH = sum(IN_SPLITS)
IN_SPLIT_POINTS = tuple(int(v) for v in np.cumsum(IN_SPLITS)[:-1])


def rmsnorm(x, g):
    xf = x.astype(jnp.float32)
    y = xf * lax.rsqrt(jnp.mean(xf * xf, axis=-1, keepdims=True) + NORM_EPS)
    return (y * g.astype(jnp.float32)).astype(x.dtype)

def rope_tables(seqlen):
    pos = jnp.arange(seqlen, dtype=jnp.float32)
    inv_freq = ROPE_THETA ** (-jnp.arange(0, ROPE_DIM, 2, dtype=jnp.float32) / ROPE_DIM)
    ang = pos[:, None] * inv_freq[None, :]
    return jnp.cos(ang), jnp.sin(ang)

def partial_rope(x, cos, sin):
    half = ROPE_DIM // 2
    xf = x.astype(jnp.float32)
    x1, x2, rest = xf[..., :half], xf[..., half:ROPE_DIM], xf[..., ROPE_DIM:]
    c, s = cos[:, None, :], sin[:, None, :]
    return jnp.concatenate([x1 * c - x2 * s, x2 * c + x1 * s, rest], axis=-1).astype(x.dtype)

def gla_chunked(q, k, v, log_a):
    bsz, seqlen, nh, dk = q.shape
    dv = v.shape[-1]
    c = GLA_CHUNK
    n = seqlen // c

    def to_chunks(t):
        return t.astype(jnp.float32).reshape(bsz, n, c, nh, t.shape[-1]).transpose(0, 3, 1, 2, 4)

    qc = to_chunks(q) * (dk ** -0.5)
    kc, vc, ac = to_chunks(k), to_chunks(v), to_chunks(log_a)
    b = jnp.cumsum(ac, axis=3)
    b_ref = b[:, :, :, c // 2:c // 2 + 1]
    b_last = b[:, :, :, -1:]
    causal = jnp.tril(jnp.ones((c, c), dtype=bool))
    att = jnp.einsum('bhntd,bhnsd->bhnts', qc * jnp.exp(b - b_ref), kc * jnp.exp(b_ref - b))
    att = jnp.where(causal, att, 0.0)
    o_intra = jnp.einsum('bhnts,bhnse->bhnte', att, vc)
    q_inter = qc * jnp.exp(b)
    k_end = kc * jnp.exp(b_last - b)
    decay_end = jnp.exp(b_last[:, :, :, 0])

    def step(state, xs):
        qi, ki, vi, di = xs
        out = jnp.einsum('bhtd,bhde->bhte', qi, state)
        state = di[..., None] * state + jnp.einsum('bhsd,bhse->bhde', ki, vi)
        return state, out

    state0 = jnp.zeros((bsz, nh, dk, dv), jnp.float32)
    xs = (jnp.moveaxis(q_inter, 2, 0), jnp.moveaxis(k_end, 2, 0), jnp.moveaxis(vc, 2, 0), jnp.moveaxis(decay_end, 2, 0))
    _, o_inter = lax.scan(step, state0, xs)
    o = o_intra + jnp.moveaxis(o_inter, 0, 2)
    return o.transpose(0, 2, 3, 1, 4).reshape(bsz, seqlen, nh, dv)

def swa_sink_attention(q, k, v, sinks):
    bsz, seqlen, nh, hd = q.shape
    kvh = k.shape[2]
    grp = nh // kvh
    L = SWA_BLOCK
    n = seqlen // L
    qb = q.reshape(bsz, n, L, kvh, grp, hd)
    kb = k.reshape(bsz, n, L, kvh, hd)
    vb = v.reshape(bsz, n, L, kvh, hd)
    kk = jnp.concatenate([jnp.concatenate([jnp.zeros_like(kb[:, :1]), kb[:, :-1]], axis=1), kb], axis=2)
    vv = jnp.concatenate([jnp.concatenate([jnp.zeros_like(vb[:, :1]), vb[:, :-1]], axis=1), vb], axis=2)
    s = jnp.einsum('bnqhgd,bnkhd->bnhgqk', qb, kk).astype(jnp.float32) * (hd ** -0.5)
    qpos = jnp.arange(L)[:, None] + L
    kpos = jnp.arange(2 * L)[None, :]
    rel = qpos - kpos
    band = (rel >= 0) & (rel < SWA_WINDOW)
    valid = band[None] & ((jnp.arange(n)[:, None, None] > 0) | (kpos[None] >= L))
    s = jnp.where(valid[None, :, None, None], s, -jnp.inf)
    sink = sinks.astype(jnp.float32).reshape(kvh, grp)[None, None, :, :, None, None]
    m = jnp.maximum(jnp.max(s, axis=-1, keepdims=True), sink)
    p = jnp.exp(s - m)
    denom = jnp.sum(p, axis=-1, keepdims=True) + jnp.exp(sink - m)
    o = jnp.einsum('bnhgqk,bnkhd->bnqhgd', (p / denom).astype(v.dtype), vv)
    return o.reshape(bsz, seqlen, nh, hd)

def peer_layer(xn, w_pq, sub_keys, expert_u, expert_v):
    bsz, seqlen, d = xn.shape
    t = bsz * seqlen
    xt = xn.reshape(t, d)
    qp = (xt @ w_pq).reshape(t, PEER_HEADS, 2, PEER_QDIM // 2)
    scores = jnp.einsum('thpd,hpkd->thpk', qp, sub_keys).astype(jnp.float32)
    s_top, i_top = lax.top_k(scores, PEER_TOPK)
    cand = (s_top[:, :, 0, :, None] + s_top[:, :, 1, None, :]).reshape(t, PEER_HEADS, PEER_TOPK * PEER_TOPK)
    cand_idx = (i_top[:, :, 0, :, None] * PEER_NKEYS + i_top[:, :, 1, None, :]).reshape(t, PEER_HEADS, PEER_TOPK * PEER_TOPK)
    best, pos = lax.top_k(cand, PEER_TOPK)
    idx = jnp.take_along_axis(cand_idx, pos, axis=-1)
    gate = jax.nn.softmax(best, axis=-1).astype(xn.dtype)
    hk = PEER_HEADS * PEER_TOPK
    nblk = t // PEER_TOKEN_BLOCK

    def expert_block(args):
        xb, ib, gb = args
        u = expert_u[ib]
        h = jax.nn.gelu(jnp.einsum('lkd,ld->lk', u, xb), approximate=False)
        return jnp.einsum('lk,lkd->ld', gb * h, expert_v[ib])

    out = lax.map(expert_block, (xt.reshape(nblk, PEER_TOKEN_BLOCK, d),
                                 idx.reshape(nblk, PEER_TOKEN_BLOCK, hk),
                                 gate.reshape(nblk, PEER_TOKEN_BLOCK, hk)))
    return out.reshape(bsz, seqlen, d)

def first_inputs(seed: int = 0) -> dict:
    key = jax.random.key(seed)
    ks = jax.random.split(key, 17)
    f32 = jnp.float32
    nrm = lambda k, shape, scale: jax.random.normal(k, shape, f32) * scale
    return {
        'x': nrm(ks[0], (BATCH, SEQ, D_MODEL), 1.0),
        'norm_mix_g': 1.0 + nrm(ks[1], (DEPTH, D_MODEL), 0.02),
        'w_in': nrm(ks[2], (DEPTH, D_MODEL, IN_WIDTH), D_MODEL ** -0.5),
        'w_gk2': nrm(ks[3], (DEPTH, GLA_GATE_RANK, GLA_KW), GLA_GATE_RANK ** -0.5),
        'b_gk': nrm(ks[4], (DEPTH, GLA_KW), 0.1),
        'gla_norm_g': 1.0 + nrm(ks[5], (DEPTH, GLA_DV), 0.02),
        'q_norm_g': 1.0 + nrm(ks[6], (DEPTH, SWA_HEAD_DIM), 0.02),
        'k_norm_g': 1.0 + nrm(ks[7], (DEPTH, SWA_HEAD_DIM), 0.02),
        'attn_sinks': nrm(ks[8], (DEPTH, SWA_HEADS), 0.1),
        'w_branch_a': nrm(ks[9], (DEPTH, GLA_VW, D_MODEL), GLA_VW ** -0.5),
        'w_branch_b': nrm(ks[10], (DEPTH, SWA_QW, D_MODEL), SWA_QW ** -0.5),
        'w_out': nrm(ks[11], (DEPTH, D_MODEL, D_MODEL), D_MODEL ** -0.5),
        'norm_ffn_g': 1.0 + nrm(ks[12], (DEPTH, D_MODEL), 0.02),
        'w_peer_q': nrm(ks[13], (DEPTH, D_MODEL, PEER_HEADS * PEER_QDIM), D_MODEL ** -0.5),
        'peer_sub_keys': nrm(ks[14], (DEPTH, PEER_HEADS, 2, PEER_NKEYS, PEER_QDIM // 2), (PEER_QDIM // 2) ** -0.5),
        'peer_u': nrm(ks[15], (DEPTH, PEER_EXPERTS, D_MODEL), D_MODEL ** -0.5),
        'peer_v': nrm(ks[16], (DEPTH, PEER_EXPERTS, D_MODEL), D_MODEL ** -0.5),
    }

def first_block(x, norm_mix_g, w_in, w_gk2, b_gk, gla_norm_g, q_norm_g, k_norm_g, attn_sinks,
              w_branch_a, w_branch_b, w_out, norm_ffn_g, w_peer_q, peer_sub_keys, peer_u, peer_v):
    bsz, seqlen, d = x.shape
    cos, sin = rope_tables(seqlen)
    for l in range(DEPTH):
        h = rmsnorm(x, norm_mix_g[l])
        proj = h @ w_in[l]
        gq, gk, gv, gr, glr, sq, sk, sv, gate_a, gate_b = jnp.split(proj, IN_SPLIT_POINTS, axis=-1)
        log_a = jax.nn.log_sigmoid((glr @ w_gk2[l] + b_gk[l]).astype(jnp.float32)) / GLA_GATE_NORM
        o_a = gla_chunked(gq.reshape(bsz, seqlen, GLA_HEADS, GLA_DK),
                          gk.reshape(bsz, seqlen, GLA_HEADS, GLA_DK),
                          gv.reshape(bsz, seqlen, GLA_HEADS, GLA_DV),
                          log_a.reshape(bsz, seqlen, GLA_HEADS, GLA_DK))
        o_a = rmsnorm(o_a, gla_norm_g[l]).astype(x.dtype) * jax.nn.silu(gr.reshape(bsz, seqlen, GLA_HEADS, GLA_DV))
        y_a = o_a.reshape(bsz, seqlen, GLA_VW) @ w_branch_a[l]
        q = partial_rope(rmsnorm(sq.reshape(bsz, seqlen, SWA_HEADS, SWA_HEAD_DIM), q_norm_g[l]), cos, sin)
        k = partial_rope(rmsnorm(sk.reshape(bsz, seqlen, SWA_KV_HEADS, SWA_HEAD_DIM), k_norm_g[l]), cos, sin)
        o_b = swa_sink_attention(q, k, sv.reshape(bsz, seqlen, SWA_KV_HEADS, SWA_HEAD_DIM), attn_sinks[l])
        y_b = o_b.reshape(bsz, seqlen, SWA_QW) @ w_branch_b[l]
        merged = jax.nn.sigmoid(gate_a) * y_a + jax.nn.sigmoid(gate_b) * y_b
        x = x + merged @ w_out[l]
        x = x + peer_layer(rmsnorm(x, norm_ffn_g[l]), w_peer_q[l], peer_sub_keys[l], peer_u[l], peer_v[l])
    return x


DEPTH_2 = 2

N_MIXERS = 2

GDN_K_HEADS = 8
GDN_V_HEADS = 16
GDN_HEAD_K = 128
GDN_HEAD_V = 128
GDN_CONV = 4
GDN_CHUNK = 64
GDN_QK = GDN_K_HEADS * GDN_HEAD_K
GDN_V = GDN_V_HEADS * GDN_HEAD_V
GDN_CONV_DIM = 2 * GDN_QK + GDN_V
GDN_PROJ = GDN_CONV_DIM + GDN_V + 2 * GDN_V_HEADS

SC_WIDTH = 2 * D_MODEL
SC_CONV = 3
SC_PROJ = 4 * SC_WIDTH

N_GDN_LAYERS = (DEPTH_2 + 1) // 2
N_SC_LAYERS = DEPTH_2 // 2


def rms_norm(x, w):
    xf = x.astype(jnp.float32)
    y = xf * lax.rsqrt(jnp.mean(xf * xf, axis=-1, keepdims=True) + NORM_EPS)
    return y * w.astype(jnp.float32)

def l2_normalize(x):
    xf = x.astype(jnp.float32)
    return xf * lax.rsqrt(jnp.sum(xf * xf, axis=-1, keepdims=True) + NORM_EPS)

def causal_depthwise_conv(x, w):
    width = w.shape[0]
    t = x.shape[1]
    xp = jnp.pad(x, ((0, 0), (width - 1, 0), (0, 0)))
    return sum(w[j] * xp[:, j:j + t] for j in range(width))

def chunked_gated_delta_rule(q, k, v, g, beta):
    b, h, t, dk = q.shape
    dv = v.shape[-1]
    c = GDN_CHUNK
    n = t // c
    q = q * (dk ** -0.5)
    kb = k * beta[..., None]
    vb = v * beta[..., None]
    q, k, kb = [a.reshape(b, h, n, c, dk) for a in (q, k, kb)]
    vb = vb.reshape(b, h, n, c, dv)
    g = jnp.cumsum(g.reshape(b, h, n, c), axis=-1)
    incl = jnp.tril(jnp.ones((c, c), dtype=bool))
    strict = jnp.tril(jnp.ones((c, c), dtype=bool), k=-1)
    diff = g[..., :, None] - g[..., None, :]
    decay = jnp.where(incl, jnp.exp(jnp.where(incl, diff, 0.0)), 0.0)
    a_mat = jnp.where(strict, jnp.einsum('bhnid,bhnjd->bhnij', kb, k) * decay, 0.0)
    ia = a_mat + jnp.eye(c, dtype=a_mat.dtype)
    u = lax.linalg.triangular_solve(ia, vb, left_side=True, lower=True, unit_diagonal=True)
    w = lax.linalg.triangular_solve(ia, kb * jnp.exp(g)[..., None], left_side=True, lower=True,
                                    unit_diagonal=True)
    qk = jnp.where(incl, jnp.einsum('bhnid,bhnjd->bhnij', q, k) * decay, 0.0)
    q_dec = q * jnp.exp(g)[..., None]
    g_last = g[..., -1]
    k_dec = k * jnp.exp(g_last[..., None] - g)[..., None]
    state_decay = jnp.exp(g_last)

    def step(s, xs):
        q_c, k_c, u_c, w_c, qk_c, sd_c = xs
        v_new = u_c - jnp.einsum('bhck,bhkv->bhcv', w_c, s)
        o_c = jnp.einsum('bhck,bhkv->bhcv', q_c, s) + jnp.einsum('bhij,bhjv->bhiv', qk_c, v_new)
        s = s * sd_c[..., None, None] + jnp.einsum('bhck,bhcv->bhkv', k_c, v_new)
        return s, o_c

    xs = tuple(jnp.moveaxis(a, 2, 0) for a in (q_dec, k_dec, u, w, qk, state_decay))
    s0 = jnp.zeros((b, h, dk, dv), dtype=jnp.float32)
    _, o = lax.scan(step, s0, xs)
    return jnp.moveaxis(o, 0, 2).reshape(b, h, t, dv)

def gated_deltanet_mixer(h, w_in, conv_w, a_log, dt_bias, norm_w, w_out):
    bsz, t, _ = h.shape
    proj = h @ w_in
    qkv, z, b_logit, a_logit = jnp.split(
        proj, [GDN_CONV_DIM, GDN_CONV_DIM + GDN_V, GDN_CONV_DIM + GDN_V + GDN_V_HEADS], axis=-1)
    qkv = jax.nn.silu(causal_depthwise_conv(qkv, conv_w))
    q, k, v = jnp.split(qkv, [GDN_QK, 2 * GDN_QK], axis=-1)
    rep = GDN_V_HEADS // GDN_K_HEADS
    q = jnp.repeat(l2_normalize(q.reshape(bsz, t, GDN_K_HEADS, GDN_HEAD_K)), rep, axis=2)
    k = jnp.repeat(l2_normalize(k.reshape(bsz, t, GDN_K_HEADS, GDN_HEAD_K)), rep, axis=2)
    v = v.reshape(bsz, t, GDN_V_HEADS, GDN_HEAD_V).astype(jnp.float32)
    beta = jax.nn.sigmoid(b_logit.astype(jnp.float32))
    g = -jnp.exp(a_log.astype(jnp.float32)) * jax.nn.softplus(
        a_logit.astype(jnp.float32) + dt_bias.astype(jnp.float32))
    to_bht = lambda a: jnp.swapaxes(a, 1, 2)
    o = chunked_gated_delta_rule(to_bht(q), to_bht(k), to_bht(v), to_bht(g), to_bht(beta))
    o = jnp.swapaxes(o, 1, 2)
    gate = jax.nn.silu(z.reshape(bsz, t, GDN_V_HEADS, GDN_HEAD_V).astype(jnp.float32))
    o = rms_norm(o, norm_w) * gate
    return o.reshape(bsz, t, GDN_V).astype(h.dtype) @ w_out

def short_conv_mixer(h, w_in, conv_w, w_out):
    u, b_gate, c_gate, z = jnp.split(h @ w_in, 4, axis=-1)
    y = b_gate * causal_depthwise_conv(c_gate * u, conv_w)
    return (y * jax.nn.silu(z)) @ w_out

def second_inputs(seed: int = 0) -> dict:
    key = jax.random.key(seed)
    ks = jax.random.split(key, 12)
    f32 = jnp.float32
    x = jax.random.normal(ks[0], (BATCH, SEQ, D_MODEL), f32)
    pre_norm_w = 1.0 + 0.05 * jax.random.normal(ks[1], (DEPTH_2, D_MODEL), f32)
    post_norm_w = 1.0 + 0.05 * jax.random.normal(ks[2], (DEPTH_2, D_MODEL), f32)
    gdn_w_in = jax.random.normal(ks[3], (N_GDN_LAYERS, D_MODEL, GDN_PROJ), f32) * D_MODEL ** -0.5
    gdn_conv_w = jax.random.normal(ks[4], (N_GDN_LAYERS, GDN_CONV, GDN_CONV_DIM), f32) * GDN_CONV ** -0.5
    gdn_A_log = jnp.log(jax.random.uniform(ks[5], (N_GDN_LAYERS, GDN_V_HEADS), f32, 1.0, 16.0))
    dt = jnp.exp(jax.random.uniform(ks[6], (N_GDN_LAYERS, GDN_V_HEADS), f32,
                                    float(np.log(1e-3)), float(np.log(1e-1))))
    gdn_dt_bias = dt + jnp.log(-jnp.expm1(-dt))
    gdn_norm_w = 1.0 + 0.05 * jax.random.normal(ks[7], (N_GDN_LAYERS, GDN_HEAD_V), f32)
    gdn_w_out = jax.random.normal(ks[8], (N_GDN_LAYERS, GDN_V, D_MODEL), f32) * GDN_V ** -0.5
    sc_w_in = jax.random.normal(ks[9], (N_SC_LAYERS, D_MODEL, SC_PROJ), f32) * D_MODEL ** -0.5
    sc_conv_w = jax.random.normal(ks[10], (N_SC_LAYERS, SC_CONV, SC_WIDTH), f32) * SC_CONV ** -0.5
    sc_w_out = jax.random.normal(ks[11], (N_SC_LAYERS, SC_WIDTH, D_MODEL), f32) * SC_WIDTH ** -0.5
    return {"x": x, "pre_norm_w": pre_norm_w, "post_norm_w": post_norm_w,
            "gdn_w_in": gdn_w_in, "gdn_conv_w": gdn_conv_w, "gdn_A_log": gdn_A_log,
            "gdn_dt_bias": gdn_dt_bias, "gdn_norm_w": gdn_norm_w, "gdn_w_out": gdn_w_out,
            "sc_w_in": sc_w_in, "sc_conv_w": sc_conv_w, "sc_w_out": sc_w_out}

def second_block(x, pre_norm_w, post_norm_w, gdn_w_in, gdn_conv_w, gdn_A_log, gdn_dt_bias, gdn_norm_w,
              gdn_w_out, sc_w_in, sc_conv_w, sc_w_out):
    for i in range(DEPTH_2):
        h = rms_norm(x, pre_norm_w[i]).astype(x.dtype)
        j = i // N_MIXERS
        if i % N_MIXERS == 0:
            y = gated_deltanet_mixer(h, gdn_w_in[j], gdn_conv_w[j], gdn_A_log[j], gdn_dt_bias[j],
                                     gdn_norm_w[j], gdn_w_out[j])
        else:
            y = short_conv_mixer(h, sc_w_in[j], sc_conv_w[j], sc_w_out[j])
        x = x + rms_norm(y, post_norm_w[i]).astype(x.dtype)
    return x


def setup_inputs(seed=0):
    out = dict(first_inputs(seed))
    for name, value in second_inputs(seed + 1).items():
        if name != "x":
            out[name + "_2"] = value
    return out


def reference(
    x, norm_mix_g, w_in, w_gk2, b_gk, gla_norm_g, q_norm_g, k_norm_g, attn_sinks, w_branch_a,
    w_branch_b, w_out, norm_ffn_g, w_peer_q, peer_sub_keys, peer_u, peer_v, pre_norm_w_2,
    post_norm_w_2, gdn_w_in_2, gdn_conv_w_2, gdn_A_log_2, gdn_dt_bias_2, gdn_norm_w_2,
    gdn_w_out_2, sc_w_in_2, sc_conv_w_2, sc_w_out_2,
):
    x = first_block(
        x, norm_mix_g, w_in, w_gk2, b_gk, gla_norm_g, q_norm_g, k_norm_g, attn_sinks,
        w_branch_a, w_branch_b, w_out, norm_ffn_g, w_peer_q, peer_sub_keys, peer_u, peer_v,
    )
    return second_block(
        x, pre_norm_w_2, post_norm_w_2, gdn_w_in_2, gdn_conv_w_2, gdn_A_log_2, gdn_dt_bias_2,
        gdn_norm_w_2, gdn_w_out_2, sc_w_in_2, sc_conv_w_2, sc_w_out_2,
    )


_drawn_inputs = setup_inputs


def setup_inputs(seed=0):
    import zlib

    import numpy as np

    out = dict(_drawn_inputs(seed))
    spreads = {}
    factors = {'gla_norm_g': 4.431,
     'q_norm_g': 8.0,
     'k_norm_g': 8.0,
     'attn_sinks': 8.0,
     'norm_ffn_g': 8.0}
    for name, (base, spread) in spreads.items():
        noise = np.random.default_rng([zlib.crc32(name.encode()), seed]).standard_normal(out[name].shape)
        drawn = base * np.exp(spread * noise) if base else spread * noise
        out[name] = __import__('jax').numpy.asarray(drawn.astype(out[name].dtype))
    for name, factor in factors.items():
        out[name] = (out[name] * factor).astype(out[name].dtype)
    return out
```

```python
from contextlib import ExitStack

import numpy as np
import concourse.bass as bass
from concourse import mybir

F32 = mybir.dt.float32
F32R = mybir.dt.float32r
U32 = mybir.dt.uint32
ALU = mybir.AluOpType
ACT = mybir.ActivationFunctionType
AX_X = mybir.AxisListType.X

P = 128
T = 512
NT = T // P
D = 1024
KD = D // P
EPS = 1e-6
C = 64
NCH = T // C

GLA_H, GLA_DK, GLA_DV, GLA_R = 4, 128, 256, 16
GLA_COLS = 2 * GLA_DK + 2 * GLA_DV
SWA_H, SWA_KV, HD = 16, 4, 64
GRP = SWA_H // SWA_KV
SWA_COLS = (GRP + 2) * HD
ROPE_HALF = 8
PEER_H, PEER_K, NKEYS = 8, 16, 128
EB = 4
NEB = NKEYS // EB
GDN_KH, GDN_VH = 8, 16
GDN_COLS = 6 * P
SC_TILES = 16
NEG = -1e30


def mm3(pe, out, lhs, rhs, start, stop):
    (lh, ll), (rh, rl) = lhs, rhs
    pe.matmul(out, lh, rh, start=start, stop=False)
    pe.matmul(out, lh, rl, start=False, stop=False)
    return pe.matmul(out, ll, rh, start=False, stop=stop)


def after(eng, sem, count):
    if not (isinstance(count, int) and count == 0):
        eng.wait_ge(sem, count)


def steps(eng, n, body):
    body(0)
    with eng.Fori(1, n - 1) as i:
        body(i)
    body(n - 1)


def flat(ap):
    return ap.rearrange("p a b -> p (a b)")


class Phase:

    def __init__(self, nc, tag):
        self.nc, self.tag, self.ctx, self.sems = nc, tag, ExitStack(), []

    def __enter__(self):
        return self

    def __exit__(self, *a):
        if a[0] is None:
            self.nc.clear_and_free_semaphores(self.sems)
            self.nc.all_engine_barrier()
        return self.ctx.__exit__(*a)

    def sb(self, name, shape, dt=F32):
        return self.ctx.enter_context(self.nc.sbuf_tensor(f"{self.tag}_{name}", shape, dt))

    def psum(self, name="ps"):
        return self.ctx.enter_context(self.nc.psum_tensor(f"{self.tag}_{name}", [P, 8, 512], F32))

    def sem(self, name):
        self.sems.append(self.nc.alloc_semaphore(f"{self.tag}_{name}"))
        return self.sems[-1]


def norm_transposed(nc, tag, x, gain_dram, ident, hh, hl, load_from=None):
    with Phase(nc, tag) as ph:
        xn = ph.sb("xn", [P, NT, D])
        gain = ph.sb("gain", [P, KD])
        ss = ph.sb("ss", [P, NT])
        ms = ph.sb("ms", [P, NT])
        rt = ph.sb("rt", [P, NT])
        rs = ph.sb("rs", [P, NT])
        ps = ph.psum()
        gain_in, x_in, squared, mean_ok, root_ok, rstd_ok, scaled, turned, hi_ok, lo_ok = (
            ph.sem(n) for n in ("gain_in", "x_in", "squared", "mean_ok", "root_ok", "rstd_ok", "scaled",
                                "turned", "hi_ok", "lo_ok"))
        with nc.Block() as block:
            @block.sync
            def _(sp):
                if load_from is not None:
                    for n in range(NT):
                        sp.dma_start(x[:, n, :], load_from[n * P:(n + 1) * P, :]).then_inc(x_in, 16)
                sp.dma_start(gain[:], gain_dram).then_inc(gain_in, 16)

            @block.scalar
            def _(act):
                for n in range(NT):
                    if load_from is not None and n == 0:
                        act.wait_ge(x_in, 16 * NT)
                    act.activation(xn[:, n, :], x[:, n, :], ACT.Square, accum_out=ss[:, n:n + 1]).then_inc(squared, 1)
                act.wait_ge(mean_ok, 1)
                act.activation(rt[:], ms[:], ACT.Sqrt).then_inc(root_ok, 1)
                act.wait_ge(gain_in, 16)
                for k in range(KD):
                    act.wait_ge(turned, k + 1)
                    act.activation(hh[:, k, :], ps[:, k, :], ACT.Copy, scale=gain[:, k:k + 1]).then_inc(hi_ok, 1)

            @block.vector
            def _(dve):
                dve.wait_ge(squared, NT)
                dve.tensor_scalar(ms[:], ss[:], 1.0 / D, EPS, ALU.mult, ALU.add).then_inc(mean_ok, 1)
                dve.wait_ge(root_ok, 1)
                dve.reciprocal(rs[:], rt[:]).then_inc(rstd_ok, 1)
                dve.wait_ge(rstd_ok, 1)
                for n in range(NT):
                    dve.tensor_scalar(xn[:, n, :], x[:, n, :], rs[:, n:n + 1], None, ALU.mult).then_inc(scaled, 1)
                for k in range(KD):
                    dve.wait_ge(hi_ok, k + 1)
                    dve.scalar_tensor_tensor(hl[:, k, :], ps[:, k, :], gain[:, k:k + 1], hh[:, k, :].bitcast(F32),
                                             ALU.mult, ALU.subtract).then_inc(lo_ok, 1)

            @block.tensor
            def _(pe):
                pe.wait_ge(scaled, NT)
                for k in range(KD):
                    for n in range(NT):
                        last = pe.transpose(ps[:, k, n * P:(n + 1) * P], xn[:, n, k * P:(k + 1) * P], ident[:])
                    last.then_inc(turned, 1)


def gla(nc, hh, hl, oa, ident, drams):
    w_dram, glr_dram, gk2_dram, bgk_dram, gain_dram, tri_dram, reset_dram = drams
    with Phase(nc, "gla") as ph:
        raw = ph.sb("raw", [P, KD, GLA_COLS])
        wh = ph.sb("wh", [P, KD, GLA_COLS], F32R)
        wl = ph.sb("wl", [P, KD, GLA_COLS], F32R)
        glr = ph.sb("glr", [P, KD, GLA_R])
        gh = wh[:, :, 0:P]
        gl = wl[:, :, 0:P]
        glrT = ph.sb("glrT", [GLA_R, T])
        gk2 = ph.sb("gk2", [GLA_R, GLA_H * GLA_DK])
        bgk = ph.sb("bgk", [P, GLA_H])
        gain = ph.sb("gain", [P, GLA_DV])
        tri = ph.sb("tri", [P, C], U32)
        b = ph.sb("b", [P, GLA_H, NCH, C])
        z = raw[:, 0:4, 0:512]
        za = raw[:, 4:8, 0:512]
        reset = ph.sb("reset", [P, T])
        dref = ph.sb("dref", [P, NCH, C])
        dend = ph.sb("dend", [P, NCH, C])
        e1 = ph.sb("e1", [P, T])
        e2 = ph.sb("e2", [P, T])
        e3 = ph.sb("e3", [P, T])
        e4 = ph.sb("e4", [P, T])
        dec = ph.sb("dec", [P, NCH])
        qa = ph.sb("qa", [P, T])
        ka = ph.sb("ka", [P, T])
        ke = ph.sb("ke", [P, T])
        qi = ph.sb("qi", [P, 2, NT, P])
        kend = ph.sb("kend", [P, NT, GLA_DK])
        attm = ph.sb("attm", [P, NT, P])
        v = ph.sb("v", [P, NT, GLA_DV])
        rg = ph.sb("rg", [P, NT, GLA_DV])
        S = ph.sb("S", [P, NCH, GLA_DV])
        og = ph.sb("og", [P, NT, GLA_DV])
        ss = ph.sb("ss", [P, NT])
        ms = ph.sb("ms", [P, NT])
        rt = ph.sb("rt", [P, NT])
        rs = ph.sb("rs", [P, NT])
        rt_seen = ph.sb("rt_seen", [P, 1])
        ps = ph.psum()

        small_in = ph.sem("small_in")
        zeroed = ph.sem("zeroed")
        pre = ph.sem("pre")
        glr_hi, glr_lo, glr_ok, glr_sb, gk_ok = (ph.sem(n) for n in ("glr_hi", "glr_lo", "glr_ok", "glr_sb", "gk_ok"))
        gate_v, gate_a, b_ok = ph.sem("gate_v"), ph.sem("gate_a"), ph.sem("b_ok")
        raw_in, w_hi, w_lo = ph.sem("raw_in"), ph.sem("w_hi"), ph.sem("w_lo")
        q_ok, k_ok, v_ok, r_ok = (ph.sem(n) for n in ("q_ok", "k_ok", "v_ok", "r_ok"))
        diff_ok, exp_ok, qk_scaled = ph.sem("diff_ok"), ph.sem("exp_ok"), ph.sem("qk_scaled")
        ke_turned, kend_ok, att_ok, attm_ok = (ph.sem(n) for n in ("ke_turned", "kend_ok", "att_ok", "attm_ok"))
        v_sb, r_sb, rg_ok = ph.sem("v_sb"), ph.sem("r_sb"), ph.sem("rg_ok")
        ds_ok, S_ok, o_ok, sq_ok, ms_ok, root_ok, rs_ok, og_ok = (
            ph.sem(n) for n in ("ds_ok", "S_ok", "o_ok", "sq_ok", "ms_ok", "root_ok", "rs_ok", "og_ok"))
        o_turned, oa_ok, oal_ok = ph.sem("o_turned"), ph.sem("oa_ok"), ph.sem("oal_ok")
        NS = NCH - 1

        def psv(bank, n):
            return ps[:, bank + n // 2, (n % 2) * GLA_DV:(n % 2 + 1) * GLA_DV]

        def psd(c):
            return psv(2 * (c % 2), c // 2)

        with nc.Block() as block:
            @block.sync
            def _(sp):
                for dst, src in ((glr, glr_dram), (gk2, gk2_dram), (bgk, bgk_dram), (tri, tri_dram), (reset, reset_dram)):
                    sp.dma_start(dst[:], src).then_inc(small_in, 16)
                sp.dma_start(gain[:], gain_dram.partition_broadcast(P)).then_inc(small_in, 16)
                sp.wait_ge(b_ok, 1)
                sp.dma_start(raw[:], w_dram[0]).then_inc(raw_in, 16)

                def step(h):
                    sp.wait_ge(w_hi, h + 1)
                    sp.wait_ge(w_lo, h + 1)
                    sp.dma_start(raw[:], w_dram[h + 1]).then_inc(raw_in, 16)
                with sp.Fori(0, GLA_H - 1) as h:
                    step(h)

            @block.gpsimd
            def _(pool):
                pool.memset(wh[:].bitcast(F32)[:, :, 0:P], 0.0).then_inc(zeroed, 1)
                pool.memset(wl[:].bitcast(F32)[:, :, 0:P], 0.0).then_inc(zeroed, 1)
                pool.memset(qi[:], 0.0).then_inc(zeroed, 1)
                pool.memset(attm[:], 0.0).then_inc(zeroed, 1)

                pool.wait_ge(small_in, 16 * 6)
                with pool.Fori(0, GLA_H) as h:
                    pool.wait_ge(r_sb, h + 1)
                    pool.tensor_tensor(rg[:], rg[:], gain[:].unsqueeze(1).broadcast_to([P, NT, GLA_DV]),
                                       ALU.mult).then_inc(rg_ok, 1)

            @block.scalar
            def _(act):
                act.wait_ge(small_in, 16 * 6)
                act.wait_ge(zeroed, 2)
                act.activation(gh[:, :, 0:GLA_R], glr[:], ACT.Copy).then_inc(glr_hi, 1)
                act.wait_ge(glr_ok, 1)
                act.activation(glrT[:], ps[0:GLA_R, 6, :], ACT.Copy).then_inc(glr_sb, 1)
                act.wait_ge(gate_v, 2)
                act.activation(za, za, ACT.Exp).then_inc(gate_a, 1)
                act.wait_ge(gate_v, 3)
                act.activation(za, za, ACT.Ln).then_inc(gate_a, 1)

                def split(h):
                    act.wait_ge(raw_in, 16 * (h + 1))
                    act.activation(wh[:], raw[:], ACT.Copy).then_inc(w_hi, 1)

                act.wait_ge(gk_ok, 1)
                split(0)
                act.wait_ge(b_ok, 1)

                def step(h):
                    act.wait_ge(diff_ok, 2 * h + 2)
                    after(act, qk_scaled, 5 * h)
                    act.activation(e1[:], dref[:].rearrange("p a b -> p (a b)"), ACT.Exp).then_inc(exp_ok, 1)
                    act.activation(e2[:], dref[:].rearrange("p a b -> p (a b)"), ACT.Exp, scale=-1.0).then_inc(exp_ok, 1)
                    act.activation(e3[:], b[:, h, :, :].rearrange("p a b -> p (a b)"), ACT.Exp).then_inc(exp_ok, 1)
                    act.activation(e4[:], dend[:].rearrange("p a b -> p (a b)"), ACT.Exp).then_inc(exp_ok, 1)
                    after(act, S_ok, h * NS)
                    act.activation(dec[:], b[:, h, :, C - 1], ACT.Exp).then_inc(exp_ok, 1)
                    act.wait_ge(v_ok, h + 1)
                    for n in range(2):
                        act.activation(v[:, 2 * n:2 * n + 2, :].rearrange("p a b -> p (a b)"), ps[:, 2 + n, :],
                                       ACT.Copy).then_inc(v_sb, 1)
                    act.wait_ge(ke_turned, h + 1)
                    act.activation(kend[:].rearrange("p a b -> p (a b)"), ps[:, 6, :], ACT.Copy).then_inc(kend_ok, 1)
                    act.wait_ge(r_ok, h + 1)
                    after(act, og_ok, h * NT)
                    for n in range(2):
                        last_r = act.activation(rg[:, 2 * n:2 * n + 2, :].rearrange("p a b -> p (a b)"),
                                                ps[:, 4 + n, :], ACT.Silu)
                    last_r.then_inc(r_sb, 1)
                    if h is not GLA_H - 1:
                        split(h + 1)
                    for n in range(NT):
                        act.wait_ge(o_ok, h * NT + n // 2 * 2 + 2)
                        act.activation(og[:, n, :], psv(4, n), ACT.Square, accum_out=ss[:, n:n + 1]).then_inc(sq_ok, 1)
                    act.wait_ge(ms_ok, h + 1)
                    act.activation(rt[:], ms[:], ACT.Sqrt).then_inc(root_ok, 1)
                    for e in range(2):
                        act.wait_ge(o_turned, 2 * h + e + 1)
                        act.activation(oa[0][:, h * 2 + e, :], ps[:, 6 + e, :], ACT.Copy).then_inc(oa_ok, 1)

                steps(act, GLA_H, step)

            @block.vector
            def _(dve):
                dve.wait_ge(glr_hi, 1)
                dve.tensor_tensor(gl[:, :, 0:GLA_R], glr[:], gh[:, :, 0:GLA_R].bitcast(F32), ALU.subtract).then_inc(glr_lo, 1)
                dve.wait_ge(gk_ok, 1)
                dve.tensor_tensor(z, ps[:, 0:GLA_H, :], bgk[:].unsqueeze(2).broadcast_to([P, GLA_H, T]),
                                  ALU.add).then_inc(gate_v, 1)
                dve.wait_ge(gate_v, 1)
                dve.tensor_scalar(za, z, 0.0, 2.0, ALU.min, ALU.mult).then_inc(pre, 1)
                dve.wait_ge(pre, 1)
                dve.tensor_tensor(za, za, z, ALU.subtract).then_inc(gate_v, 1)
                dve.wait_ge(gate_a, 1)
                dve.tensor_scalar(za, za, 1.0, None, ALU.add).then_inc(gate_v, 1)
                dve.wait_ge(gate_a, 2)
                dve.scalar_tensor_tensor(z, z, 0.0, za, ALU.min, ALU.subtract).then_inc(pre, 1)
                dve.wait_ge(pre, 2)
                dve.tensor_scalar(z, z, 1.0 / 16.0, None, ALU.mult).then_inc(pre, 1)
                dve.wait_ge(pre, 3)
                for h in range(GLA_H):
                    scan = dve.tensor_tensor_scan(b[:, h, :, :].rearrange("p a b -> p (a b)"), reset[:], z[:, h, :],
                                                  0.0, ALU.mult, ALU.add)
                scan.then_inc(b_ok, 1)
                dve.wait_ge(b_ok, 1)

                def split(h):
                    dve.wait_ge(w_hi, h + 1)
                    dve.tensor_tensor(wl[:], raw[:], wh[:].bitcast(F32), ALU.subtract).then_inc(w_lo, 1)

                split(0)
                dve.wait_ge(zeroed, 4)
                q4 = ps[:, 0, :].rearrange("p (n c w) -> p n c w", n=NT, c=2)
                e34 = e3[:].rearrange("p (n c w) -> p n c w", n=NT, c=2)
                s = GLA_DK ** -0.5

                def step(h):
                    after(dve, exp_ok, 5 * h)
                    dve.tensor_tensor(dref[:], b[:, h, :, :], b[:, h, :, C // 2:C // 2 + 1].broadcast_to([P, NCH, C]),
                                      ALU.subtract).then_inc(diff_ok, 1)
                    dve.tensor_tensor(dend[:], b[:, h, :, C - 1:C].broadcast_to([P, NCH, C]), b[:, h, :, :],
                                      ALU.subtract).then_inc(diff_ok, 1)
                    dve.wait_ge(exp_ok, 5 * h + 5)
                    dve.wait_ge(k_ok, h + 1)
                    dve.tensor_tensor(ke[:], ps[:, 1, :], e4[:], ALU.mult).then_inc(qk_scaled, 1)
                    dve.tensor_tensor(ka[:], ps[:, 1, :], e2[:], ALU.mult).then_inc(qk_scaled, 1)
                    dve.scalar_tensor_tensor(qa[:], ps[:, 0, :], s, e1[:], ALU.mult, ALU.mult).then_inc(qk_scaled, 1)
                    for c in range(2):
                        dve.scalar_tensor_tensor(qi[:, c, :, c * C:(c + 1) * C], q4[:, :, c, :], s, e34[:, :, c, :],
                                                 ALU.mult, ALU.mult).then_inc(qk_scaled, 1)
                    dve.wait_ge(att_ok, h + 1)
                    dve.tensor_copy(rt_seen[:], ident[:, 0:1])
                    for c in range(2):
                        rows = slice(c * C, (c + 1) * C)
                        dve.copy_predicated(attm[rows, :, rows], tri[rows, :].unsqueeze(1).broadcast_to([C, NT, C]),
                                            ps[rows, 7, :].rearrange("p (n w) -> p n w", n=NT)[:, :, rows]
                                            ).then_inc(attm_ok, 1)
                    dve.wait_ge(ds_ok, h * NS + NS)
                    for c in range(NS):
                        if c == 0:
                            up = dve.tensor_copy(S[:, 1, :], ps[:, 0, 0:GLA_DV])
                        else:
                            dve.wait_ge(S_ok, h * NS + c)
                            up = dve.scalar_tensor_tensor(S[:, c + 1, :], S[:, c, :], dec[:, c:c + 1], psd(c),
                                                          ALU.mult, ALU.add)
                        up.then_inc(S_ok, 1)
                    if h is not GLA_H - 1:
                        dve.wait_ge(r_ok, h + 1)
                        split(h + 1)
                    dve.wait_ge(sq_ok, h * NT + NT)
                    dve.tensor_scalar(ms[:], ss[:], 1.0 / GLA_DV, EPS, ALU.mult, ALU.add).then_inc(ms_ok, 1)
                    dve.wait_ge(root_ok, h + 1)
                    dve.reciprocal(rs[:], rt[:]).then_inc(rs_ok, 1)
                    dve.wait_ge(rs_ok, h + 1)
                    dve.wait_ge(rg_ok, h + 1)
                    for n in range(NT):
                        dve.scalar_tensor_tensor(og[:, n, :], psv(4, n), rs[:, n:n + 1], rg[:, n, :],
                                                 ALU.mult, ALU.mult).then_inc(og_ok, 1)
                    for e in range(2):
                        dve.wait_ge(oa_ok, 2 * h + e + 1)
                        dve.tensor_tensor(oa[1][:, h * 2 + e, :], ps[:, 6 + e, :], oa[0][:, h * 2 + e, :].bitcast(F32),
                                          ALU.subtract).then_inc(oal_ok, 1)

                steps(dve, GLA_H, step)

            @block.tensor
            def _(pe):
                pe.wait_ge(glr_lo, 1)
                for k in range(KD):
                    last = mm3(pe, ps[:, 6, :], (gh[:, k, :], gl[:, k, :]), (hh[:, k, :], hl[:, k, :]), k == 0, k == KD - 1)
                last.then_inc(glr_ok, 1)
                pe.wait_ge(glr_sb, 1)
                for h in range(GLA_H):
                    last = pe.matmul(ps[:, h, :], gk2[:, h * P:(h + 1) * P], glrT[:], start=True, stop=True)
                last.then_inc(gk_ok, 1)
                pe.wait_ge(gate_v, 1)

                def step(h):
                    pe.wait_ge(w_hi, h + 1)
                    pe.wait_ge(w_lo, h + 1)
                    after(pe, S_ok, h * NS)
                    for bank, col, sem in ((0, 0, q_ok), (1, P, k_ok)):
                        for k in range(KD):
                            last = mm3(pe, ps[:, bank, :], (wh[:, k, col:col + P], wl[:, k, col:col + P]),
                                       (hh[:, k, :], hl[:, k, :]), k == 0, k == KD - 1)
                        last.then_inc(sem, 1)
                    for bank, col, sem in ((2, 2 * P, v_ok), (4, 2 * P + GLA_DV, r_ok)):
                        if bank == 4:
                            after(pe, og_ok, h * NT)
                        for n in range(NT):
                            for k in range(KD):
                                rows = slice(n * P, (n + 1) * P)
                                cols = slice(col, col + GLA_DV)
                                last = mm3(pe, psv(bank, n), (hh[:, k, rows], hl[:, k, rows]),
                                           (wh[:, k, cols], wl[:, k, cols]), k == 0, k == KD - 1)
                        last.then_inc(sem, 1)
                    pe.wait_ge(qk_scaled, 5 * h + 1)
                    after(pe, oal_ok, 2 * h)
                    for n in range(NT):
                        last = pe.transpose(ps[:, 6, n * P:(n + 1) * P], ke[:, n * P:(n + 1) * P], ident[:])
                    last.then_inc(ke_turned, 1)
                    pe.wait_ge(qk_scaled, 5 * h + 5)
                    for n in range(NT):
                        rows = slice(n * P, (n + 1) * P)
                        last = pe.matmul(ps[:, 7, rows], ka[:, rows], qa[:, rows], start=True, stop=True)
                    last.then_inc(att_ok, 1)
                    pe.wait_ge(kend_ok, h + 1)
                    pe.wait_ge(v_sb, 2 * h + 2)
                    for c in range(NS):
                        rows = slice((c % 2) * C, (c % 2 + 1) * C)
                        last = pe.matmul(psd(c), kend[rows, c // 2, :], v[rows, c // 2, :], start=True, stop=True)
                        last.then_inc(ds_ok, 1)
                    pe.wait_ge(attm_ok, 2 * h + 2)
                    pe.wait_ge(r_sb, h + 1)
                    for n in range(NT):
                        pe.matmul(psv(4, n), attm[:, n, :], v[:, n, :], start=True, stop=False)
                        pe.wait_ge(S_ok, h * NS + min(2 * n + 1, NS))
                        if n:
                            pe.matmul(psv(4, n), qi[:, 0, n, :], S[:, 2 * n, :], start=False, stop=False)
                        pe.matmul(psv(4, n), qi[:, 1, n, :], S[:, 2 * n + 1, :], start=False, stop=True).then_inc(o_ok, 1)
                    pe.wait_ge(og_ok, h * NT + NT)
                    for e in range(2):
                        for n in range(NT):
                            last = pe.transpose(ps[:, 6 + e, n * P:(n + 1) * P], og[:, n, e * P:(e + 1) * P], ident[:])
                        last.then_inc(o_turned, 1)

                steps(pe, GLA_H, step)


def swa(nc, hh, hl, ob, ident, drams):
    w_dram, qg_dram, kg_dram, cos_dram, sin_dram, mask_dram, sinks_dram = drams
    NH = GRP + 1
    W = 2 * P
    with Phase(nc, "swa") as ph:
        raw = ph.sb("raw", [P, KD, SWA_COLS])
        wh = ph.sb("wh", [P, KD, SWA_COLS], F32R)
        wl = ph.sb("wl", [P, KD, SWA_COLS], F32R)
        gain = ph.sb("gain", [P, NH, HD])
        cos = ph.sb("cos", [P, NT, ROPE_HALF])
        sin = ph.sb("sin", [P, NT, ROPE_HALF])
        mask = ph.sb("mask", [P, W])
        sinks = ph.sb("sinks", [P, SWA_KV, GRP])
        sq = ph.sb("sq", [P, NT, NH, HD])
        ss = ph.sb("ss", [P, NT * NH])
        ms = ph.sb("ms", [P, NT * NH])
        rt = ph.sb("rt", [P, NT * NH])
        rs = ph.sb("rs", [P, NT * NH])
        qk = ph.sb("qk", [P, NT, NH + 1, HD])
        v = ph.sb("v", [P, NT, HD])
        ro = [ph.sb(f"ro{i}", [P, NT, NH, ROPE_HALF]) for i in range(4)]
        qT = ph.sb("qT", [P, 2, T])
        kT = ph.sb("kT", [P, T])
        sc = ph.sb("sc", [P, 2, GRP, W])
        mx = ph.sb("mx", [P, NT, GRP])
        m = ph.sb("m", [P, NT, GRP])
        nm = ph.sb("nm", [P, NT, GRP])
        sd = ph.sb("sd", [P, NT, GRP])
        se = ph.sb("se", [P, NT, GRP])
        den = ph.sb("den", [P, NT, GRP])
        dn = ph.sb("dn", [P, NT, GRP])
        rd = ph.sb("rd", [P, NT, GRP])
        pT = ph.sb("pT", [P, 2, 2, T])
        ps = ph.psum()
        names = ("small_in raw_in w_hi w_lo proj sq_ok ss_ok ms_ok root_ok rs_ok v_sb normed gained r1 r2 roped dup "
                 "turned qk_sb scored masked mx_ok m_ok negm sd_ok exp_ok se_ok dn_ok rd_ok p_ok p_turned pT_ok "
                 "pv_ok ob_hi ob_lo").split()
        (small_in, raw_in, w_hi, w_lo, proj, sq_ok, ss_ok, ms_ok, root_ok, rs_ok, v_sb, normed, gained, r1, r2, roped,
         dup, turned, qk_sb, scored, masked, mx_ok, m_ok, negm, sd_ok, exp_ok, se_ok, dn_ok, rd_ok, p_ok, p_turned,
         pT_ok, pv_ok, ob_hi, ob_lo) = (ph.sem(n) for n in names)
        x1, x2 = qk[:, :, 0:NH, 0:ROPE_HALF], qk[:, :, 0:NH, ROPE_HALF:2 * ROPE_HALF]
        cosb = cos[:].unsqueeze(2).broadcast_to([P, NT, NH, ROPE_HALF])
        sinb = sin[:].unsqueeze(2).broadcast_to([P, NT, NH, ROPE_HALF])

        def at(sem, h, n):
            return h * NT + n + 1

        with nc.Block() as block:
            @block.sync
            def _(sp):
                sp.dma_start(raw[:], w_dram[0]).then_inc(raw_in, 16)
                for g in range(GRP):
                    sp.dma_start(gain[:, g, :], qg_dram.partition_broadcast(P)).then_inc(small_in, 16)
                sp.dma_start(gain[:, GRP, :], kg_dram.partition_broadcast(P)).then_inc(small_in, 16)
                sp.dma_start(sinks[:], sinks_dram.partition_broadcast(P)).then_inc(small_in, 16)
                for dst, src in ((cos, cos_dram), (sin, sin_dram), (mask, mask_dram)):
                    sp.dma_start(dst[:], src).then_inc(small_in, 16)
                with sp.Fori(0, SWA_KV - 1) as h:
                    sp.wait_ge(w_hi, h + 1)
                    sp.wait_ge(w_lo, h + 1)
                    sp.dma_start(raw[:], w_dram[h + 1]).then_inc(raw_in, 16)

            @block.scalar
            def _(act):
                def split(h):
                    act.wait_ge(raw_in, 16 * (h + 1))
                    act.activation(wh[:], raw[:], ACT.Copy).then_inc(w_hi, 1)

                split(0)

                def step(h):
                    for n in range(NT):
                        act.wait_ge(proj, h * NT + n + 1)
                        after(act, ss_ok, h)
                        act.activation(sq[:, n, :, :].rearrange("p a b -> p (a b)"), ps[:, n, 0:NH * HD],
                                       ACT.Square).then_inc(sq_ok, 1)
                    if h is not SWA_KV - 1:
                        split(h + 1)
                    act.wait_ge(ms_ok, h + 1)
                    act.activation(rt[:], ms[:], ACT.Sqrt).then_inc(root_ok, 1)
                    after(act, pv_ok, h * NT)
                    act.wait_ge(normed, h + 1)
                    act.activation(v[:], ps[:, 0:NT, NH * HD:SWA_COLS], ACT.Copy).then_inc(v_sb, 1)
                    act.wait_ge(turned, h + 1)
                    for j in range(2):
                        act.activation(qT[:, j, :], ps[:, 4 + j, :], ACT.Copy).then_inc(qk_sb, 1)
                    act.activation(kT[:], ps[:, 6, :], ACT.Copy).then_inc(qk_sb, 1)

                    def exps(n):
                        act.wait_ge(negm, at(0, h, n))
                        for s in range(GRP):
                            act.activation(sc[:, n % 2, s, :], sc[:, n % 2, s, :], ACT.Exp, bias=nm[:, n, s:s + 1],
                                           accum_out=den[:, n, s:s + 1]).then_inc(exp_ok, 1)
                        act.wait_ge(sd_ok, at(0, h, n))
                        act.activation(se[:, n, :], sd[:, n, :], ACT.Exp).then_inc(se_ok, 1)

                    exps(0)
                    for n in range(NT):
                        if n + 1 < NT:
                            exps(n + 1)
                        act.wait_ge(p_turned, at(0, h, n))
                        for half in range(0 if n else 1, 2):
                            last = act.activation(pT[:, n % 2, half, :], ps[:, 4 + 2 * (n % 2) + half, :], ACT.Copy)
                        last.then_inc(pT_ok, 1)
                        act.wait_ge(pv_ok, at(0, h, n))
                        for odd in range(2):
                            act.activation(ob[0][odd * HD:(odd + 1) * HD, bass.ds(2 * h, 2), n * P:(n + 1) * P],
                                           ps[0:HD, 2 * (n % 2), odd * W:(odd + 1) * W].rearrange("p (a b) -> p a b", a=2),
                                           ACT.Copy).then_inc(ob_hi, 1)

                steps(act, SWA_KV, step)

            @block.gpsimd
            def _(pool):
                def step(h):
                    for n in range(NT):
                        pool.wait_ge(rd_ok, at(0, h, n))
                        pool.tensor_tensor(sc[:, n % 2, :, :], sc[:, n % 2, :, :],
                                           rd[:, n, :].unsqueeze(2).broadcast_to([P, GRP, W]), ALU.mult).then_inc(p_ok, 1)
                steps(pool, SWA_KV, step)

            @block.vector
            def _(dve):
                def split(h):
                    dve.wait_ge(w_hi, h + 1)
                    dve.tensor_tensor(wl[:], raw[:], wh[:].bitcast(F32), ALU.subtract).then_inc(w_lo, 1)

                split(0)
                dve.wait_ge(small_in, 16 * 9)

                def step(h):
                    dve.wait_ge(sq_ok, h * NT + NT)
                    dve.tensor_reduce(ss[:], sq[:].rearrange("p a b c -> p (a b) c"), AX_X, ALU.add).then_inc(ss_ok, 1)
                    dve.wait_ge(ss_ok, h + 1)
                    dve.tensor_scalar(ms[:], ss[:], 1.0 / HD, EPS, ALU.mult, ALU.add).then_inc(ms_ok, 1)
                    if h is not SWA_KV - 1:
                        split(h + 1)
                    dve.wait_ge(root_ok, h + 1)
                    dve.reciprocal(rs[:], rt[:]).then_inc(rs_ok, 1)
                    dve.wait_ge(rs_ok, h + 1)
                    after(dve, turned, h)
                    for n in range(NT):
                        last = dve.tensor_tensor(qk[:, n, 0:NH, :], ps[:, n, 0:NH * HD].rearrange("p (a b) -> p a b", a=NH),
                                                 rs[:, n * NH:(n + 1) * NH].unsqueeze(2).broadcast_to([P, NH, HD]), ALU.mult)
                    last.then_inc(normed, 1)
                    dve.wait_ge(normed, h + 1)
                    for n in range(NT):
                        last = dve.tensor_tensor(qk[:, n, 0:NH, :], qk[:, n, 0:NH, :], gain[:], ALU.mult)
                    last.then_inc(gained, 1)
                    dve.wait_ge(gained, h + 1)
                    dve.tensor_tensor(ro[0][:], x1, cosb, ALU.mult)
                    dve.tensor_tensor(ro[1][:], x2, sinb, ALU.mult)
                    dve.tensor_tensor(ro[2][:], x2, cosb, ALU.mult)
                    dve.tensor_tensor(ro[3][:], x1, sinb, ALU.mult).then_inc(r1, 1)
                    dve.wait_ge(r1, h + 1)
                    dve.tensor_tensor(x1, ro[0][:], ro[1][:], ALU.subtract)
                    dve.tensor_tensor(x2, ro[2][:], ro[3][:], ALU.add).then_inc(roped, 1)
                    dve.wait_ge(roped, h + 1)
                    dve.tensor_copy(qk[:, :, NH, :], qk[:, :, NH - 1, :]).then_inc(dup, 1)

                    def soft(n):
                        i = at(0, h, n)
                        dve.wait_ge(scored, i)
                        if n >= 2:
                            dve.wait_ge(p_turned, i - 2)
                        else:
                            after(dve, p_turned, h * NT)
                        cols = slice(0, W) if n else slice(P, W)
                        if n == 0:
                            dve.memset(sc[:, 0, :, 0:P], NEG)
                        dve.scalar_tensor_tensor(sc[:, n % 2, :, cols],
                                                 ps[:, 2 * (n % 2):2 * (n % 2) + 2, :].rearrange("p a (s w) -> p (a s) w", s=2)[:, :, cols],
                                                 HD ** -0.5, mask[:, cols].unsqueeze(1).broadcast_to([P, GRP, cols.stop - cols.start]),
                                                 ALU.mult, ALU.add).then_inc(masked, 1)
                        dve.wait_ge(masked, i)
                        dve.tensor_reduce(mx[:, n, :], sc[:, n % 2, :, :], AX_X, ALU.max).then_inc(mx_ok, 1)
                        dve.wait_ge(mx_ok, i)
                        dve.tensor_tensor(m[:, n, :], mx[:, n, :], sinks[:, h, :], ALU.max).then_inc(m_ok, 1)
                        dve.wait_ge(m_ok, i)
                        dve.tensor_scalar(nm[:, n, :], m[:, n, :], -1.0, None, ALU.mult).then_inc(negm, 1)
                        dve.tensor_tensor(sd[:, n, :], sinks[:, h, :], m[:, n, :], ALU.subtract).then_inc(sd_ok, 1)

                    soft(0)
                    for n in range(NT):
                        if n + 1 < NT:
                            soft(n + 1)
                        i = at(0, h, n)
                        dve.wait_ge(se_ok, i)
                        dve.tensor_tensor(dn[:, n, :], den[:, n, :], se[:, n, :], ALU.add).then_inc(dn_ok, 1)
                        dve.wait_ge(dn_ok, i)
                        dve.reciprocal(rd[:, n, :], dn[:, n, :]).then_inc(rd_ok, 1)
                        dve.wait_ge(ob_hi, 2 * i)
                        for odd in range(2):
                            rows = slice(odd * HD, (odd + 1) * HD)
                            last = dve.tensor_tensor(ob[1][rows, bass.ds(2 * h, 2), n * P:(n + 1) * P],
                                                     ps[0:HD, 2 * (n % 2), odd * W:(odd + 1) * W].rearrange("p (a b) -> p a b", a=2),
                                                     ob[0][rows, bass.ds(2 * h, 2), n * P:(n + 1) * P].bitcast(F32),
                                                     ALU.subtract)
                        last.then_inc(ob_lo, 1)

                steps(dve, SWA_KV, step)

            @block.tensor
            def _(pe):
                def step(h):
                    pe.wait_ge(w_hi, h + 1)
                    pe.wait_ge(w_lo, h + 1)
                    after(pe, ob_lo, h * NT)
                    for n in range(NT):
                        rows = slice(n * P, (n + 1) * P)
                        for k in range(KD):
                            last = mm3(pe, ps[:, n, 0:SWA_COLS], (hh[:, k, rows], hl[:, k, rows]),
                                       (wh[:, k, :], wl[:, k, :]), k == 0, k == KD - 1)
                        last.then_inc(proj, 1)
                    pe.wait_ge(dup, h + 1)
                    after(pe, pT_ok, h * NT)
                    for j in range(3):
                        for n in range(NT):
                            last = pe.transpose(ps[:, 4 + j, n * P:(n + 1) * P],
                                                qk[:, n, 2 * j:2 * j + 2, :].rearrange("p a b -> p (a b)"), ident[:])
                    last.then_inc(turned, 1)
                    pe.wait_ge(qk_sb, 3 * h + 3)
                    pe.wait_ge(v_sb, h + 1)

                    def score(n):
                        if n >= 2:
                            pe.wait_ge(ob_lo, h * NT + n - 1)
                        keys = slice((n - 1) * P, (n + 1) * P) if n else slice(0, P)
                        cols = slice(0, W) if n else slice(P, W)
                        for s in range(GRP):
                            half = slice((s // 2) * HD, (s // 2 + 1) * HD)
                            last = pe.matmul(ps[:, 2 * (n % 2) + s // 2, (s % 2) * W:(s % 2 + 1) * W][:, cols],
                                             qT[half, s % 2, n * P:(n + 1) * P], kT[half, keys], start=True, stop=True)
                        last.then_inc(scored, 1)

                    score(0)
                    for n in range(NT):
                        if n == 0:
                            score(1)
                        pe.wait_ge(p_ok, at(0, h, n))
                        if n >= 2:
                            pe.wait_ge(pT_ok, h * NT + n - 1)
                        for half in range(0 if n else 1, 2):
                            for s in range(GRP):
                                last = pe.transpose(ps[:, 4 + 2 * (n % 2) + half, s * P:(s + 1) * P],
                                                    sc[:, n % 2, s, half * P:(half + 1) * P], ident[:])
                        last.then_inc(p_turned, 1)
                        pe.wait_ge(pT_ok, at(0, h, n))
                        if n:
                            pe.matmul(ps[0:HD, 2 * (n % 2), :], v[:, n - 1, :], pT[:, n % 2, 0, :], start=True, stop=False)
                        pe.matmul(ps[0:HD, 2 * (n % 2), :], v[:, n, :], pT[:, n % 2, 1, :], start=(n == 0),
                                  stop=True).then_inc(pv_ok, 1)
                        if n + 2 < NT:
                            score(n + 2)

                steps(pe, SWA_KV, step)


def merge(nc, hh, hl, oa, ob, mt, w_dram):
    with Phase(nc, "mrg") as ph:
        raw = [ph.sb(f"raw{u}", [P, 2, KD, P]) for u in range(2)]
        wh = [ph.sb(f"wh{u}", [P, 2, KD, P], F32R) for u in range(2)]
        wl = [ph.sb(f"wl{u}", [P, 2, KD, P], F32R) for u in range(2)]
        sg = [ph.sb(f"sg{u}", [P, T]) for u in range(2)]
        pr = [ph.sb(f"pr{u}", [P, T]) for u in range(2)]
        mv = ph.sb("mv", [P, T])
        ps = ph.psum()
        raw_in, w_hi, w_lo, gemm, sig_ok, prod, sum_ok, mt_hi, mt_lo = (
            [ph.sem(f"{n}{u}") for u in range(2)] for n in
            ("raw_in", "w_hi", "w_lo", "gemm", "sig_ok", "prod", "sum_ok", "mt_hi", "mt_lo"))
        sum_ok, mt_hi, mt_lo = sum_ok[0], mt_hi[0], mt_lo[0]
        with nc.Block() as block:
            @block.sync
            def _(sp):
                def step(j):
                    for u in range(2):
                        after(sp, w_hi[u], j)
                        after(sp, w_lo[u], j)
                        sp.dma_start(raw[u][:], w_dram[j, u]).then_inc(raw_in[u], 16)
                steps(sp, KD, step)

            @block.scalar
            def _(act):
                def split(j, u):
                    act.wait_ge(raw_in[u], 16 * (j + 1))
                    after(act, gemm[u], 2 * j)
                    act.activation(wh[u][:], raw[u][:], ACT.Copy).then_inc(w_hi[u], 1)

                def step(j):
                    for u in range(2):
                        act.wait_ge(gemm[u], 2 * j + 1)
                        after(act, prod[u], j)
                        act.activation(sg[u][:], ps[:, 2 * u, :], ACT.Sigmoid).then_inc(sig_ok[u], 1)
                        if j is not KD - 1:
                            split(j + 1, u)
                    act.wait_ge(sum_ok, j + 1)
                    act.activation(mt[0][:, j, :], mv[:], ACT.Copy).then_inc(mt_hi, 1)

                split(0, 0)
                split(0, 1)
                steps(act, KD, step)

            @block.vector
            def _(dve):
                def split(j, u):
                    dve.wait_ge(w_hi[u], j + 1)
                    dve.tensor_tensor(wl[u][:], raw[u][:], wh[u][:].bitcast(F32), ALU.subtract).then_inc(w_lo[u], 1)

                def step(j):
                    for u in range(2):
                        dve.wait_ge(sig_ok[u], j + 1)
                        dve.wait_ge(gemm[u], 2 * j + 2)
                        dve.tensor_tensor(pr[u][:], sg[u][:], ps[:, 2 * u + 1, :], ALU.mult).then_inc(prod[u], 1)
                        if j is not KD - 1:
                            split(j + 1, u)
                    dve.wait_ge(prod[0], j + 1)
                    dve.wait_ge(prod[1], j + 1)
                    dve.tensor_tensor(mv[:], pr[0][:], pr[1][:], ALU.add).then_inc(sum_ok, 1)
                    dve.wait_ge(mt_hi, j + 1)
                    dve.tensor_tensor(mt[1][:, j, :], mv[:], mt[0][:, j, :].bitcast(F32), ALU.subtract).then_inc(mt_lo, 1)

                split(0, 0)
                split(0, 1)
                steps(dve, KD, step)

            @block.tensor
            def _(pe):
                def step(j):
                    for u, branch in ((0, oa), (1, ob)):
                        pe.wait_ge(w_hi[u], j + 1)
                        pe.wait_ge(w_lo[u], j + 1)
                        after(pe, prod[u], j)
                        for half, moving in ((0, (hh, hl)), (1, branch)):
                            for k in range(KD):
                                last = mm3(pe, ps[:, 2 * u + half, :], (wh[u][:, half, k, :], wl[u][:, half, k, :]),
                                           (moving[0][:, k, :], moving[1][:, k, :]), k == 0, k == KD - 1)
                            last.then_inc(gemm[u], 1)
                steps(pe, KD, step)


def out_projection(nc, tag, src, kt, w_dram, res_dram, x, store, post_gain=None):
    CB = 256
    NB = D // CB
    with Phase(nc, tag) as ph:
        raw = ph.sb("raw", [P, kt, CB])
        wh = [ph.sb(f"wh{u}", [P, kt, CB], F32R) for u in range(2)]
        wl = [ph.sb(f"wl{u}", [P, kt, CB], F32R) for u in range(2)]
        ss, ms, rt, rs = (ph.sb(n, [P, NT]) for n in ("ss", "ms", "rt", "rs"))
        ps = ph.psum()
        names = "res_in gain_in raw_in w_hi w_lo gemm y_ok sq_ok ms_ok root_ok rs_ok scaled gained x_ok stored".split()
        (res_in, gain_in, raw_in, w_hi, w_lo, gemm, y_ok, sq_ok, ms_ok, root_ok, rs_ok, scaled, gained, x_ok,
         stored) = (ph.sem(n) for n in names)
        if post_gain is not None:
            gain = ph.sb("gain", [P, D])
            res = flat(raw[:]).rearrange("p (n d) -> p n d", n=NT)
            junk = wh[0][:].rearrange("p a b -> p (a b)").rearrange("p (n d) -> p n d", n=NT)
        with nc.Block() as block:
            @block.sync
            def _(sp):
                for blk in range(NB):
                    if blk:
                        sp.wait_ge(w_hi, blk)
                        sp.wait_ge(w_lo, blk)
                    sp.dma_start(raw[:], w_dram[blk]).then_inc(raw_in, 16)
                    if blk == 0 and post_gain is None:
                        sp.dma_start(x[:], res_dram.rearrange("(n p) d -> p n d", p=P)).then_inc(res_in, 16)
                if post_gain is not None:
                    sp.dma_start(gain[:], post_gain.partition_broadcast(P)).then_inc(gain_in, 16)
                    sp.wait_ge(w_hi, NB)
                    sp.wait_ge(w_lo, NB)
                    sp.dma_start(res, res_dram.rearrange("(n p) d -> p n d", p=P)).then_inc(res_in, 16)
                for n in range(NT):
                    sp.wait_ge(x_ok, n + 1 if post_gain is not None else (NB - 1) * NT + n + 1)
                    sp.dma_start(store[n * P:(n + 1) * P, :], x[:, n, :]).then_inc(stored, 16)
                sp.wait_ge(stored, 16 * NT)

            @block.scalar
            def _(act):
                for blk in range(NB):
                    act.wait_ge(raw_in, 16 * (blk + 1))
                    if blk >= 2:
                        act.wait_ge(gemm, (blk - 1) * NT)
                    act.activation(wh[blk % 2][:], raw[:], ACT.Copy).then_inc(w_hi, 1)
                if post_gain is not None:
                    act.wait_ge(gemm, (NB - 1) * NT)
                    for n in range(NT):
                        act.wait_ge(y_ok, (NB - 1) * NT + n + 1)
                        act.activation(junk[:, n, :], x[:, n, :], ACT.Square, accum_out=ss[:, n:n + 1]).then_inc(sq_ok, 1)
                    act.wait_ge(ms_ok, 1)
                    act.activation(rt[:], ms[:], ACT.Sqrt).then_inc(root_ok, 1)

            @block.vector
            def _(dve):
                def split(blk):
                    dve.wait_ge(w_hi, blk + 1)
                    dve.tensor_tensor(wl[blk % 2][:], raw[:], wh[blk % 2][:].bitcast(F32),
                                      ALU.subtract).then_inc(w_lo, 1)

                split(0)
                split(1)
                if post_gain is None:
                    dve.wait_ge(res_in, 16)
                for blk in range(NB):
                    for n in range(NT):
                        dve.wait_ge(gemm, blk * NT + n + 1)
                        cols = slice(blk * CB, (blk + 1) * CB)
                        bank = ps[:, blk % 2 * 4 + n, 0:CB]
                        if post_gain is None:
                            dve.tensor_tensor(x[:, n, cols], bank, x[:, n, cols], ALU.add).then_inc(x_ok, 1)
                        else:
                            dve.tensor_copy(x[:, n, cols], bank).then_inc(y_ok, 1)
                    if blk + 2 < NB:
                        split(blk + 2)
                if post_gain is not None:
                    dve.wait_ge(sq_ok, NT)
                    dve.tensor_scalar(ms[:], ss[:], 1.0 / D, EPS, ALU.mult, ALU.add).then_inc(ms_ok, 1)
                    dve.wait_ge(root_ok, 1)
                    dve.reciprocal(rs[:], rt[:]).then_inc(rs_ok, 1)
                    dve.wait_ge(rs_ok, 1)
                    dve.wait_ge(gain_in, 16)
                    for n in range(NT):
                        dve.scalar_tensor_tensor(x[:, n, :], x[:, n, :], rs[:, n:n + 1], gain[:], ALU.mult,
                                                 ALU.mult).then_inc(scaled, 1)
                    dve.wait_ge(res_in, 16)
                    for n in range(NT):
                        dve.wait_ge(scaled, n + 1)
                        dve.tensor_tensor(x[:, n, :], x[:, n, :], res[:, n, :], ALU.add).then_inc(x_ok, 1)

            @block.tensor
            def _(pe):
                read = y_ok if post_gain is not None else x_ok
                for blk in range(NB):
                    pe.wait_ge(w_hi, blk + 1)
                    pe.wait_ge(w_lo, blk + 1)
                    if blk >= 2:
                        pe.wait_ge(read, (blk - 1) * NT)
                    for n in range(NT):
                        rows = slice(n * P, (n + 1) * P)
                        for k in range(kt):
                            last = mm3(pe, ps[:, blk % 2 * 4 + n, 0:CB], (src[0][:, k, rows], src[1][:, k, rows]),
                                       (wh[blk % 2][:, k, :], wl[blk % 2][:, k, :]), k == 0, k == kt - 1)
                        last.then_inc(gemm, 1)


def route(nc, hh, hl, iT, jT, gT, ident, drams):
    w_dram, keys_dram, iota_dram = drams
    K2 = PEER_K * PEER_K
    LOW = -3.4e38
    with Phase(nc, "rt") as ph:
        raw = ph.sb("raw", [P, KD, 2 * P])
        wh = ph.sb("wh", [P, KD, 2 * P], F32R)
        wl = ph.sb("wl", [P, KD, 2 * P], F32R)
        keys = ph.sb("keys", [P, 2, NKEYS])
        iota = ph.sb("iota", [P, NKEYS])
        qp = ph.sb("qp", [P, 2, T])
        s0 = ph.sb("s0", [P, NT, 2, NKEYS])
        s1 = ph.sb("s1", [P, NT, 2, NKEYS])
        top = ph.sb("top", [P, NT, 2, PEER_K])
        idx = ph.sb("idx", [P, NT, 2, PEER_K], U32)
        idf = ph.sb("idf", [P, NT, 2, PEER_K])
        cand = ph.sb("cand", [P, NT, PEER_K, PEER_K])
        cand1 = ph.sb("cand1", [P, NT, K2])
        best = ph.sb("best", [P, NT, PEER_K])
        pos = ph.sb("pos", [P, NT, PEER_K], U32)
        part = ph.sb("part", [P, 2, NT, PEER_K], U32)
        partf = ph.sb("partf", [P, 2, NT, PEER_K])
        hot = [ph.sb(f"hot{i}", [P, NT, PEER_K, PEER_K]) for i in range(2)]
        sub = ph.sb("sub", [P, NT, PEER_K])
        ex = ph.sb("ex", [P, NT, PEER_K])
        den = ph.sb("den", [P, NT])
        rden = ph.sb("rden", [P, NT])
        nat = [ph.sb(f"nat{i}", [P, NT, P]) for i in range(3)]
        tick = ph.sb("tick", [P, 1])
        ps = ph.psum()
        names = ("small_in raw_in keys_in w_hi w_lo qp_ok qp_sb scored s0_ok m1 x1 r1 m2 x2 idf_ok cand_ok "
                 "cm1 cr1 cm2 cx part_ok partf_ok eq_ok hot_ok pick_ok sub_ok ex_ok den_ok rden_ok gate_ok turned out_ok").split()
        (small_in, raw_in, keys_in, w_hi, w_lo, qp_ok, qp_sb, scored, s0_ok, m1, x1, r1, m2, x2, idf_ok, cand_ok,
         cm1, cr1, cm2, cx, part_ok, partf_ok, eq_ok, hot_ok, pick_ok, sub_ok, ex_ok, den_ok, rden_ok, gate_ok,
         turned, out_ok) = (ph.sem(n) for n in names)
        pairs = [(n, p) for n in range(NT) for p in range(2)]

        def bank(n, p):
            return ps[:, 2 + n // 2, (n % 2) * 2 * NKEYS + p * NKEYS:(n % 2) * 2 * NKEYS + (p + 1) * NKEYS]

        with nc.Block() as block:
            @block.sync
            def _(sp):
                sp.dma_start(raw[:], w_dram[0]).then_inc(raw_in, 16)
                sp.dma_start(keys[:], keys_dram[0]).then_inc(keys_in, 16)
                sp.dma_start(iota[:], iota_dram).then_inc(small_in, 16)
                with sp.Fori(0, PEER_H - 1) as h:
                    sp.wait_ge(w_hi, h + 1)
                    sp.wait_ge(w_lo, h + 1)
                    sp.dma_start(raw[:], w_dram[h + 1]).then_inc(raw_in, 16)
                    sp.wait_ge(scored, h + 1)
                    sp.dma_start(keys[:], keys_dram[h + 1]).then_inc(keys_in, 16)

            @block.scalar
            def _(act):
                def split(h):
                    act.wait_ge(raw_in, 16 * (h + 1))
                    act.activation(wh[:], raw[:], ACT.Copy).then_inc(w_hi, 1)

                split(0)

                def step(h):
                    act.wait_ge(qp_ok, h + 1)
                    after(act, scored, h)
                    for p in range(2):
                        last = act.activation(qp[:, p, :], ps[:, p, :], ACT.Copy)
                    last.then_inc(qp_sb, 1)
                    if h is not PEER_H - 1:
                        split(h + 1)
                    act.wait_ge(scored, h + 1)
                    after(act, r1, h)
                    after(act, x1, h)
                    for half in range(2):
                        last = act.activation(s0[:, 2 * half:2 * half + 2, :, :].rearrange("p a b c -> p (a b c)"),
                                              ps[:, 2 + half, :], ACT.Copy)
                    last.then_inc(s0_ok, 1)
                    act.wait_ge(sub_ok, h + 1)
                    act.activation(ex[:], sub[:], ACT.Exp).then_inc(ex_ok, 1)

                steps(act, PEER_H, step)
                for i, dst in enumerate((iT, jT, gT)):
                    act.wait_ge(turned, i + 1)
                    act.activation(dst[:], ps[:, i, :], ACT.Copy).then_inc(out_ok, 1)

            @block.vector
            def _(dve):
                def split(h):
                    dve.wait_ge(w_hi, h + 1)
                    dve.tensor_tensor(wl[:], raw[:], wh[:].bitcast(F32), ALU.subtract).then_inc(w_lo, 1)

                split(0)
                dve.wait_ge(small_in, 16)
                grid = [P, NT, PEER_K, PEER_K]

                def step(h):
                    if h is not PEER_H - 1:
                        split(h + 1)
                    dve.wait_ge(s0_ok, h + 1)
                    dve.tensor_copy(tick[:], iota[:, 0:1])
                    for n, p in pairs:
                        last = dve.max(top[:, n, p, 0:8], s0[:, n, p, :])
                    last.then_inc(m1, 1)
                    dve.wait_ge(m1, h + 1)
                    dve.tensor_copy(tick[:], iota[:, 0:1])
                    for n, p in pairs:
                        last = dve.max_index(idx[:, n, p, 0:8], top[:, n, p, 0:8], s0[:, n, p, :])
                    last.then_inc(x1, 1)
                    for n, p in pairs:
                        last = dve.match_replace(s1[:, n, p, :], top[:, n, p, 0:8], s0[:, n, p, :], LOW)
                    last.then_inc(r1, 1)
                    dve.wait_ge(r1, h + 1)
                    dve.tensor_copy(tick[:], iota[:, 0:1])
                    for n, p in pairs:
                        last = dve.max(top[:, n, p, 8:16], s1[:, n, p, :])
                    last.then_inc(m2, 1)
                    dve.wait_ge(m2, h + 1)
                    dve.tensor_copy(tick[:], iota[:, 0:1])
                    for n, p in pairs:
                        last = dve.max_index(idx[:, n, p, 8:16], top[:, n, p, 8:16], s1[:, n, p, :])
                    last.then_inc(x2, 1)
                    dve.tensor_tensor(cand[:], top[:, :, 0, :].unsqueeze(3).broadcast_to(grid),
                                      top[:, :, 1, :].unsqueeze(2).broadcast_to(grid), ALU.add).then_inc(cand_ok, 1)
                    dve.wait_ge(x2, h + 1)
                    dve.tensor_copy(idf[:], idx[:]).then_inc(idf_ok, 1)
                    dve.wait_ge(cand_ok, h + 1)
                    dve.tensor_copy(tick[:], iota[:, 0:1])
                    flat_cand = cand[:].rearrange("p n a b -> p n (a b)")
                    for n in range(NT):
                        last = dve.max(best[:, n, 0:8], flat_cand[:, n, :])
                    last.then_inc(cm1, 1)
                    dve.wait_ge(cm1, h + 1)
                    dve.tensor_copy(tick[:], iota[:, 0:1])
                    for n in range(NT):
                        dve.max_index(pos[:, n, 0:8], best[:, n, 0:8], flat_cand[:, n, :])
                        last = dve.match_replace(cand1[:, n, :], best[:, n, 0:8], flat_cand[:, n, :], LOW)
                    last.then_inc(cr1, 1)
                    dve.wait_ge(cr1, h + 1)
                    dve.tensor_copy(tick[:], iota[:, 0:1])
                    for n in range(NT):
                        last = dve.max(best[:, n, 8:16], cand1[:, n, :])
                    last.then_inc(cm2, 1)
                    dve.wait_ge(cm2, h + 1)
                    after(dve, ex_ok, h)
                    dve.tensor_tensor(sub[:], best[:], best[:, :, 0:1].broadcast_to([P, NT, PEER_K]),
                                      ALU.subtract).then_inc(sub_ok, 1)
                    dve.tensor_copy(tick[:], iota[:, 0:1])
                    for n in range(NT):
                        last = dve.max_index(pos[:, n, 8:16], best[:, n, 8:16], cand1[:, n, :])
                    last.then_inc(cx, 1)
                    dve.wait_ge(cx, h + 1)
                    dve.tensor_scalar(part[:, 0, :, :], pos[:], 4, None, ALU.logical_shift_right)
                    dve.tensor_scalar(part[:, 1, :, :], pos[:], 15, None, ALU.bitwise_and).then_inc(part_ok, 1)
                    dve.wait_ge(part_ok, h + 1)
                    dve.tensor_copy(partf[:], part[:]).then_inc(partf_ok, 1)
                    dve.wait_ge(partf_ok, h + 1)
                    dve.wait_ge(idf_ok, h + 1)
                    for p in range(2):
                        last = dve.tensor_tensor(hot[p][:], partf[:, p, :, :].unsqueeze(3).broadcast_to(grid),
                                                 iota[:, 0:PEER_K].unsqueeze(1).unsqueeze(1).broadcast_to(grid), ALU.is_equal)
                    last.then_inc(eq_ok, 1)
                    dve.wait_ge(eq_ok, h + 1)
                    for p in range(2):
                        last = dve.tensor_tensor(hot[p][:], hot[p][:], idf[:, :, p, :].unsqueeze(2).broadcast_to(grid),
                                                 ALU.mult)
                    last.then_inc(hot_ok, 1)
                    dve.wait_ge(hot_ok, h + 1)
                    for p in range(2):
                        last = dve.tensor_reduce(nat[p][:, :, bass.ds(h * PEER_K, PEER_K)], hot[p][:], AX_X, ALU.add)
                    last.then_inc(pick_ok, 1)
                    dve.wait_ge(ex_ok, h + 1)
                    dve.tensor_reduce(den[:], ex[:], AX_X, ALU.add).then_inc(den_ok, 1)
                    dve.wait_ge(den_ok, h + 1)
                    dve.reciprocal(rden[:], den[:]).then_inc(rden_ok, 1)
                    dve.wait_ge(rden_ok, h + 1)
                    dve.tensor_tensor(nat[2][:, :, bass.ds(h * PEER_K, PEER_K)], ex[:],
                                      rden[:].unsqueeze(2).broadcast_to([P, NT, PEER_K]), ALU.mult).then_inc(gate_ok, 1)

                steps(dve, PEER_H, step)

            @block.tensor
            def _(pe):
                def step(h):
                    pe.wait_ge(w_hi, h + 1)
                    pe.wait_ge(w_lo, h + 1)
                    for p in range(2):
                        for k in range(KD):
                            last = mm3(pe, ps[:, p, :], (wh[:, k, p * P:(p + 1) * P], wl[:, k, p * P:(p + 1) * P]),
                                       (hh[:, k, :], hl[:, k, :]), k == 0, k == KD - 1)
                    last.then_inc(qp_ok, 1)
                    pe.wait_ge(qp_sb, h + 1)
                    pe.wait_ge(keys_in, 16 * (h + 1))
                    after(pe, s0_ok, h)
                    for n, p in pairs:
                        last = pe.matmul(bank(n, p), qp[:, p, n * P:(n + 1) * P], keys[:, p, :], start=True, stop=True)
                    last.then_inc(scored, 1)

                steps(pe, PEER_H, step)
                pe.wait_ge(gate_ok, PEER_H)
                pe.wait_ge(pick_ok, PEER_H)
                for i in range(3):
                    for n in range(NT):
                        last = pe.transpose(ps[:, i, n * P:(n + 1) * P], nat[i][:, n, :], ident[:])
                    last.then_inc(turned, 1)


def gate_matrix(nc, iT, jT, gT, iota_dram, g_dram):
    GT = P
    Q = 4
    PER = GT // (2 * Q)
    with Phase(nc, "gm") as ph:
        iota = ph.sb("iota", [P, NKEYS])
        first = [ph.sb(f"first{u}", [P, Q, NKEYS]) for u in range(2)]
        second = [ph.sb(f"second{u}", [P, Q, NKEYS]) for u in range(2)]
        turn = ph.sb("turn", [P, 2])
        zero = ph.sb("zero", [P, 2 * Q])
        cols = ph.sb("cols", [P, 2 * Q])
        stage = [ph.sb(f"stage{u}", [P, NKEYS, GT]) for u in range(2)]
        ps = ph.psum()
        zero_ok, iota_in, cols_ok, stored = ph.sem("zero_ok"), ph.sem("iota_in"), ph.sem("cols_ok"), [ph.sem(f"stored{u}") for u in range(2)]
        first_ok, second_ok, built, staged = ([ph.sem(f"{n}{u}") for u in range(2)]
                                              for n in ("first_ok", "second_ok", "built", "staged"))
        groups = range(T // GT)

        def group_steps(eng, g, body):
            if g == 0:
                body(0, 0)
            with eng.Fori(0 if g else 1, PER) as q:
                body(g * PER + q, q)

        with nc.Block() as block:
            @block.sync
            def _(sp):
                sp.dma_start(iota[:], iota_dram).then_inc(iota_in, 16)
                for g in groups:
                    for u in range(2):
                        sp.wait_ge(staged[u], (g + 1) * PER)
                    sp.dma_start(g_dram[g], stage[g % 2][:]).then_inc(stored[g % 2], 16)
                for u in range(2):
                    sp.wait_ge(stored[u], 16 * len(groups) // 2)

            @block.gpsimd
            def _(pool):
                pool.memset(zero[:], 0.0).then_inc(zero_ok, 1)
                pool.wait_ge(zero_ok, 1)
                pool.wait_ge(iota_in, 16)

                def body(it, q):
                    after(pool, second_ok[1], it)
                    pool.tensor_tensor(cols[:], jT[:, bass.ds(it * (2 * Q), 2 * Q)], zero[:], ALU.add).then_inc(cols_ok, 1)
                    pool.wait_ge(cols_ok, it + 1)
                    for u in range(2):
                        after(pool, built[u], it)
                        pool.tensor_tensor(turn[:, u:u + 1], zero[:, 0:1], zero[:, 0:1], ALU.add)
                        for m in range(Q):
                            t = u * Q + m
                            last = pool.tensor_scalar(second[u][:, m, :], iota[:], cols[:, t:t + 1], None, ALU.is_equal)
                        last.then_inc(second_ok[u], 1)

                for g in groups:
                    group_steps(pool, g, body)

            @block.vector
            def _(dve):
                dve.wait_ge(iota_in, 16)

                def body(it, q):
                    for u in range(2):
                        after(dve, built[u], it)
                        for m in range(Q):
                            t = it * (2 * Q) + (u * Q + m)
                            last = dve.tensor_scalar(first[u][:, m, :], iota[:], iT[:, bass.ds(t, 1)],
                                                     gT[:, bass.ds(t, 1)], ALU.is_equal, ALU.mult)
                        last.then_inc(first_ok[u], 1)

                for g in groups:
                    group_steps(dve, g, body)

            @block.tensor
            def _(pe):
                def body(it, q):
                    for u in range(2):
                        pe.wait_ge(second_ok[u], it + 1)
                        pe.wait_ge(first_ok[u], it + 1)
                        after(pe, staged[u], it)
                        for m in range(Q):
                            last = pe.matmul(ps[:, u, m * P:(m + 1) * P], second[u][:, m, :], first[u][:, m, :],
                                             start=True, stop=True)
                        last.then_inc(built[u], 1)

                for g in groups:
                    group_steps(pe, g, body)

            @block.scalar
            def _(act):
                for g in groups:
                    if g >= 2:
                        act.wait_ge(stored[g % 2], 16 * (g // 2))

                    def body(it, q):
                        for u in range(2):
                            act.wait_ge(built[u], it + 1)
                            act.activation(stage[g % 2][:, :, bass.ds(q * (2 * Q) + u * Q, Q)],
                                           ps[:, u, :].rearrange("p (m i) -> p i m", m=Q), ACT.Copy).then_inc(staged[u], 1)
                    group_steps(act, g, body)


def experts(nc, hh, hl, x, u_dram, v_dram, g_dram, store):
    with Phase(nc, "ex") as ph:
        u_raw = ph.sb("u_raw", [P, KD, EB * P])
        uh = ph.sb("uh", [P, KD, EB * P], F32R)
        ul = ph.sb("ul", [P, KD, EB * P], F32R)
        v_raw = ph.sb("v_raw", [P, EB, D])
        vh = ph.sb("vh", [P, EB, D], F32R)
        vl = ph.sb("vl", [P, EB, D], F32R)
        gate = [ph.sb(f"gate{i}", [P, T // P, EB, P]) for i in range(2)]
        act_h = ph.sb("act_h", [P, EB, T])
        w = ph.sb("w", [P, EB, T])
        whi = ph.sb("whi", [P, EB, T], F32R)
        wlo = ph.sb("wlo", [P, EB, T], F32R)
        ps = ph.psum()
        names = "u_in v_in u_hi u_lo v_hi v_lo hid gelu_ok w_ok w_hi w_lo outp added stored".split()
        (u_in, v_in, u_hi, u_lo, v_hi, v_lo, hid, gelu_ok, w_ok, w_hi, w_lo, outp, added, stored) = (ph.sem(n) for n in names)
        g_in = [ph.sem(f"g_in{i}") for i in range(2)]
        PAIRS = NEB // 2

        def is_last(i, r):
            return i is PAIRS - 1 and r == 1

        with nc.Block() as block:
            @block.sync
            def _(sp):
                def step(i):
                    for r in range(2):
                        b = i * 2 + r
                        after(sp, u_hi, b)
                        after(sp, u_lo, b)
                        sp.dma_start(u_raw[:], u_dram[b]).then_inc(u_in, 16)
                        if isinstance(i, int) and i == 0:
                            after(sp, w_ok, 0)
                        else:
                            sp.wait_ge(w_ok, (b - 1) * EB)
                        sp.dma_start(gate[r][:], g_dram[:, :, bass.ds(b * EB, EB), :].rearrange("g j i t -> j g (i t)")
                                     ).then_inc(g_in[r], 16)
                        after(sp, v_hi, b)
                        after(sp, v_lo, b)
                        sp.dma_start(v_raw[:], v_dram[b]).then_inc(v_in, 16)
                steps(sp, PAIRS, step)
                for n in range(NT):
                    sp.wait_ge(added, (NEB - 1) * 8 + 2 * n + 2)
                    sp.dma_start(store[n * P:(n + 1) * P, :], x[:, n, :]).then_inc(stored, 16)
                sp.wait_ge(stored, 16 * NT)

            @block.scalar
            def _(act):
                def split_u(b):
                    act.wait_ge(u_in, 16 * (b + 1))
                    act.activation(uh[:], u_raw[:], ACT.Copy).then_inc(u_hi, 1)

                def split_v(b):
                    act.wait_ge(v_in, 16 * (b + 1))
                    act.activation(vh[:], v_raw[:], ACT.Copy).then_inc(v_hi, 1)

                split_u(0)
                split_v(0)

                def step(i):
                    for r in range(2):
                        b = i * 2 + r
                        after(act, w_ok, b * EB)
                        for e in range(EB + 1):
                            if e < EB:
                                act.wait_ge(hid, b * EB + e + 1)
                                act.activation(act_h[:, e, :], ps[:, 4 * r + e, :], ACT.Gelu).then_inc(gelu_ok, 1)
                            if e:
                                act.wait_ge(w_ok, b * EB + e)
                                if e == 1:
                                    after(act, outp, b * 8)
                                act.activation(whi[:, e - 1, :], w[:, e - 1, :], ACT.Copy).then_inc(w_hi, 1)
                        if not is_last(i, r):
                            split_u(b + 1)
                            act.wait_ge(outp, b * 8 + 8)
                            split_v(b + 1)
                steps(act, PAIRS, step)

            @block.vector
            def _(dve):
                def split_u(b):
                    dve.wait_ge(u_hi, b + 1)
                    dve.tensor_tensor(ul[:], u_raw[:], uh[:].bitcast(F32), ALU.subtract).then_inc(u_lo, 1)

                def split_v(b):
                    dve.wait_ge(v_hi, b + 1)
                    dve.tensor_tensor(vl[:], v_raw[:], vh[:].bitcast(F32), ALU.subtract).then_inc(v_lo, 1)

                split_u(0)
                split_v(0)

                def step(i):
                    for r in range(2):
                        b = i * 2 + r
                        dve.wait_ge(g_in[r], 16 * (i + 1))
                        after(dve, w_hi, b * EB)
                        for e in range(EB):
                            dve.wait_ge(gelu_ok, b * EB + e + 1)
                            dve.tensor_tensor(w[:, e, :].rearrange("p (a b) -> p a b", a=T // P),
                                              act_h[:, e, :].rearrange("p (a b) -> p a b", a=T // P),
                                              gate[r][:, :, e, :], ALU.mult).then_inc(w_ok, 1)
                            dve.wait_ge(w_hi, b * EB + e + 1)
                            dve.tensor_tensor(wlo[:, e, :], w[:, e, :], whi[:, e, :].bitcast(F32),
                                              ALU.subtract).then_inc(w_lo, 1)
                        if not is_last(i, r):
                            split_u(b + 1)
                        for o in range(8):
                            dve.wait_ge(outp, b * 8 + o + 1)
                            n, half = o // 2, o % 2
                            after(dve, added, b * 8)
                            dve.tensor_tensor(x[:, n, half * 512:(half + 1) * 512],
                                              ps[:, (4 * (1 - r) + o) % 8, :],
                                              x[:, n, half * 512:(half + 1) * 512], ALU.add).then_inc(added, 1)
                        if not is_last(i, r):
                            split_v(b + 1)
                steps(dve, PAIRS, step)

            @block.tensor
            def _(pe):
                def step(i):
                    for r in range(2):
                        b = i * 2 + r
                        pe.wait_ge(u_hi, b + 1)
                        pe.wait_ge(u_lo, b + 1)
                        for e in range(EB):
                            if e == 0:
                                if isinstance(b, int):
                                    after(pe, added, max(b * 8 - 4, 0))
                                else:
                                    pe.wait_ge(added, b * 8 - 4)
                            cols = slice(e * P, (e + 1) * P)
                            for k in range(KD):
                                last = mm3(pe, ps[:, 4 * r + e, :], (uh[:, k, cols], ul[:, k, cols]),
                                           (hh[:, k, :], hl[:, k, :]), k == 0, k == KD - 1)
                            last.then_inc(hid, 1)
                        pe.wait_ge(v_hi, b + 1)
                        pe.wait_ge(v_lo, b + 1)
                        after(pe, added, b * 8)
                        for turn in range(2):
                            if turn == 1:
                                pe.wait_ge(gelu_ok, b * EB + EB)
                            for first, some in ((True, range(EB - 1)), (False, range(EB - 1, EB))):
                                for o in range(4 * turn, 4 * turn + 4):
                                    n, half = o // 2, o % 2
                                    for e in some:
                                        if turn == 0 and o == 0:
                                            pe.wait_ge(w_lo, b * EB + e + 1)
                                        rows = slice(n * P, (n + 1) * P)
                                        cols = slice(half * 512, (half + 1) * 512)
                                        last = mm3(pe, ps[:, (4 * (1 - r) + o) % 8, :], (whi[:, e, rows], wlo[:, e, rows]),
                                                   (vh[:, e, cols], vl[:, e, cols]), e == 0, e == EB - 1)
                                    if not first:
                                        last.then_inc(outp, 1)
                steps(pe, PAIRS, step)


def gdn(nc, hh, hl, ot, ident, g_dram, sd_dram, drams):
    w_dram, b_dram, a_dram, conv_dram, alog_dram, dt_dram, gain_dram, reset_dram, masks_dram = drams
    KH, VH, NL = GDN_KH, GDN_VH, 6
    with Phase(nc, "gdn") as ph:
        raw = ph.sb("raw", [P, KD, 2 * P])
        wa = (ph.sb("wah", [P, KD, 2 * P], F32R), ph.sb("wal", [P, KD, 2 * P], F32R))
        wb = (ph.sb("wbh", [P, KD, 2 * P], F32R), ph.sb("wbl", [P, KD, 2 * P], F32R))
        cin = ph.sb("cin", [P, 4 * (T + 3)])
        cin4 = cin[:].rearrange("p (a b) -> p a b", a=4)
        cs = ph.sb("cs", [P, 4, T])
        conv = ph.sb("conv", [P, KH, 4, 4])
        gain = ph.sb("gain", [P, P])
        masks = ph.sb("masks", [P, NL + 2, P])
        cols = ph.sb("cols", [P, 4, NT, VH])
        cc = ph.sb("cc", [P, 4, NT, 2])
        be = ph.sb("be", [P, NT, 2])
        knq = ph.sb("knq", [P, 2, NT, P])
        kn, qn = knq[:, 0, :, :], knq[:, 1, :, :]
        knT = ph.sb("knT", [P, NT, P])
        qnT = ph.sb("qnT", [P, NT, P])
        kbg = ph.sb("kbg", [P, NT, 2, P])
        kdec = ph.sb("kdec", [P, NT, 2, P])
        vb = ph.sb("vb", [P, NT, 2, P])
        qd = ph.sb("qd", [P, NT, 2, P])
        qdT = ph.sb("qdT", [P, 2, NT, P])
        gz = ph.sb("gz", [P, 2 * T])
        dd = ph.sb("dd", [P, NT, 2, P])
        am = ph.sb("am", [P, NT, 2, P])
        qkt = ph.sb("qkt", [P, NT, 2, P])
        sdec = ph.sb("sdec", [P, 2, NCH])
        S = ph.sb("S", [P, 4, 2, P])
        ss, ms, rt, rs = (ph.sb(n, [P, 2, NT]) for n in ("ss", "ms", "rt", "rs"))
        os_, om, ort, ors = (ph.sb(n, [P, NT, 2]) for n in ("os", "om", "ort", "ors"))
        small = ph.sb("small", [VH, 4])
        ps = ph.psum()
        U = cin[:, 0:8 * P].rearrange("p (n a w) -> p n a w", n=NT, a=2)
        Tm = cin[:, 8 * P:16 * P].rearrange("p (n a w) -> p n a w", n=NT, a=2)
        Y = flat(cs[:])[:, 0:8 * P].rearrange("p (n a w) -> p n a w", n=NT, a=2)
        As = flat(cs[:])[:, 8 * P:16 * P].rearrange("p (n a w) -> p n a w", n=NT, a=2)
        vn, u, og = qd, dd, am
        wT = knq[:].rearrange("p a n w -> p (a n w)").rearrange("p (n a w) -> p n a w", n=NT, a=2)
        grow = gz[:].rearrange("p (a n w) -> p n a w", a=2, n=NT)
        zg = gz[:].rearrange("p (n b) -> p n b", n=NT)
        rows = [flat(cs[:])[0:VH, i * T:(i + 1) * T] for i in range(4)]
        rows += [kbg[:].rearrange("p a b c -> p (a b c)")[0:VH, i * T:(i + 1) * T] for i in range(2)]
        yrow, erow, grow_, beta, egrow, ekrow = rows
        reset = vb[:].rearrange("p a b c -> p (a b c)")[0:VH, 0:T]
        dlrow = vb[:].rearrange("p a b c -> p (a b c)")[0:VH, T:2 * T]
        sdrow = kdec[:].rearrange("p a b c -> p (a b c)")[0:VH, 0:NCH]

        names = ("small_in g_in raw_in a_hi a_lo b_hi b_lo zeroed pre_w pre_lo pre_mm row_v row_a row_t cols_ok stored "
                 "qk_ok v_ok z_ok cin_ok cc_ok be_ok tap silu_ok natural sq_ok ms_ok root_ok rs_ok kq_ok prods kq_turned kqT_ok "
                 "kk_ok qd_turned qdT_ok dd_ok lim exp_ok masked prod2 a_ok t_ok t_turned u_ok as1_ok "
                 "u_mm u_sb w_sb vp_ok vn_ok ds_ok S_ok o_ok og_ok osq_ok om_ok oroot_ok ors_ok z_sb zg_ok normed "
                 "o_turned hi_ok lo_ok tz").split()
        s = {n: ph.sem(n) for n in names}
        (small_in, g_in, raw_in, a_hi, a_lo, b_hi, b_lo, zeroed, pre_w, pre_lo, pre_mm, row_v, row_a, row_t, cols_ok,
         stored, qk_ok, v_ok, z_ok, cin_ok, cc_ok, be_ok, tap, silu_ok, natural, sq_ok, ms_ok, root_ok, rs_ok, kq_ok,
         prods, kq_turned, kqT_ok, kk_ok, qd_turned, qdT_ok, dd_ok, lim, exp_ok, masked, prod2, a_ok, t_ok, t_turned,
         u_ok, as1_ok, u_mm, u_sb, w_sb, vp_ok, vn_ok, ds_ok, S_ok, o_ok, og_ok, osq_ok,
         om_ok, oroot_ok, ors_ok, z_sb, zg_ok, normed, o_turned, hi_ok, lo_ok, tz) = (s[n] for n in names)
        as_ok, y_mm, y_ok, u_mm_lv, t_mm_lv, u_up, t_up = (
            [ph.sem(f"{n}{half}") for half in range(2)]
            for n in ("as_ok", "y_mm", "y_ok", "u_mm_lv", "t_mm_lv", "u_up", "t_up"))
        full = [P, NT, 2, P]
        last_h = KH - 1

        def per(v):
            return v.unsqueeze(3).broadcast_to(full)

        def both(v):
            return v.unsqueeze(2).broadcast_to(full)

        def every(i):
            return masks[:, i, :].unsqueeze(1).unsqueeze(1).broadcast_to(full)

        def two(bank):
            return ps[:, bank:bank + 2, :].rearrange("p x (n a w) -> p (x n) a w", n=2, a=2)

        def cell(bank, n, a):
            return ps[:, bank + n // 2, ((n % 2) * 2 + a) * P:((n % 2) * 2 + a + 1) * P]

        def halved(ap, half):
            return ap[:, 2 * half:2 * half + 2, :, :]

        def some(half):
            return problems[4 * half:4 * half + 4]

        problems = [(n, a) for n in range(NT) for a in range(2)]

        with nc.Block() as block:
            @block.sync
            def _(sp):
                sp.dma_start(raw[:, :, 0:VH], b_dram).then_inc(small_in, 16)
                sp.dma_start(raw[:, :, P:P + VH], a_dram).then_inc(small_in, 16)
                sp.dma_start(small[:, 0:1], alog_dram).then_inc(small_in, 16)
                sp.dma_start(small[:, 1:2], dt_dram).then_inc(small_in, 16)
                sp.dma_start(conv[:], conv_dram).then_inc(small_in, 16)
                sp.dma_start(gain[:], gain_dram.partition_broadcast(P)).then_inc(small_in, 16)
                sp.dma_start(masks[:], masks_dram).then_inc(small_in, 16)
                sp.dma_start(reset, reset_dram[0:VH, :]).then_inc(small_in, 16)
                sp.wait_ge(pre_lo, 2)
                sp.dma_start(raw[:], w_dram[0, 0]).then_inc(raw_in, 16)
                sp.wait_ge(row_v, 6)
                sp.dma_start(g_dram, grow_).then_inc(stored, 16)
                sp.wait_ge(row_a, 7)
                sp.dma_start(sd_dram, sdrow).then_inc(stored, 16)
                sp.wait_ge(stored, 32)

                def values_and_gates(h):
                    sp.wait_ge(a_hi, 2 * h + 1)
                    sp.wait_ge(a_lo, 2 * h + 1)
                    sp.dma_start(raw[:], w_dram[h, 1]).then_inc(raw_in, 16)
                    sp.wait_ge(b_hi, h + 1)
                    sp.wait_ge(b_lo, h + 1)
                    sp.dma_start(raw[:], w_dram[h, 2]).then_inc(raw_in, 16)

                values_and_gates(0)

                def step(h):
                    after(sp, normed, h)
                    sp.dma_start(gz[:].rearrange("p (a b) -> p a b", a=2),
                                 g_dram[bass.ds(h * 2, 2), :].partition_broadcast(P)).then_inc(g_in, 16)
                    after(sp, S_ok, h * (NCH - 1))
                    sp.dma_start(sdec[:], sd_dram[bass.ds(h * 2, 2), :].partition_broadcast(P)).then_inc(g_in, 16)
                    if h is not last_h:
                        sp.wait_ge(a_hi, 2 * h + 2)
                        sp.wait_ge(a_lo, 2 * h + 2)
                        sp.dma_start(raw[:], w_dram[h + 1, 0]).then_inc(raw_in, 16)
                        values_and_gates(h + 1)
                steps(sp, KH, step)

            @block.gpsimd
            def _(pool):
                for w in (wa[0], wa[1], wb[0], wb[1]):
                    pool.memset(w[:].bitcast(F32)[:, :, 0:P], 0.0).then_inc(zeroed, 1)
                pool.wait_ge(small_in, 16 * 8)

                def low(w, hi_ok, lo_done, count):
                    pool.wait_ge(hi_ok, count)
                    pool.tensor_tensor(w[1][:], raw[:], w[0][:].bitcast(F32), ALU.subtract).then_inc(lo_done, 1)

                low(wa, a_hi, a_lo, 1)
                low(wb, b_hi, b_lo, 1)
                low(wa, a_hi, a_lo, 2)

                def step(h):
                    pool.wait_ge(z_sb, h + 1)
                    pool.tensor_tensor(gz[:].rearrange("p (n w) -> p n w", w=P), gz[:].rearrange("p (n w) -> p n w", w=P),
                                       gain[:].unsqueeze(1).broadcast_to([P, 2 * NT, P]), ALU.mult).then_inc(zg_ok, 1)
                    if h is not last_h:
                        low(wa, a_hi, a_lo, 2 * h + 3)
                        low(wb, b_hi, b_lo, h + 2)
                        low(wa, a_hi, a_lo, 2 * h + 4)
                steps(pool, KH, step)

            @block.scalar
            def _(act):
                act.wait_ge(small_in, 16 * 8)
                act.wait_ge(zeroed, 4)
                act.activation(wa[0][:, :, 0:VH], raw[:, :, 0:VH], ACT.Copy).then_inc(pre_w, 1)
                act.activation(wb[0][:, :, 0:VH], raw[:, :, P:P + VH], ACT.Copy).then_inc(pre_w, 1)
                act.activation(small[:, 2:3], small[:, 0:1], ACT.Exp).then_inc(row_a, 1)
                act.wait_ge(pre_mm, 1)
                act.activation(beta, ps[0:VH, 6, :], ACT.Sigmoid).then_inc(row_a, 1)
                act.wait_ge(row_v, 2)
                act.activation(erow, erow, ACT.Exp).then_inc(row_a, 1)
                act.wait_ge(row_v, 3)
                act.activation(erow, erow, ACT.Ln).then_inc(row_a, 1)
                act.wait_ge(row_v, 7)
                act.activation(egrow, grow_, ACT.Exp).then_inc(row_a, 1)
                act.activation(ekrow, dlrow, ACT.Exp).then_inc(row_a, 1)
                act.activation(sdrow, grow_.rearrange("p (c w) -> p c w", c=NCH)[:, :, C - 1], ACT.Exp).then_inc(row_a, 1)
                act.wait_ge(row_t, 1)
                act.activation(cols[:].rearrange("p a b c -> p (a b c)"), ps[:, 5, 0:4 * NT * VH], ACT.Copy).then_inc(cols_ok, 1)

                def split_qk(h):
                    act.wait_ge(raw_in, 48 * h + 16)
                    act.activation(wa[0][:], raw[:], ACT.Copy).then_inc(a_hi, 1)

                def split_v(h):
                    act.wait_ge(raw_in, 48 * h + 32)
                    act.activation(wb[0][:], raw[:], ACT.Copy).then_inc(b_hi, 1)

                def split_z(h):
                    act.wait_ge(qk_ok, h + 1)
                    act.wait_ge(raw_in, 48 * h + 48)
                    act.activation(wa[0][:], raw[:], ACT.Copy).then_inc(a_hi, 1)

                act.wait_ge(pre_mm, 2)
                split_qk(0)
                split_v(0)
                split_z(0)

                def step(h):
                    act.wait_ge(qk_ok, h + 1)
                    after(act, u_mm, 2 * h)
                    act.activation(cin4[:, 0:2, 3:T + 3], ps[:, 0:2, :], ACT.Copy).then_inc(cin_ok, 1)
                    act.wait_ge(v_ok, h + 1)
                    act.activation(cin4[:, 2:4, 3:T + 3], ps[:, 2:4, :], ACT.Copy).then_inc(cin_ok, 1)
                    act.wait_ge(tap, 5 * h + 5)
                    act.activation(flat(cs[:]), flat(cs[:]), ACT.Silu).then_inc(silu_ok, 1)
                    act.wait_ge(dd_ok, h + 1)
                    act.wait_ge(z_ok, h + 1)
                    for half in range(2):
                        last = act.activation(gz[:, half * T:(half + 1) * T], ps[:, 4 + half, :], ACT.Silu)
                    last.then_inc(z_sb, 1)
                    act.wait_ge(natural, h + 1)
                    after(act, u_mm, 2 * h)
                    for j in range(2):
                        for n in range(NT):
                            last = act.activation(kbg[:, n, j, :], ps[:, j, n * P:(n + 1) * P], ACT.Square,
                                                  accum_out=ss[:, j, n:n + 1])
                    last.then_inc(sq_ok, 1)
                    act.wait_ge(ms_ok, h + 1)
                    act.activation(rt[:], ms[:], ACT.Sqrt).then_inc(root_ok, 1)
                    for j, dst in enumerate((knT, qnT)):
                        act.wait_ge(kq_turned, 2 * h + j + 1)
                        act.activation(flat(dst[:]), ps[:, 6 + j, :], ACT.Copy).then_inc(kqT_ok, 1)
                    act.wait_ge(lim, 2 * h + 2)
                    act.activation(am[:].rearrange("p a b c -> p (a b c)"), am[:].rearrange("p a b c -> p (a b c)"),
                                   ACT.Exp).then_inc(exp_ok, 1)
                    act.activation(qkt[:].rearrange("p a b c -> p (a b c)"), qkt[:].rearrange("p a b c -> p (a b c)"),
                                   ACT.Exp, scale=-1.0).then_inc(exp_ok, 1)
                    act.wait_ge(qd_turned, h + 1)
                    for a in range(2):
                        last = act.activation(flat(qdT[:, a, :, :]), ps[:, a, :], ACT.Copy)
                    last.then_inc(qdT_ok, 1)
                    act.wait_ge(t_turned, h + 1)
                    for half in range(2):
                        act.activation(halved(U, half), halved(two(2), half), ACT.Copy).then_inc(u_ok, 1)
                    for lv in range(1, NL):
                        for half in range(2):
                            act.wait_ge(y_mm[half], h * (NL - 1) + lv)
                            act.activation(halved(Y, half), halved(two(0), half), ACT.Copy).then_inc(y_ok[half], 1)
                    if h is not last_h:
                        split_qk(h + 1)
                    act.wait_ge(u_mm, 2 * h + 1)
                    act.activation(u[:], two(0), ACT.Copy).then_inc(u_sb, 1)
                    act.wait_ge(u_mm, 2 * h + 2)
                    act.activation(wT, two(2), ACT.Copy).then_inc(w_sb, 1)
                    for n in range(NT):
                        act.wait_ge(o_ok, h * NT + n + 1)
                        for c in range(2):
                            part = slice(c * C, (c + 1) * C)
                            last = act.activation(og[part, n, :, :], ps[part, 6 + n % 2, c * 2 * P:(c + 1) * 2 * P].rearrange(
                                "p (a w) -> p a w", a=2), ACT.Copy)
                        last.then_inc(og_ok, 1)
                        if h is not last_h:
                            if n == 0:
                                split_v(h + 1)
                            if n == 2:
                                split_z(h + 1)
                    act.wait_ge(og_ok, h * NT + NT)
                    for n, a in problems:
                        last = act.activation(kdec[:, n, a, :], og[:, n, a, :], ACT.Square, accum_out=os_[:, n, a:a + 1])
                    last.then_inc(osq_ok, 1)
                    act.wait_ge(om_ok, h + 1)
                    act.activation(ort[:], om[:], ACT.Sqrt).then_inc(oroot_ok, 1)
                    act.wait_ge(o_turned, h + 1)
                    act.activation(ot[0][:, bass.ds(2 * h, 2), :], ps[:, 6:8, :], ACT.Copy).then_inc(hi_ok, 1)

                steps(act, KH, step)

            @block.vector
            def _(dve):
                dve.wait_ge(pre_w, 2)
                dve.tensor_tensor(wa[1][:, :, 0:VH], raw[:, :, 0:VH], wa[0][:, :, 0:VH].bitcast(F32), ALU.subtract).then_inc(pre_lo, 1)
                dve.tensor_tensor(wb[1][:, :, 0:VH], raw[:, :, P:P + VH], wb[0][:, :, 0:VH].bitcast(F32), ALU.subtract).then_inc(pre_lo, 1)
                dve.wait_ge(pre_mm, 2)
                dve.tensor_scalar(yrow, ps[0:VH, 7, :], small[:, 1:2], None, ALU.add).then_inc(tz, 1)
                dve.wait_ge(tz, 1)
                dve.tensor_scalar(erow, yrow, 0.0, 2.0, ALU.min, ALU.mult).then_inc(row_v, 1)
                dve.wait_ge(row_v, 1)
                dve.tensor_tensor(erow, erow, yrow, ALU.subtract).then_inc(row_v, 1)
                dve.wait_ge(row_a, 3)
                dve.tensor_scalar(erow, erow, 1.0, None, ALU.add).then_inc(row_v, 1)
                dve.wait_ge(row_a, 4)
                dve.scalar_tensor_tensor(yrow, yrow, 0.0, erow, ALU.max, ALU.add).then_inc(row_v, 1)
                dve.wait_ge(row_v, 4)
                dve.tensor_scalar(yrow, yrow, small[:, 2:3], -1.0, ALU.mult, ALU.mult).then_inc(row_v, 1)
                dve.wait_ge(row_v, 5)
                dve.tensor_tensor_scan(grow_, reset, yrow, 0.0, ALU.mult, ALU.add).then_inc(row_v, 1)
                dve.wait_ge(row_v, 6)
                g3 = grow_.rearrange("p (c w) -> p c w", c=NCH)
                dve.tensor_tensor(dlrow.rearrange("p (c w) -> p c w", c=NCH), g3[:, :, C - 1:C].broadcast_to([VH, NCH, C]),
                                  g3, ALU.subtract).then_inc(row_v, 1)
                dve.wait_ge(cols_ok, 1)

                def step(h):
                    dve.tensor_copy(cc[:], cols[:, :, :, bass.ds(2 * h, 2)]).then_inc(cc_ok, 1)
                    dve.wait_ge(cc_ok, h + 1)
                    g_c, beta_c, eg_c, ek_c = (cc[:, i, :, :] for i in range(4))
                    dve.tensor_tensor(be[:], beta_c, eg_c, ALU.mult).then_inc(be_ok, 1)
                    dve.wait_ge(cin_ok, 2 * h + 2)
                    dve.memset(cin4[:, :, 0:3], 0.0).then_inc(tap, 1)
                    dve.wait_ge(tap, 5 * h + 1)
                    for j in range(4):
                        for g in range(4):
                            wj = conv[:, h, g, j:j + 1]
                            if j == 0:
                                last = dve.tensor_scalar(cs[:, g, :], cin4[:, g, 0:T], wj, None, ALU.mult)
                            else:
                                last = dve.scalar_tensor_tensor(cs[:, g, :], cin4[:, g, j:j + T], wj, cs[:, g, :],
                                                                ALU.mult, ALU.add)
                        last.then_inc(tap, 1)
                        dve.wait_ge(tap, 5 * h + j + 2)
                    dve.wait_ge(g_in, 32 * h + 32)
                    dve.tensor_tensor(dd[:], per(g_c), grow, ALU.subtract).then_inc(dd_ok, 1)
                    dve.wait_ge(dd_ok, h + 1)
                    after(dve, normed, h)
                    dve.tensor_scalar(am[:], dd[:], 0.0, None, ALU.min).then_inc(lim, 1)
                    dve.tensor_scalar(qkt[:], dd[:], 0.0, None, ALU.max).then_inc(lim, 1)
                    dve.wait_ge(sq_ok, h + 1)
                    dve.tensor_scalar(ms[:], ss[:], 1.0, EPS, ALU.mult, ALU.add).then_inc(ms_ok, 1)
                    dve.wait_ge(root_ok, h + 1)
                    dve.reciprocal(rs[:], rt[:]).then_inc(rs_ok, 1)
                    dve.wait_ge(rs_ok, h + 1)
                    shape = [P, NT, P]
                    dve.tensor_tensor(kn, ps[:, 1, :].rearrange("p (n w) -> p n w", n=NT),
                                      rs[:, 1, :].unsqueeze(2).broadcast_to(shape), ALU.mult).then_inc(kq_ok, 1)
                    dve.scalar_tensor_tensor(qn, ps[:, 0, :].rearrange("p (n w) -> p n w", n=NT), P ** -0.5,
                                             rs[:, 0, :].unsqueeze(2).broadcast_to(shape), ALU.mult, ALU.mult).then_inc(kq_ok, 1)
                    dve.wait_ge(kq_ok, 2 * h + 2)
                    dve.wait_ge(be_ok, h + 1)
                    dve.tensor_tensor(qd[:], both(qn), per(eg_c), ALU.mult).then_inc(prods, 1)
                    dve.tensor_tensor(vb[:], ps[:, 2:4, :].rearrange("p a (n w) -> p n a w", n=NT), per(beta_c),
                                      ALU.mult).then_inc(prods, 1)
                    dve.wait_ge(exp_ok, 2 * h + 2)
                    dve.tensor_tensor(am[:], am[:], every(0), ALU.mult)
                    dve.tensor_tensor(qkt[:], qkt[:], every(1), ALU.mult).then_inc(masked, 1)
                    dve.tensor_tensor(kbg[:], both(kn), per(be[:]), ALU.mult).then_inc(prods, 1)
                    dve.wait_ge(masked, h + 1)
                    dve.tensor_tensor(am[:], am[:], per(beta_c), ALU.mult).then_inc(prod2, 1)
                    dve.tensor_tensor(kdec[:], both(kn), per(ek_c), ALU.mult).then_inc(prods, 1)
                    dve.wait_ge(kk_ok, h + 1)
                    dve.wait_ge(prod2, h + 1)
                    dve.tensor_tensor(am[:], am[:], both(ps[:, 6, :].rearrange("p (n w) -> p n w", n=NT)),
                                      ALU.mult).then_inc(a_ok, 1)
                    dve.tensor_tensor(qkt[:], qkt[:], both(ps[:, 7, :].rearrange("p (n w) -> p n w", n=NT)),
                                      ALU.mult).then_inc(a_ok, 1)
                    dve.wait_ge(a_ok, 2 * h + 2)
                    dve.tensor_tensor(As, am[:], every(2), ALU.mult).then_inc(as1_ok, 1)
                    dve.wait_ge(as1_ok, h + 1)
                    dve.tensor_tensor(Tm, ident[:].unsqueeze(1).unsqueeze(1).broadcast_to(full), As,
                                      ALU.subtract).then_inc(t_ok, 1)
                    dve.wait_ge(t_ok, h + 1)
                    dve.wait_ge(u_ok, 2 * h + 2)
                    for lv in range(1, NL):
                        base = h * (NL - 1) + lv
                        for half in range(2):
                            if lv > 1:
                                dve.wait_ge(y_mm[half], base - 1)
                            dve.tensor_tensor(halved(As, half), halved(am[:], half), halved(every(2 + lv), half),
                                              ALU.mult).then_inc(as_ok[half], 1)
                        for half in range(2):
                            dve.wait_ge(u_mm_lv[half], base)
                            dve.tensor_tensor(halved(U, half), halved(U, half), halved(two(2), half),
                                              ALU.subtract).then_inc(u_up[half], 1)
                        for half in range(2):
                            if lv < NL - 1:
                                dve.wait_ge(t_mm_lv[half], h * (NL - 2) + lv)
                                dve.tensor_tensor(halved(Tm, half), halved(Tm, half), halved(two(6), half),
                                                  ALU.subtract).then_inc(t_up[half], 1)
                    dve.wait_ge(u_sb, h + 1)
                    NS = NCH - 1
                    for i in range(NCH):
                        n, part = i // 2, slice((i % 2) * C, (i % 2 + 1) * C)
                        if i == 0:
                            dve.wait_ge(qd_turned, h + 1)
                            dve.tensor_copy(vn[part, n, :, :], u[part, n, :, :]).then_inc(vn_ok, 1)
                        else:
                            dve.wait_ge(vp_ok, h * NS + i)
                            dve.tensor_tensor(vn[part, n, :, :], u[part, n, :, :],
                                              ps[part, 4, 0:2 * P].rearrange("p (a w) -> p a w", a=2),
                                              ALU.subtract).then_inc(vn_ok, 1)
                        if i == NCH - 1:
                            break
                        dve.wait_ge(ds_ok, h * NS + i + 1)
                        if i == 0:
                            dve.tensor_copy(flat(S[:, 1, :, :]), ps[:, 5, 0:2 * P]).then_inc(S_ok, 1)
                        else:
                            dve.wait_ge(S_ok, h * NS + i)
                            if i >= 3:
                                dve.wait_ge(o_ok, h * NT + (i - 1) // 2)
                            for a in range(2):
                                last = dve.scalar_tensor_tensor(S[:, (i + 1) % 4, a, :], S[:, i % 4, a, :],
                                                                sdec[:, a, i:i + 1], ps[:, 5, a * P:(a + 1) * P],
                                                                ALU.mult, ALU.add)
                            last.then_inc(S_ok, 1)
                    dve.wait_ge(osq_ok, h + 1)
                    dve.tensor_scalar(om[:], os_[:], 1.0 / P, EPS, ALU.mult, ALU.add).then_inc(om_ok, 1)
                    dve.wait_ge(oroot_ok, h + 1)
                    dve.reciprocal(ors[:], ort[:]).then_inc(ors_ok, 1)
                    dve.wait_ge(ors_ok, h + 1)
                    dve.tensor_tensor(og[:], og[:], per(ors[:]), ALU.mult).then_inc(tz, 1)
                    dve.wait_ge(tz, h + 2)
                    dve.wait_ge(zg_ok, h + 1)
                    dve.tensor_tensor(og[:], og[:], zg.rearrange("p n (a w) -> p n a w", a=2), ALU.mult).then_inc(normed, 1)
                    dve.wait_ge(hi_ok, h + 1)
                    dve.tensor_tensor(ot[1][:, bass.ds(2 * h, 2), :], ps[:, 6:8, :],
                                      ot[0][:, bass.ds(2 * h, 2), :].bitcast(F32), ALU.subtract).then_inc(lo_ok, 1)

                steps(dve, KH, step)

            @block.tensor
            def _(pe):
                pe.wait_ge(pre_lo, 2)
                for bank, w in ((6, wa), (7, wb)):
                    for k in range(KD):
                        last = mm3(pe, ps[:, bank, :], (w[0][:, k, 0:P], w[1][:, k, 0:P]), (hh[:, k, :], hl[:, k, :]),
                                   k == 0, k == KD - 1)
                    last.then_inc(pre_mm, 1)
                pe.wait_ge(row_a, 7)
                for i, row in enumerate((grow_, beta, egrow, ekrow)):
                    for n in range(NT):
                        last = pe.transpose(ps[:, 5, (i * NT + n) * VH:(i * NT + n + 1) * VH], row[:, n * P:(n + 1) * P],
                                            ident[0:VH, 0:VH])
                last.then_inc(row_t, 1)

                def project(h):
                    for bank, w, col, done in ((0, wa, 0, None), (1, wa, P, qk_ok), (2, wb, 0, None), (3, wb, P, v_ok)):
                        if bank == 0:
                            pe.wait_ge(a_hi, 2 * h + 1)
                            pe.wait_ge(a_lo, 2 * h + 1)
                        if bank == 2:
                            pe.wait_ge(b_hi, h + 1)
                            pe.wait_ge(b_lo, h + 1)
                        for k in range(KD):
                            last = mm3(pe, ps[:, bank, :], (w[0][:, k, col:col + P], w[1][:, k, col:col + P]),
                                       (hh[:, k, :], hl[:, k, :]), k == 0, k == KD - 1)
                            if k == KD - 1 and done is not None:
                                last.then_inc(done, 1)
                            yield

                def step(h):
                    pe.wait_ge(a_hi, 2 * h + 2)
                    pe.wait_ge(a_lo, 2 * h + 2)
                    if isinstance(h, int) and h == 0:
                        pe.wait_ge(cols_ok, 1)
                    for n in range(NT):
                        for k in range(KD):
                            rws = slice(n * P, (n + 1) * P)
                            last = mm3(pe, ps[:, 4 + n // 2, (n % 2) * 2 * P:(n % 2 + 1) * 2 * P],
                                       (hh[:, k, rws], hl[:, k, rws]), (wa[0][:, k, :], wa[1][:, k, :]), k == 0, k == KD - 1)
                    last.then_inc(z_ok, 1)
                    pe.wait_ge(silu_ok, h + 1)
                    for g in range(4):
                        for n in range(NT):
                            last = pe.transpose(ps[:, g, n * P:(n + 1) * P], cs[:, g, n * P:(n + 1) * P], ident[:])
                    last.then_inc(natural, 1)
                    after(pe, lo_ok, h)
                    for j, src in enumerate((kn, qn)):
                        pe.wait_ge(kq_ok, 2 * h + j + 1)
                        for n in range(NT):
                            last = pe.transpose(ps[:, 6 + j, n * P:(n + 1) * P], src[:, n, :], ident[:])
                        last.then_inc(kq_turned, 1)
                    pe.wait_ge(kqT_ok, 2 * h + 2)
                    for j, src in enumerate((knT, qnT)):
                        for n in range(NT):
                            last = pe.matmul(ps[:, 6 + j, n * P:(n + 1) * P], knT[:, n, :], src[:, n, :], start=True, stop=True)
                    last.then_inc(kk_ok, 1)
                    pe.wait_ge(prods, 4 * h + 2)
                    for n, a in problems:
                        last = pe.transpose(ps[:, a, n * P:(n + 1) * P], qd[:, n, a, :], ident[:])
                    last.then_inc(qd_turned, 1)
                    pe.wait_ge(t_ok, h + 1)
                    for n, a in problems:
                        last = pe.transpose(cell(2, n, a), Tm[:, n, a, :], ident[:])
                    last.then_inc(t_turned, 1)
                    pe.wait_ge(u_ok, 2 * h + 2)
                    pe.wait_ge(qdT_ok, h + 1)
                    for lv in range(1, NL):
                        base = h * (NL - 1) + lv
                        for half in range(2):
                            pe.wait_ge(as_ok[half], base)
                            if lv > 1:
                                pe.wait_ge(u_up[half], base - 1)
                            for n, a in some(half):
                                last = pe.matmul(cell(0, n, a), As[:, n, a, :], U[:, n, a, :], start=True, stop=True)
                            last.then_inc(y_mm[half], 1)
                        for half in range(2):
                            pe.wait_ge(y_ok[half], base)
                            if lv > 1:
                                pe.wait_ge(t_up[half], h * (NL - 2) + lv - 1)
                            for n, a in some(half):
                                last = pe.matmul(cell(2, n, a), Tm[:, n, a, :], Y[:, n, a, :], start=True, stop=True)
                            last.then_inc(u_mm_lv[half], 1)
                        if lv < NL - 1:
                            for half in range(2):
                                for n, a in some(half):
                                    last = pe.matmul(cell(6, n, a), Y[:, n, a, :], Tm[:, n, a, :], start=True, stop=True)
                                last.then_inc(t_mm_lv[half], 1)
                    for half in range(2):
                        pe.wait_ge(u_up[half], h * (NL - 1) + NL - 1)
                    pe.wait_ge(prods, 4 * h + 4)
                    for n, a in problems:
                        last = pe.matmul(cell(0, n, a), U[:, n, a, :], vb[:, n, a, :], start=True, stop=True)
                    last.then_inc(u_mm, 1)
                    for n, a in problems:
                        last = pe.matmul(cell(2, n, a), kbg[:, n, a, :], U[:, n, a, :], start=True, stop=True)
                    last.then_inc(u_mm, 1)
                    pe.wait_ge(z_sb, h + 1)
                    pe.wait_ge(w_sb, h + 1)
                    NS = NCH - 1
                    ahead = iter(()) if h is last_h else project(h + 1)

                    def fill(count):
                        for _ in zip(range(count), ahead):
                            pass

                    for i in range(NCH):
                        n, part = i // 2, slice((i % 2) * C, (i % 2 + 1) * C)
                        fill(2)
                        if i:
                            pe.wait_ge(S_ok, h * NS + i)
                            for a in range(2):
                                last = pe.matmul(ps[:, 4, a * P:(a + 1) * P], wT[:, n, a, :], S[:, i % 4, a, :],
                                                 start=True, stop=True)
                            last.then_inc(vp_ok, 1)
                        fill(2)
                        pe.wait_ge(vn_ok, h * NCH + i + 1)
                        if i < NS:
                            for a in range(2):
                                last = pe.matmul(ps[:, 5, a * P:(a + 1) * P], kdec[part, n, a, :], vn[part, n, a, :],
                                                 start=True, stop=True)
                            last.then_inc(ds_ok, 1)
                        if i % 2:
                            if n >= 2:
                                pe.wait_ge(og_ok, h * NT + n - 1)
                            for c in range(2):
                                for a in range(2):
                                    out = ps[:, 6 + n % 2, (c * 2 + a) * P:(c * 2 + a + 1) * P]
                                    inter = 2 * n + c > 0
                                    last = pe.matmul(out, qkt[:, n, a, :], vn[:, n, a, :], start=True, stop=not inter)
                                    if inter:
                                        last = pe.matmul(out, qdT[:, a, n, :], S[:, (2 * n + c) % 4, a, :], start=False, stop=True)
                            last.then_inc(o_ok, 1)
                    fill(4 * KD)
                    pe.wait_ge(normed, h + 1)
                    for n, a in problems:
                        last = pe.transpose(ps[:, 6 + a, n * P:(n + 1) * P], og[:, n, a, :], ident[:])
                    last.then_inc(o_turned, 1)

                for _ in project(0):
                    pass
                steps(pe, KH, step)


def short_conv(nc, hh, hl, ot, drams):
    w_dram, conv_dram = drams
    N = SC_TILES
    with Phase(nc, "sc") as ph:
        raw = [ph.sb(f"raw{i}", [P, KD, 2 * P]) for i in range(2)]
        wh = [ph.sb(f"wh{i}", [P, KD, 2 * P], F32R) for i in range(2)]
        wl = [ph.sb(f"wl{i}", [P, KD, 2 * P], F32R) for i in range(2)]
        conv = ph.sb("conv", [P, N, 3])
        cg = ph.sb("cg", [P, T])
        cu = ph.sb("cu", [P, T + 2])
        acc = [ph.sb(f"acc{i}", [P, T]) for i in range(3)]
        sz = ph.sb("sz", [P, T])
        y = ph.sb("y", [P, T])
        yz = ph.sb("yz", [P, T])
        ps = ph.psum()
        conv_in, zeroed, cg_ok, cu_ok, tap, sz_ok, y_ok, yz_ok, hi_ok, lo_ok = (
            ph.sem(n) for n in ("conv_in", "zeroed", "cg_ok", "cu_ok", "tap", "sz_ok", "y_ok", "yz_ok", "hi_ok", "lo_ok"))
        raw_in, w_hi, w_lo, gemm = ([ph.sem(f"{n}{i}") for i in range(2)] for n in ("raw_in", "w_hi", "w_lo", "gemm"))
        with nc.Block() as block:
            @block.sync
            def _(sp):
                sp.dma_start(conv[:], conv_dram).then_inc(conv_in, 16)

                def step(j):
                    for i in range(2):
                        after(sp, w_hi[i], j)
                        after(sp, w_lo[i], j)
                        sp.dma_start(raw[i][:], w_dram[j, i]).then_inc(raw_in[i], 16)
                steps(sp, N, step)

            @block.scalar
            def _(act):
                def split(j, i):
                    act.wait_ge(raw_in[i], 16 * (j + 1))
                    after(act, gemm[i], 2 * j)
                    act.activation(wh[i][:], raw[i][:], ACT.Copy).then_inc(w_hi[i], 1)

                def step(j):
                    act.wait_ge(gemm[0], 2 * j + 2)
                    after(act, cu_ok, j)
                    act.activation(cg[:], ps[:, 1, :], ACT.Copy).then_inc(cg_ok, 1)
                    if j is not N - 1:
                        split(j + 1, 0)
                    act.wait_ge(gemm[1], 2 * j + 2)
                    after(act, yz_ok, j)
                    act.activation(sz[:], ps[:, 3, :], ACT.Silu).then_inc(sz_ok, 1)
                    if j is not N - 1:
                        split(j + 1, 1)
                    act.wait_ge(yz_ok, j + 1)
                    act.activation(ot[0][:, j, :], yz[:], ACT.Copy).then_inc(hi_ok, 1)

                split(0, 0)
                split(0, 1)
                steps(act, N, step)

            @block.vector
            def _(dve):
                def split(j, i):
                    dve.wait_ge(w_hi[i], j + 1)
                    dve.tensor_tensor(wl[i][:], raw[i][:], wh[i][:].bitcast(F32), ALU.subtract).then_inc(w_lo[i], 1)

                def step(j):
                    dve.wait_ge(cg_ok, j + 1)
                    dve.tensor_tensor(cu[:, 2:T + 2], cg[:], ps[:, 0, :], ALU.mult).then_inc(cu_ok, 1)
                    if j is not N - 1:
                        split(j + 1, 0)
                    dve.wait_ge(cu_ok, j + 1)
                    dve.tensor_scalar(acc[0][:], cu[:, 0:T], conv[:, j, 0:1], None, ALU.mult).then_inc(tap, 1)
                    for i in range(1, 3):
                        dve.wait_ge(tap, 3 * j + i)
                        dve.scalar_tensor_tensor(acc[i][:], cu[:, i:T + i], conv[:, j, i:i + 1], acc[i - 1][:],
                                                 ALU.mult, ALU.add).then_inc(tap, 1)
                    dve.wait_ge(tap, 3 * j + 3)
                    dve.wait_ge(sz_ok, j + 1)
                    dve.tensor_tensor(y[:], acc[2][:], ps[:, 2, :], ALU.mult).then_inc(y_ok, 1)
                    dve.wait_ge(y_ok, j + 1)
                    dve.tensor_tensor(yz[:], y[:], sz[:], ALU.mult).then_inc(yz_ok, 1)
                    if j is not N - 1:
                        split(j + 1, 1)
                    dve.wait_ge(hi_ok, j + 1)
                    dve.tensor_tensor(ot[1][:, j, :], yz[:], ot[0][:, j, :].bitcast(F32), ALU.subtract).then_inc(lo_ok, 1)

                dve.memset(cu[:, 0:2], 0.0).then_inc(zeroed, 1)
                dve.wait_ge(zeroed, 1)
                dve.wait_ge(conv_in, 16)
                split(0, 0)
                split(0, 1)
                steps(dve, N, step)

            @block.tensor
            def _(pe):
                def step(j):
                    for i in range(2):
                        pe.wait_ge(w_hi[i], j + 1)
                        pe.wait_ge(w_lo[i], j + 1)
                        after(pe, (cu_ok, y_ok)[i], j)
                        for half in range(2):
                            for k in range(KD):
                                cols = slice(half * P, (half + 1) * P)
                                last = mm3(pe, ps[:, 2 * i + half, :], (wh[i][:, k, cols], wl[i][:, k, cols]),
                                           (hh[:, k, :], hl[:, k, :]), k == 0, k == KD - 1)
                            last.then_inc(gemm[i], 1)
                steps(pe, N, step)


def second_block(nc, sb, ident, hh, hl, a, x2_dram, grow_dram, sd_dram, x3_dram, out):
    with ExitStack() as o:
        ot = (sb("oth", [P, 2 * KD, T], F32R, o), sb("otl", [P, 2 * KD, T], F32R, o))
        gdn(nc, hh, hl, ot, ident, grow_dram, sd_dram,
            [a[n] for n in ("gdn_w", "gdn_b", "gdn_a", "gdn_conv", "a_log", "dt_bias", "gdn_gain", "reset", "gdn_masks")])
        xo = sb("x3", [P, NT, D], F32, o)
        out_projection(nc, "go", ot, 2 * KD, a["gdn_wo"], x2_dram, xo, x3_dram, a["post_gain0"])
        norm_transposed(nc, "n4", xo, a["pre_gain1"], ident, hh, hl)
        short_conv(nc, hh, hl, ot, (a["sc_w"], a["sc_conv"]))
        out_projection(nc, "so", ot, 2 * KD, a["sc_wo"], x3_dram, xo, out, a["post_gain1"])


def program(nc, a, out):
    x1_dram = nc.dram_tensor("x1_scratch", (T, D), F32, kind="Internal").ap()
    x2_dram = nc.dram_tensor("x2_scratch", (T, D), F32, kind="Internal").ap()
    x3_dram = nc.dram_tensor("x3_scratch", (T, D), F32, kind="Internal").ap()
    grow_dram = nc.dram_tensor("g_scratch", (GDN_VH, T), F32, kind="Internal").ap()
    sd_dram = nc.dram_tensor("sd_scratch", (GDN_VH, NCH), F32, kind="Internal").ap()
    g_dram = nc.dram_tensor("gate_scratch", (T // P, NKEYS, NKEYS, P), F32, kind="Internal").ap()
    with ExitStack() as top:
        def sb(name, shape, dt=F32, ctx=top):
            return ctx.enter_context(nc.sbuf_tensor(name, shape, dt))
        ident = sb("ident", [P, P])
        hh = sb("hh", [P, KD, T], F32R)
        hl = sb("hl", [P, KD, T], F32R)
        ident_in = nc.alloc_semaphore("ident_in")
        with nc.Block() as block:
            @block.sync
            def _(sp):
                sp.dma_start(ident[:], a["ident"]).then_inc(ident_in, 16)
                sp.wait_ge(ident_in, 16)
        with nc.sbuf_tensor("x_in", [P, NT, D], F32) as x:
            norm_transposed(nc, "n1", x, a["mix_gain"], ident, hh, hl, load_from=a["x"])
        with ExitStack() as mix:
            oa = (sb("oah", [P, KD, T], F32R, mix), sb("oal", [P, KD, T], F32R, mix))
            gla(nc, hh, hl, oa, ident, [a[n] for n in ("gla_w", "glr_w", "gk2", "bgk", "gla_gain", "tri", "reset")])
            ob = (sb("obh", [P, KD, T], F32R, mix), sb("obl", [P, KD, T], F32R, mix))
            swa(nc, hh, hl, ob, ident, [a[n] for n in ("swa_w", "qg", "kg", "cos", "sin", "mask", "sinks")])
            mt = (sb("mth", [P, KD, T], F32R, mix), sb("mtl", [P, KD, T], F32R, mix))
            merge(nc, hh, hl, oa, ob, mt, a["mrg_w"])
            with ExitStack() as o:
                xo = sb("xo", [P, NT, D], F32, o)
                out_projection(nc, "wo", mt, KD, a["wo_w"], a["x"], xo, x1_dram)
        with ExitStack() as peer:
            x = sb("x_peer", [P, NT, D], F32, peer)
            norm_transposed(nc, "n2", x, a["ffn_gain"], ident, hh, hl, load_from=x1_dram)
            with ExitStack() as rt:
                iT, jT, gT = (sb(n, [P, T], F32, rt) for n in ("iT", "jT", "gT"))
                route(nc, hh, hl, iT, jT, gT, ident, (a["pq_w"], a["keys"], a["iota"]))
                gate_matrix(nc, iT, jT, gT, a["iota"], g_dram)
            experts(nc, hh, hl, x, a["u_w"], a["v_w"], g_dram, x2_dram)
            norm_transposed(nc, "n3", x, a["pre_gain0"], ident, hh, hl)
        second_block(nc, sb, ident, hh, hl, a, x2_dram, grow_dram, sd_dram, x3_dram, out)


OUT = ("out", (T, D))


def finish(r):
    return r.reshape(1, T, D)


def columns(v):
    return v.reshape(-1, P).T


def k_major(w, cols):
    return w[:, cols].reshape(-1, P, len(cols)).transpose(1, 0, 2)


def laid_out(i):
    ar = np.arange
    splits = np.cumsum([0, 512, 512, 1024, 1024, 16, 1024, 256, 256, 1024, 1024])
    gq, gk, gv, gr, glr, sq, sk, sv, ga, gb = splits[:10]
    w = i["w_in"][0]
    a = {"x": i["x"][0], "ident": np.eye(P, dtype=np.float32), "mix_gain": columns(i["norm_mix_g"][0])}
    a["gla_w"] = np.stack([k_major(w, np.concatenate([gq + h * 128 + ar(128), gk + h * 128 + ar(128),
                                                      gv + h * 256 + ar(256), gr + h * 256 + ar(256)]))
                           for h in range(GLA_H)])
    a["glr_w"] = k_major(w, glr + ar(GLA_R))
    a["gk2"] = i["w_gk2"][0]
    a["bgk"] = columns(i["b_gk"][0])
    a["gla_gain"] = i["gla_norm_g"][0]
    a["tri"] = np.tile(np.triu(np.ones((C, C), np.uint32)), (2, 1))
    a["reset"] = np.tile((ar(T) % C != 0).astype(np.float32), (P, 1))
    a["swa_w"] = np.stack([k_major(w, np.concatenate([sq + h * 256 + ar(256), sk + h * 64 + ar(64), sv + h * 64 + ar(64)]))
                           for h in range(SWA_KV)])
    a["qg"], a["kg"] = i["q_norm_g"][0], i["k_norm_g"][0]
    pos = ar(T, dtype=np.float32)
    inv_freq = np.float32(500000.0) ** (-ar(0, 16, 2, dtype=np.float32) / np.float32(16))
    ang = pos[:, None] * inv_freq[None, :]
    for n, f in (("cos", np.cos), ("sin", np.sin)):
        a[n] = f(ang).astype(np.float32).reshape(NT, P, ROPE_HALF).transpose(1, 0, 2)
    q, k = ar(P)[:, None] + P, ar(2 * P)[None, :]
    a["mask"] = np.where((q - k >= 0) & (q - k < P), 0.0, NEG).astype(np.float32)
    a["sinks"] = i["attn_sinks"][0].reshape(SWA_KV, GRP)[:, [0, 2, 1, 3]]
    wa, wb = i["w_branch_a"][0], i["w_branch_b"][0]
    a["mrg_w"] = np.stack([np.stack([np.stack([k_major(w, g + j * P + ar(P)), k_major(br, j * P + ar(P))], axis=1)
                                     for g, br in ((ga, wa), (gb, wb))]) for j in range(KD)])
    a["wo_w"] = np.stack([k_major(i["w_out"][0], j * 256 + ar(256)) for j in range(4)])
    a["ffn_gain"] = columns(i["norm_ffn_g"][0])
    a["pq_w"] = np.stack([k_major(i["w_peer_q"][0], h * 256 + ar(256)) for h in range(PEER_H)])
    a["keys"] = i["peer_sub_keys"][0].transpose(0, 3, 1, 2)
    a["iota"] = np.tile(ar(NKEYS, dtype=np.float32), (P, 1))
    a["u_w"] = i["peer_u"][0].reshape(NEB, EB * P, KD, P).transpose(0, 3, 2, 1)
    a["v_w"] = i["peer_v"][0].reshape(NEB, EB, P, D).transpose(0, 2, 1, 3)
    a["pre_gain0"], a["pre_gain1"] = (columns(i["pre_norm_w_2"][l]) for l in range(2))
    a["post_gain0"], a["post_gain1"] = (i["post_norm_w_2"][l] for l in range(2))
    w, c = i["gdn_w_in_2"][0], i["gdn_conv_w_2"][0]
    kw, vw = GDN_KH * P, GDN_VH * P
    a["gdn_w"] = np.stack([np.stack([
        k_major(w, np.concatenate([h * P + ar(P), kw + h * P + ar(P)])),
        k_major(w, 2 * kw + 2 * h * P + ar(2 * P)),
        k_major(w, 2 * kw + vw + 2 * h * P + ar(2 * P))]) for h in range(GDN_KH)])
    a["gdn_b"] = k_major(w, 2 * kw + 2 * vw + ar(GDN_VH))
    a["gdn_a"] = k_major(w, 2 * kw + 2 * vw + GDN_VH + ar(GDN_VH))
    ch = np.stack([np.stack([h * P + ar(P), kw + h * P + ar(P), 2 * kw + 2 * h * P + ar(P),
                             2 * kw + (2 * h + 1) * P + ar(P)]) for h in range(GDN_KH)])
    a["gdn_conv"] = c[:, ch].transpose(3, 1, 2, 0)
    a["a_log"], a["dt_bias"] = i["gdn_A_log_2"][0][:, None], i["gdn_dt_bias_2"][0][:, None]
    a["gdn_gain"] = i["gdn_norm_w_2"][0]
    r, q = ar(P)[:, None], ar(P)[None, :]
    same = r // C == q // C
    lv = [(r // (2 * s) == q // (2 * s)) & (r // s % 2 == 1) & (q // s % 2 == 0) for s in (1, 2, 4, 8, 16, 32)]
    a["gdn_masks"] = np.stack([same & (q < r), same & (r <= q)] + lv, axis=1).astype(np.float32)
    a["gdn_wo"] = np.stack([k_major(i["gdn_w_out_2"][0], j * 256 + ar(256)) for j in range(4)])
    w, sw = i["sc_w_in_2"][0], SC_TILES * P
    a["sc_w"] = np.stack([np.stack([k_major(w, np.concatenate([g * sw + j * P + ar(P) for g in pair]))
                                    for pair in ((0, 2), (1, 3))]) for j in range(SC_TILES)])
    a["sc_conv"] = i["sc_conv_w_2"][0].reshape(3, SC_TILES, P).transpose(2, 1, 0)
    a["sc_wo"] = np.stack([k_major(i["sc_w_out_2"][0], j * 256 + ar(256)) for j in range(4)])
    return {n: np.ascontiguousarray(v) for n, v in a.items()}


def kernel(**inputs):
    import concourse.bacc as bacc
    from concourse.bass_utils import run_bass_kernel_spmd

    nc = bacc.Bacc("TRN2", target_bir_lowering=False, num_devices=1)
    arrays = laid_out({n: np.asarray(v) for n, v in inputs.items()})
    aps = {n: nc.dram_tensor(f"in_{n}", v.shape, mybir.dt.from_np(v.dtype), kind="ExternalInput").ap()
           for n, v in arrays.items()}
    name, shape = OUT
    out = nc.dram_tensor(name, shape, F32, kind="ExternalOutput").ap()
    program(nc, aps, out)
    r = run_bass_kernel_spmd(nc, [{f"in_{n}": v for n, v in arrays.items()}], core_ids=[0])
    return finish(r.results[0][name])
```

```python
from contextlib import ExitStack

import numpy as np
import concourse.bass as bass
from concourse import mybir

F32 = mybir.dt.float32
F32R = mybir.dt.float32r
U32 = mybir.dt.uint32
ALU = mybir.AluOpType
ACT = mybir.ActivationFunctionType
AX_X = mybir.AxisListType.X

P = 128
T = 512
NT = T // P
D = 1024
KD = D // P
EPS = 1e-6
C = 64
NCH = T // C

GLA_H, GLA_DK, GLA_DV, GLA_R = 4, 128, 256, 16
GLA_COLS = 2 * GLA_DK + 2 * GLA_DV
SWA_H, SWA_KV, HD = 16, 4, 64
GRP = SWA_H // SWA_KV
SWA_COLS = (GRP + 2) * HD
ROPE_HALF = 8
PEER_H, PEER_K, NKEYS = 8, 16, 128
EB = 4
NEB = NKEYS // EB
GDN_KH, GDN_VH = 8, 16
GDN_COLS = 6 * P
SC_TILES = 16
NEG = -1e30


def mm3(pe, out, lhs, rhs, start, stop):
    (lh, ll), (rh, rl) = lhs, rhs
    pe.matmul(out, lh, rh, start=start, stop=False)
    pe.matmul(out, lh, rl, start=False, stop=False)
    return pe.matmul(out, ll, rh, start=False, stop=stop)


def after(eng, sem, count):
    if not (isinstance(count, int) and count == 0):
        eng.wait_ge(sem, count)


def steps(eng, n, body):
    body(0)
    with eng.Fori(1, n - 1) as i:
        body(i)
    body(n - 1)


def flat(ap):
    return ap.rearrange("p a b -> p (a b)")


class Phase:

    def __init__(self, nc, tag):
        self.nc, self.tag, self.ctx, self.sems = nc, tag, ExitStack(), []

    def __enter__(self):
        return self

    def __exit__(self, *a):
        if a[0] is None:
            self.nc.clear_and_free_semaphores(self.sems)
            self.nc.all_engine_barrier()
        return self.ctx.__exit__(*a)

    def sb(self, name, shape, dt=F32):
        return self.ctx.enter_context(self.nc.sbuf_tensor(f"{self.tag}_{name}", shape, dt))

    def psum(self, name="ps"):
        return self.ctx.enter_context(self.nc.psum_tensor(f"{self.tag}_{name}", [P, 8, 512], F32))

    def sem(self, name):
        self.sems.append(self.nc.alloc_semaphore(f"{self.tag}_{name}"))
        return self.sems[-1]


def norm_transposed(nc, tag, x, gain_dram, ident, hh, hl, load_from=None):
    with Phase(nc, tag) as ph:
        xn = ph.sb("xn", [P, NT, D])
        gain = ph.sb("gain", [P, KD])
        ss = ph.sb("ss", [P, NT])
        ms = ph.sb("ms", [P, NT])
        rt = ph.sb("rt", [P, NT])
        rs = ph.sb("rs", [P, NT])
        ps = ph.psum()
        gain_in, x_in, squared, mean_ok, root_ok, rstd_ok, scaled, turned, hi_ok, lo_ok = (
            ph.sem(n) for n in ("gain_in", "x_in", "squared", "mean_ok", "root_ok", "rstd_ok", "scaled",
                                "turned", "hi_ok", "lo_ok"))
        with nc.Block() as block:
            @block.sync
            def _(sp):
                if load_from is not None:
                    for n in range(NT):
                        sp.dma_start(x[:, n, :], load_from[n * P:(n + 1) * P, :]).then_inc(x_in, 16)
                sp.dma_start(gain[:], gain_dram).then_inc(gain_in, 16)

            @block.scalar
            def _(act):
                for n in range(NT):
                    if load_from is not None and n == 0:
                        act.wait_ge(x_in, 16 * NT)
                    act.activation(xn[:, n, :], x[:, n, :], ACT.Square, accum_out=ss[:, n:n + 1]).then_inc(squared, 1)
                act.wait_ge(mean_ok, 1)
                act.activation(rt[:], ms[:], ACT.Sqrt).then_inc(root_ok, 1)
                act.wait_ge(gain_in, 16)
                for k in range(KD):
                    act.wait_ge(turned, k + 1)
                    act.activation(hh[:, k, :], ps[:, k, :], ACT.Copy, scale=gain[:, k:k + 1]).then_inc(hi_ok, 1)

            @block.vector
            def _(dve):
                dve.wait_ge(squared, NT)
                dve.tensor_scalar(ms[:], ss[:], 1.0 / D, EPS, ALU.mult, ALU.add).then_inc(mean_ok, 1)
                dve.wait_ge(root_ok, 1)
                dve.reciprocal(rs[:], rt[:]).then_inc(rstd_ok, 1)
                dve.wait_ge(rstd_ok, 1)
                for n in range(NT):
                    dve.tensor_scalar(xn[:, n, :], x[:, n, :], rs[:, n:n + 1], None, ALU.mult).then_inc(scaled, 1)
                for k in range(KD):
                    dve.wait_ge(hi_ok, k + 1)
                    dve.scalar_tensor_tensor(hl[:, k, :], ps[:, k, :], gain[:, k:k + 1], hh[:, k, :].bitcast(F32),
                                             ALU.mult, ALU.subtract).then_inc(lo_ok, 1)

            @block.tensor
            def _(pe):
                pe.wait_ge(scaled, NT)
                for k in range(KD):
                    for n in range(NT):
                        last = pe.transpose(ps[:, k, n * P:(n + 1) * P], xn[:, n, k * P:(k + 1) * P], ident[:])
                    last.then_inc(turned, 1)


def gla(nc, hh, hl, oa, ident, drams):
    w_dram, glr_dram, gk2_dram, bgk_dram, gain_dram, tri_dram, reset_dram = drams
    with Phase(nc, "gla") as ph:
        raw = ph.sb("raw", [P, KD, GLA_COLS])
        wh = ph.sb("wh", [P, KD, GLA_COLS], F32R)
        wl = ph.sb("wl", [P, KD, GLA_COLS], F32R)
        glr = ph.sb("glr", [P, KD, GLA_R])
        gh = wh[:, :, 0:P]
        gl = wl[:, :, 0:P]
        glrT = ph.sb("glrT", [GLA_R, T])
        gk2 = ph.sb("gk2", [GLA_R, GLA_H * GLA_DK])
        bgk = ph.sb("bgk", [P, GLA_H])
        gain = ph.sb("gain", [P, GLA_DV])
        tri = ph.sb("tri", [P, C], U32)
        b = ph.sb("b", [P, GLA_H, NCH, C])
        reset = ph.sb("reset", [P, T])
        z = ph.sb("z", [P, 4, T])
        dref, dend = (z[:, i, :].rearrange("p (a b) -> p a b", a=NCH) for i in range(2))
        e1, e2 = z[:, 2, :], z[:, 3, :]
        e3 = ph.sb("e3", [P, T])
        e4 = ph.sb("e4", [P, T])
        dec = ph.sb("dec", [P, NCH])
        qa = ph.sb("qa", [P, T])
        ka = ph.sb("ka", [P, T])
        ke = ph.sb("ke", [P, T])
        qi = ph.sb("qi", [P, 2, NT, P])
        kend = ph.sb("kend", [P, NT, GLA_DK])
        attm = ph.sb("attm", [P, NT, P])
        v = ph.sb("v", [P, NT, GLA_DV])
        rg = ph.sb("rg", [P, NT, GLA_DV])
        S = ph.sb("S", [P, NCH, GLA_DV])
        za = flat(S[:]).rearrange("p (a b) -> p a b", a=4)
        og = ph.sb("og", [P, NT, GLA_DV])
        ss = ph.sb("ss", [P, NT])
        ms = ph.sb("ms", [P, NT])
        rt = ph.sb("rt", [P, NT])
        rs = ph.sb("rs", [P, NT])
        rt_seen = ph.sb("rt_seen", [P, 1])
        ps = ph.psum()

        small_in, glr_in = ph.sem("small_in"), ph.sem("glr_in")
        zeroed = ph.sem("zeroed")
        pre = ph.sem("pre")
        glr_hi, glr_lo, glr_ok, glr_sb, gk_ok = (ph.sem(n) for n in ("glr_hi", "glr_lo", "glr_ok", "glr_sb", "gk_ok"))
        gate_v, gate_a, b_ok = ph.sem("gate_v"), ph.sem("gate_a"), ph.sem("b_ok")
        raw_in, w_hi, w_lo = ph.sem("raw_in"), ph.sem("w_hi"), ph.sem("w_lo")
        q_ok, k_ok, v_ok, r_ok = (ph.sem(n) for n in ("q_ok", "k_ok", "v_ok", "r_ok"))
        diff_ok, exp_ok, qk_scaled = ph.sem("diff_ok"), ph.sem("exp_ok"), ph.sem("qk_scaled")
        ke_turned, kend_ok, att_ok, attm_ok = (ph.sem(n) for n in ("ke_turned", "kend_ok", "att_ok", "attm_ok"))
        v_sb, r_sb, rg_ok = ph.sem("v_sb"), ph.sem("r_sb"), ph.sem("rg_ok")
        ds_ok, S_ok, o_ok, sq_ok, ms_ok, root_ok, rs_ok, og_ok = (
            ph.sem(n) for n in ("ds_ok", "S_ok", "o_ok", "sq_ok", "ms_ok", "root_ok", "rs_ok", "og_ok"))
        o_turned, oa_ok, oal_ok = ph.sem("o_turned"), ph.sem("oa_ok"), ph.sem("oal_ok")
        NS = NCH - 1

        def psv(bank, n):
            return ps[:, bank + n // 2, (n % 2) * GLA_DV:(n % 2 + 1) * GLA_DV]

        def psd(c):
            return psv(2 * (c % 2), c // 2)

        with nc.Block() as block:
            @block.sync
            def _(sp):
                sp.dma_start(glr[:], glr_dram).then_inc(glr_in, 16)
                sp.dma_start(raw[:], w_dram[0]).then_inc(raw_in, 16)
                for dst, src in ( (gk2, gk2_dram), (bgk, bgk_dram), (tri, tri_dram), (reset, reset_dram)):
                    sp.dma_start(dst[:], src).then_inc(small_in, 16)
                sp.dma_start(gain[:], gain_dram.partition_broadcast(P)).then_inc(small_in, 16)

                def step(h):
                    sp.wait_ge(w_hi, h + 1)
                    sp.wait_ge(w_lo, h + 1)
                    sp.dma_start(raw[:], w_dram[h + 1]).then_inc(raw_in, 16)
                with sp.Fori(0, GLA_H - 1) as h:
                    step(h)

            @block.gpsimd
            def _(pool):
                pool.memset(wh[:].bitcast(F32)[:, :, 0:P], 0.0).then_inc(zeroed, 1)
                pool.memset(wl[:].bitcast(F32)[:, :, 0:P], 0.0).then_inc(zeroed, 1)
                pool.memset(qi[:], 0.0).then_inc(zeroed, 1)
                pool.memset(attm[:], 0.0).then_inc(zeroed, 1)

                pool.wait_ge(small_in, 16 * 5)
                with pool.Fori(0, GLA_H) as h:
                    pool.wait_ge(r_sb, h + 1)
                    pool.tensor_tensor(rg[:], rg[:], gain[:].unsqueeze(1).broadcast_to([P, NT, GLA_DV]),
                                       ALU.mult).then_inc(rg_ok, 1)

            @block.scalar
            def _(act):
                act.wait_ge(glr_in, 16)
                act.wait_ge(zeroed, 2)
                act.activation(gh[:, :, 0:GLA_R], glr[:], ACT.Copy).then_inc(glr_hi, 1)
                def split(h):
                    act.wait_ge(raw_in, 16 * (h + 1))
                    act.activation(wh[:], raw[:], ACT.Copy).then_inc(w_hi, 1)

                act.wait_ge(glr_ok, 1)
                act.activation(glrT[:], ps[0:GLA_R, 6, :], ACT.Copy).then_inc(glr_sb, 1)
                split(0)
                act.wait_ge(gate_v, 2)
                act.activation(za, za, ACT.Exp).then_inc(gate_a, 1)
                act.wait_ge(gate_v, 3)
                act.activation(za, za, ACT.Ln).then_inc(gate_a, 1)

                act.wait_ge(b_ok, 1)

                def step(h):
                    act.wait_ge(diff_ok, 2 * h + 2)
                    after(act, qk_scaled, 5 * h)
                    act.activation(e1, dref.rearrange("p a b -> p (a b)"), ACT.Exp).then_inc(exp_ok, 1)
                    act.activation(e2, dref.rearrange("p a b -> p (a b)"), ACT.Exp, scale=-1.0).then_inc(exp_ok, 1)
                    act.activation(e3[:], b[:, h, :, :].rearrange("p a b -> p (a b)"), ACT.Exp).then_inc(exp_ok, 1)
                    act.activation(e4[:], dend.rearrange("p a b -> p (a b)"), ACT.Exp).then_inc(exp_ok, 1)
                    after(act, S_ok, h * NS)
                    act.activation(dec[:], b[:, h, :, C - 1], ACT.Exp).then_inc(exp_ok, 1)
                    act.wait_ge(v_ok, h + 1)
                    for n in range(2):
                        act.activation(v[:, 2 * n:2 * n + 2, :].rearrange("p a b -> p (a b)"), ps[:, 2 + n, :],
                                       ACT.Copy).then_inc(v_sb, 1)
                    act.wait_ge(ke_turned, h + 1)
                    act.activation(kend[:].rearrange("p a b -> p (a b)"), ps[:, 6, :], ACT.Copy).then_inc(kend_ok, 1)
                    act.wait_ge(r_ok, h + 1)
                    after(act, og_ok, h * NT)
                    for n in range(2):
                        last_r = act.activation(rg[:, 2 * n:2 * n + 2, :].rearrange("p a b -> p (a b)"),
                                                ps[:, 4 + n, :], ACT.Silu)
                    last_r.then_inc(r_sb, 1)
                    if h is not GLA_H - 1:
                        split(h + 1)
                    for n in range(NT):
                        act.wait_ge(o_ok, h * NT + n // 2 * 2 + 2)
                        act.activation(og[:, n, :], psv(4, n), ACT.Square, accum_out=ss[:, n:n + 1]).then_inc(sq_ok, 1)
                    act.wait_ge(ms_ok, h + 1)
                    act.activation(rt[:], ms[:], ACT.Sqrt).then_inc(root_ok, 1)
                    for e in range(2):
                        act.wait_ge(o_turned, 2 * h + e + 1)
                        act.activation(oa[0][:, h * 2 + e, :], ps[:, 6 + e, :], ACT.Copy).then_inc(oa_ok, 1)

                steps(act, GLA_H, step)

            @block.vector
            def _(dve):
                def split(h):
                    dve.wait_ge(w_hi, h + 1)
                    dve.tensor_tensor(wl[:], raw[:], wh[:].bitcast(F32), ALU.subtract).then_inc(w_lo, 1)

                dve.wait_ge(glr_hi, 1)
                dve.tensor_tensor(gl[:, :, 0:GLA_R], glr[:], gh[:, :, 0:GLA_R].bitcast(F32), ALU.subtract).then_inc(glr_lo, 1)
                dve.wait_ge(gk_ok, 1)
                dve.wait_ge(small_in, 16 * 5)
                dve.tensor_tensor(z[:], ps[:, 0:GLA_H, :], bgk[:].unsqueeze(2).broadcast_to([P, GLA_H, T]),
                                  ALU.add).then_inc(gate_v, 1)
                split(0)
                dve.wait_ge(gate_v, 1)
                dve.tensor_scalar(za, z[:], 0.0, 2.0, ALU.min, ALU.mult).then_inc(pre, 1)
                dve.wait_ge(pre, 1)
                dve.tensor_tensor(za, za, z[:], ALU.subtract).then_inc(gate_v, 1)
                dve.wait_ge(gate_a, 1)
                dve.tensor_scalar(za, za, 1.0, None, ALU.add).then_inc(gate_v, 1)
                dve.wait_ge(gate_a, 2)
                dve.scalar_tensor_tensor(z[:], z[:], 0.0, za, ALU.min, ALU.subtract).then_inc(pre, 1)
                dve.wait_ge(pre, 2)
                dve.tensor_scalar(z[:], z[:], 1.0 / 16.0, None, ALU.mult).then_inc(pre, 1)
                dve.wait_ge(pre, 3)
                for h in range(GLA_H):
                    scan = dve.tensor_tensor_scan(b[:, h, :, :].rearrange("p a b -> p (a b)"), reset[:], z[:, h, :],
                                                  0.0, ALU.mult, ALU.add)
                scan.then_inc(b_ok, 1)
                dve.wait_ge(b_ok, 1)
                dve.wait_ge(zeroed, 4)
                q4 = ps[:, 0, :].rearrange("p (n c w) -> p n c w", n=NT, c=2)
                e34 = e3[:].rearrange("p (n c w) -> p n c w", n=NT, c=2)
                s = GLA_DK ** -0.5

                def step(h):
                    after(dve, exp_ok, 5 * h)
                    dve.tensor_tensor(dref, b[:, h, :, :], b[:, h, :, C // 2:C // 2 + 1].broadcast_to([P, NCH, C]),
                                      ALU.subtract).then_inc(diff_ok, 1)
                    dve.tensor_tensor(dend, b[:, h, :, C - 1:C].broadcast_to([P, NCH, C]), b[:, h, :, :],
                                      ALU.subtract).then_inc(diff_ok, 1)
                    dve.wait_ge(exp_ok, 5 * h + 5)
                    dve.wait_ge(k_ok, h + 1)
                    dve.tensor_tensor(ke[:], ps[:, 1, :], e4[:], ALU.mult).then_inc(qk_scaled, 1)
                    dve.tensor_tensor(ka[:], ps[:, 1, :], e2, ALU.mult).then_inc(qk_scaled, 1)
                    dve.scalar_tensor_tensor(qa[:], ps[:, 0, :], s, e1, ALU.mult, ALU.mult).then_inc(qk_scaled, 1)
                    for c in range(2):
                        dve.scalar_tensor_tensor(qi[:, c, :, c * C:(c + 1) * C], q4[:, :, c, :], s, e34[:, :, c, :],
                                                 ALU.mult, ALU.mult).then_inc(qk_scaled, 1)
                    dve.wait_ge(att_ok, h + 1)
                    dve.tensor_copy(rt_seen[:], ident[:, 0:1])
                    for c in range(2):
                        rows = slice(c * C, (c + 1) * C)
                        dve.copy_predicated(attm[rows, :, rows], tri[rows, :].unsqueeze(1).broadcast_to([C, NT, C]),
                                            ps[rows, 7, :].rearrange("p (n w) -> p n w", n=NT)[:, :, rows]
                                            ).then_inc(attm_ok, 1)
                    dve.wait_ge(ds_ok, h * NS + NS)
                    for c in range(NS):
                        if c == 0:
                            up = dve.tensor_copy(S[:, 1, :], ps[:, 0, 0:GLA_DV])
                        else:
                            dve.wait_ge(S_ok, h * NS + c)
                            up = dve.scalar_tensor_tensor(S[:, c + 1, :], S[:, c, :], dec[:, c:c + 1], psd(c),
                                                          ALU.mult, ALU.add)
                        up.then_inc(S_ok, 1)
                    if h is not GLA_H - 1:
                        dve.wait_ge(r_ok, h + 1)
                        split(h + 1)
                    dve.wait_ge(sq_ok, h * NT + NT)
                    dve.tensor_scalar(ms[:], ss[:], 1.0 / GLA_DV, EPS, ALU.mult, ALU.add).then_inc(ms_ok, 1)
                    dve.wait_ge(root_ok, h + 1)
                    dve.reciprocal(rs[:], rt[:]).then_inc(rs_ok, 1)
                    dve.wait_ge(rs_ok, h + 1)
                    dve.wait_ge(rg_ok, h + 1)
                    for n in range(NT):
                        dve.scalar_tensor_tensor(og[:, n, :], psv(4, n), rs[:, n:n + 1], rg[:, n, :],
                                                 ALU.mult, ALU.mult).then_inc(og_ok, 1)
                    for e in range(2):
                        dve.wait_ge(oa_ok, 2 * h + e + 1)
                        dve.tensor_tensor(oa[1][:, h * 2 + e, :], ps[:, 6 + e, :], oa[0][:, h * 2 + e, :].bitcast(F32),
                                          ALU.subtract).then_inc(oal_ok, 1)

                steps(dve, GLA_H, step)

            @block.tensor
            def _(pe):
                pe.wait_ge(glr_lo, 1)
                for k in range(KD):
                    last = mm3(pe, ps[:, 6, :], (gh[:, k, :], gl[:, k, :]), (hh[:, k, :], hl[:, k, :]), k == 0, k == KD - 1)
                last.then_inc(glr_ok, 1)
                pe.wait_ge(glr_sb, 1)
                pe.wait_ge(small_in, 16 * 5)
                for h in range(GLA_H):
                    last = pe.matmul(ps[:, h, :], gk2[:, h * P:(h + 1) * P], glrT[:], start=True, stop=True)
                last.then_inc(gk_ok, 1)
                pe.wait_ge(gate_v, 1)

                def step(h):
                    pe.wait_ge(w_hi, h + 1)
                    pe.wait_ge(w_lo, h + 1)
                    after(pe, S_ok, h * NS)
                    for bank, col, sem in ((0, 0, q_ok), (1, P, k_ok)):
                        for k in range(KD):
                            last = mm3(pe, ps[:, bank, :], (wh[:, k, col:col + P], wl[:, k, col:col + P]),
                                       (hh[:, k, :], hl[:, k, :]), k == 0, k == KD - 1)
                        last.then_inc(sem, 1)
                    for bank, col, sem in ((2, 2 * P, v_ok), (4, 2 * P + GLA_DV, r_ok)):
                        if bank == 4:
                            after(pe, og_ok, h * NT)
                        for n in range(NT):
                            for k in range(KD):
                                rows = slice(n * P, (n + 1) * P)
                                cols = slice(col, col + GLA_DV)
                                last = mm3(pe, psv(bank, n), (hh[:, k, rows], hl[:, k, rows]),
                                           (wh[:, k, cols], wl[:, k, cols]), k == 0, k == KD - 1)
                        last.then_inc(sem, 1)
                    pe.wait_ge(qk_scaled, 5 * h + 1)
                    after(pe, oal_ok, 2 * h)
                    for n in range(NT):
                        last = pe.transpose(ps[:, 6, n * P:(n + 1) * P], ke[:, n * P:(n + 1) * P], ident[:])
                    last.then_inc(ke_turned, 1)
                    pe.wait_ge(qk_scaled, 5 * h + 5)
                    for n in range(NT):
                        rows = slice(n * P, (n + 1) * P)
                        last = pe.matmul(ps[:, 7, rows], ka[:, rows], qa[:, rows], start=True, stop=True)
                    last.then_inc(att_ok, 1)
                    pe.wait_ge(kend_ok, h + 1)
                    pe.wait_ge(v_sb, 2 * h + 2)
                    for c in range(NS):
                        rows = slice((c % 2) * C, (c % 2 + 1) * C)
                        last = pe.matmul(psd(c), kend[rows, c // 2, :], v[rows, c // 2, :], start=True, stop=True)
                        last.then_inc(ds_ok, 1)
                    pe.wait_ge(attm_ok, 2 * h + 2)
                    pe.wait_ge(r_sb, h + 1)
                    for n in range(NT):
                        pe.matmul(psv(4, n), attm[:, n, :], v[:, n, :], start=True, stop=False)
                        pe.wait_ge(S_ok, h * NS + min(2 * n + 1, NS))
                        if n:
                            pe.matmul(psv(4, n), qi[:, 0, n, :], S[:, 2 * n, :], start=False, stop=False)
                        pe.matmul(psv(4, n), qi[:, 1, n, :], S[:, 2 * n + 1, :], start=False, stop=True).then_inc(o_ok, 1)
                    pe.wait_ge(og_ok, h * NT + NT)
                    for e in range(2):
                        for n in range(NT):
                            last = pe.transpose(ps[:, 6 + e, n * P:(n + 1) * P], og[:, n, e * P:(e + 1) * P], ident[:])
                        last.then_inc(o_turned, 1)

                steps(pe, GLA_H, step)


def swa_heads(nc, hh, hl, qT, kT, v, ident, drams):
    w_dram, qg_dram, kg_dram, cos_dram, sin_dram = drams
    NH = GRP + 1
    with Phase(nc, "sh") as ph:
        raw = ph.sb("raw", [P, KD, SWA_COLS])
        wh = [ph.sb(f"wh{i}", [P, KD, SWA_COLS], F32R) for i in range(2)]
        wl = [ph.sb(f"wl{i}", [P, KD, SWA_COLS], F32R) for i in range(2)]
        gain = ph.sb("gain", [P, NH, HD])
        cos = ph.sb("cos", [P, NT, ROPE_HALF])
        sin = ph.sb("sin", [P, NT, ROPE_HALF])
        pj = ph.sb("pj", [P, NT, NH, HD])
        sq = ph.sb("sq", [P, NT, NH, HD])
        ss, ms, rt, rs = (ph.sb(n, [P, NT * NH]) for n in ("ss", "ms", "rt", "rs"))
        qk = ph.sb("qk", [P, NT, NH + 1, HD])
        ro = [ph.sb(f"ro{i}", [P, NT, NH, ROPE_HALF]) for i in range(4)]
        ps = ph.psum()
        names = ("small_in raw_in w_hi w_lo proj sq_ok pj_ok v_ok ss_ok ms_ok root_ok rs_ok normed gained r1 roped dup "
                 "turned qk_sb").split()
        (small_in, raw_in, w_hi, w_lo, proj, sq_ok, pj_ok, v_ok, ss_ok, ms_ok, root_ok, rs_ok, normed, gained, r1, roped,
         dup, turned, qk_sb) = (ph.sem(n) for n in names)
        x1, x2 = qk[:, :, 0:NH, 0:ROPE_HALF], qk[:, :, 0:NH, ROPE_HALF:2 * ROPE_HALF]
        cosb = cos[:].unsqueeze(2).broadcast_to([P, NT, NH, ROPE_HALF])
        sinb = sin[:].unsqueeze(2).broadcast_to([P, NT, NH, ROPE_HALF])
        heads = range(SWA_KV)

        with nc.Block() as block:
            @block.sync
            def _(sp):
                sp.dma_start(raw[:], w_dram[0]).then_inc(raw_in, 16)
                for g in range(GRP):
                    sp.dma_start(gain[:, g, :], qg_dram.partition_broadcast(P)).then_inc(small_in, 16)
                sp.dma_start(gain[:, GRP, :], kg_dram.partition_broadcast(P)).then_inc(small_in, 16)
                for dst, src in ((cos, cos_dram), (sin, sin_dram)):
                    sp.dma_start(dst[:], src).then_inc(small_in, 16)
                for h in range(1, SWA_KV):
                    sp.wait_ge(w_hi, h)
                    sp.wait_ge(w_lo, h)
                    sp.dma_start(raw[:], w_dram[h]).then_inc(raw_in, 16)

            @block.scalar
            def _(act):
                def split(h):
                    act.wait_ge(raw_in, 16 * (h + 1))
                    if h >= 2:
                        act.wait_ge(proj, (h - 1) * NT)
                    act.activation(wh[h % 2][:], raw[:], ACT.Copy).then_inc(w_hi, 1)

                def keep(h):
                    act.wait_ge(turned, h + 1)
                    for j in range(2):
                        act.activation(qT[:, h, j, :], ps[:, 4 + j, :], ACT.Copy)
                    act.activation(kT[:, h, :], ps[:, 6, :], ACT.Copy).then_inc(qk_sb, 1)

                split(0)
                split(1)
                for h in heads:
                    for n in range(NT):
                        act.wait_ge(proj, h * NT + n + 1)
                        after(act, ss_ok, h)
                        act.activation(flat(sq[:, n, :, :]), ps[:, n, 0:NH * HD], ACT.Square).then_inc(sq_ok, 1)
                        act.activation(v[:, h, n, :], ps[:, n, NH * HD:SWA_COLS], ACT.Copy).then_inc(v_ok, 1)
                        after(act, normed, h)
                        act.activation(flat(pj[:, n, :, :]), ps[:, n, 0:NH * HD], ACT.Copy).then_inc(pj_ok, 1)
                    act.wait_ge(ms_ok, h + 1)
                    act.activation(rt[:], ms[:], ACT.Sqrt).then_inc(root_ok, 1)
                    if h:
                        keep(h - 1)
                    if h + 2 < SWA_KV:
                        split(h + 2)
                keep(SWA_KV - 1)

            @block.gpsimd
            def _(pool):
                for h in range(1, SWA_KV):
                    pool.wait_ge(w_hi, h + 1)
                    pool.tensor_tensor(wl[h % 2][:], raw[:], wh[h % 2][:].bitcast(F32), ALU.subtract).then_inc(w_lo, 1)

            @block.vector
            def _(dve):
                dve.wait_ge(w_hi, 1)
                dve.tensor_tensor(wl[0][:], raw[:], wh[0][:].bitcast(F32), ALU.subtract).then_inc(w_lo, 1)
                dve.wait_ge(small_in, 16 * (GRP + 3))
                for h in heads:
                    dve.wait_ge(sq_ok, h * NT + NT)
                    dve.tensor_reduce(ss[:], sq[:].rearrange("p a b c -> p (a b) c"), AX_X, ALU.add).then_inc(ss_ok, 1)
                    dve.wait_ge(ss_ok, h + 1)
                    dve.tensor_scalar(ms[:], ss[:], 1.0 / HD, EPS, ALU.mult, ALU.add).then_inc(ms_ok, 1)
                    dve.wait_ge(root_ok, h + 1)
                    dve.reciprocal(rs[:], rt[:]).then_inc(rs_ok, 1)
                    dve.wait_ge(rs_ok, h + 1)
                    dve.wait_ge(pj_ok, (h + 1) * NT)
                    after(dve, turned, h)
                    dve.tensor_tensor(qk[:, :, 0:NH, :], pj[:], rs[:].rearrange("p (a b) -> p a b", a=NT).unsqueeze(3)
                                      .broadcast_to([P, NT, NH, HD]), ALU.mult).then_inc(normed, 1)
                    dve.wait_ge(normed, h + 1)
                    dve.tensor_tensor(qk[:, :, 0:NH, :], qk[:, :, 0:NH, :],
                                      gain[:].unsqueeze(1).broadcast_to([P, NT, NH, HD]), ALU.mult).then_inc(gained, 1)
                    dve.wait_ge(gained, h + 1)
                    dve.tensor_tensor(ro[0][:], x1, cosb, ALU.mult)
                    dve.tensor_tensor(ro[1][:], x2, sinb, ALU.mult)
                    dve.tensor_tensor(ro[2][:], x2, cosb, ALU.mult)
                    dve.tensor_tensor(ro[3][:], x1, sinb, ALU.mult).then_inc(r1, 1)
                    dve.wait_ge(r1, h + 1)
                    dve.tensor_tensor(x1, ro[0][:], ro[1][:], ALU.subtract)
                    dve.tensor_tensor(x2, ro[2][:], ro[3][:], ALU.add).then_inc(roped, 1)
                    dve.wait_ge(roped, h + 1)
                    dve.tensor_copy(qk[:, :, NH, :], qk[:, :, NH - 1, :]).then_inc(dup, 1)

            @block.tensor
            def _(pe):
                def project(h):
                    pe.wait_ge(w_hi, h + 1)
                    pe.wait_ge(w_lo, h + 1)
                    for n in range(NT):
                        if h:
                            pe.wait_ge(pj_ok, (h - 1) * NT + n + 1)
                        rows = slice(n * P, (n + 1) * P)
                        for k in range(KD):
                            last = mm3(pe, ps[:, n, 0:SWA_COLS], (hh[:, k, rows], hl[:, k, rows]),
                                       (wh[h % 2][:, k, :], wl[h % 2][:, k, :]), k == 0, k == KD - 1)
                        last.then_inc(proj, 1)

                project(0)
                for h in heads:
                    if h + 1 < SWA_KV:
                        project(h + 1)
                    pe.wait_ge(dup, h + 1)
                    after(pe, qk_sb, h)
                    for j in range(3):
                        for n in range(NT):
                            last = pe.transpose(ps[:, 4 + j, n * P:(n + 1) * P], flat(qk[:, n, 2 * j:2 * j + 2, :]), ident[:])
                    last.then_inc(turned, 1)


def swa_attend(nc, qT, kT, v, ob, ident, drams):
    mask_dram, sinks_dram = drams
    W = 2 * P
    U = SWA_KV * NT
    SLOTS = 4
    with Phase(nc, "swa") as ph:
        mask = ph.sb("mask", [P, W])
        sinks = ph.sb("sinks", [P, SWA_KV, GRP])
        sc = ph.sb("sc", [P, SLOTS, GRP, W])
        mx, m, nm, sd, se, den, dn, rd = (ph.sb(n, [P, U, GRP]) for n in ("mx", "m", "nm", "sd", "se", "den", "dn", "rd"))
        pT = ph.sb("pT", [P, 2, 2, T])
        ps = ph.psum()
        names = "small_in scored masked mx_ok m_ok negm sd_ok exp_ok se_ok dn_ok rd_ok p_ok p_turned pT_ok pv_ok ob_hi ob_lo"
        (small_in, scored, masked, mx_ok, m_ok, negm, sd_ok, exp_ok, se_ok, dn_ok, rd_ok, p_ok, p_turned, pT_ok, pv_ok,
         ob_hi, ob_lo) = (ph.sem(n) for n in names.split())

        def sight(u):
            return slice(0, W) if u % NT else slice(P, W)

        with nc.Block() as block:
            @block.sync
            def _(sp):
                sp.dma_start(sinks[:], sinks_dram.partition_broadcast(P)).then_inc(small_in, 16)
                sp.dma_start(mask[:], mask_dram).then_inc(small_in, 16)

            @block.scalar
            def _(act):
                def exps(u):
                    c = sight(u)
                    act.wait_ge(negm, u + 1)
                    for s in range(GRP):
                        last = act.activation(sc[:, u % SLOTS, s, c], sc[:, u % SLOTS, s, c], ACT.Exp,
                                              bias=nm[:, u, s:s + 1], accum_out=den[:, u, s:s + 1])
                    last.then_inc(exp_ok, 1)
                    act.wait_ge(sd_ok, u + 1)
                    act.activation(se[:, u, :], sd[:, u, :], ACT.Exp).then_inc(se_ok, 1)

                exps(0)
                exps(1)
                for u in range(U):
                    h, n, b = u // NT, u % NT, u % 2
                    act.wait_ge(p_turned, u + 1)
                    if u >= 2:
                        act.wait_ge(pv_ok, u - 1)
                    for half in range(0 if n else 1, 2):
                        last = act.activation(pT[:, b, half, :], ps[:, 4 + 2 * b + half, :], ACT.Copy)
                    last.then_inc(pT_ok, 1)
                    if u + 2 < U:
                        exps(u + 2)
                    act.wait_ge(pv_ok, u + 1)
                    for odd in range(2):
                        last = act.activation(ob[0][odd * HD:(odd + 1) * HD, 2 * h:2 * h + 2, n * P:(n + 1) * P],
                                              ps[0:HD, 4 + 2 * b, odd * W:(odd + 1) * W].rearrange("p (a b) -> p a b", a=2),
                                              ACT.Copy)
                    last.then_inc(ob_hi, 1)

            @block.gpsimd
            def _(pool):
                for u in range(U):
                    c = sight(u)
                    pool.wait_ge(rd_ok, u + 1)
                    pool.tensor_tensor(sc[:, u % SLOTS, :, c], sc[:, u % SLOTS, :, c],
                                       rd[:, u, :].unsqueeze(2).broadcast_to([P, GRP, c.stop - c.start]),
                                       ALU.mult).then_inc(p_ok, 1)

            @block.vector
            def _(dve):
                def soft(u):
                    h, b, c, i = u // NT, u % 2, sight(u), u + 1
                    dve.wait_ge(scored, i)
                    if u >= SLOTS:
                        dve.wait_ge(p_turned, i - SLOTS)
                    dve.scalar_tensor_tensor(sc[:, u % SLOTS, :, c],
                                             ps[:, 2 * b:2 * b + 2, :].rearrange("p a (s w) -> p (a s) w", s=2)[:, :, c],
                                             HD ** -0.5, mask[:, c].unsqueeze(1).broadcast_to([P, GRP, c.stop - c.start]),
                                             ALU.mult, ALU.add).then_inc(masked, 1)
                    dve.wait_ge(masked, i)
                    dve.tensor_reduce(mx[:, u, :], sc[:, u % SLOTS, :, c], AX_X, ALU.max).then_inc(mx_ok, 1)
                    dve.wait_ge(mx_ok, i)
                    dve.tensor_tensor(m[:, u, :], mx[:, u, :], sinks[:, h, :], ALU.max).then_inc(m_ok, 1)
                    dve.wait_ge(m_ok, i)
                    dve.tensor_scalar(nm[:, u, :], m[:, u, :], -1.0, None, ALU.mult).then_inc(negm, 1)
                    dve.tensor_tensor(sd[:, u, :], sinks[:, h, :], m[:, u, :], ALU.subtract).then_inc(sd_ok, 1)

                def total(u):
                    dve.wait_ge(se_ok, u + 1)
                    dve.tensor_tensor(dn[:, u, :], den[:, u, :], se[:, u, :], ALU.add).then_inc(dn_ok, 1)
                    dve.wait_ge(dn_ok, u + 1)
                    dve.reciprocal(rd[:, u, :], dn[:, u, :]).then_inc(rd_ok, 1)

                dve.wait_ge(small_in, 32)
                soft(0)
                soft(1)
                total(0)
                for u in range(U):
                    h, n, b = u // NT, u % NT, u % 2
                    if u + 1 < U:
                        total(u + 1)
                    if u + 2 < U:
                        soft(u + 2)
                    dve.wait_ge(ob_hi, u + 1)
                    for odd in range(2):
                        rows = slice(odd * HD, (odd + 1) * HD)
                        last = dve.tensor_tensor(ob[1][rows, 2 * h:2 * h + 2, n * P:(n + 1) * P],
                                                 ps[0:HD, 4 + 2 * b, odd * W:(odd + 1) * W].rearrange("p (a b) -> p a b", a=2),
                                                 ob[0][rows, 2 * h:2 * h + 2, n * P:(n + 1) * P].bitcast(F32),
                                                 ALU.subtract)
                    last.then_inc(ob_lo, 1)

            @block.tensor
            def _(pe):
                def score(u):
                    h, n, b, c = u // NT, u % NT, u % 2, sight(u)
                    if u >= 2:
                        pe.wait_ge(masked, u - 1)
                    keys = slice((n - 1) * P, (n + 1) * P) if n else slice(0, P)
                    for s in range(GRP):
                        half = slice((s // 2) * HD, (s // 2 + 1) * HD)
                        last = pe.matmul(ps[:, 2 * b + s // 2, (s % 2) * W:(s % 2 + 1) * W][:, c],
                                         qT[half, h, s % 2, n * P:(n + 1) * P], kT[half, h, keys], start=True, stop=True)
                    last.then_inc(scored, 1)

                score(0)
                score(1)
                for u in range(U):
                    h, n, b = u // NT, u % NT, u % 2
                    pe.wait_ge(p_ok, u + 1)
                    if u >= 2:
                        pe.wait_ge(ob_lo, u - 1)
                    for half in range(0 if n else 1, 2):
                        for s in range(GRP):
                            last = pe.transpose(ps[:, 4 + 2 * b + half, s * P:(s + 1) * P],
                                                sc[:, u % SLOTS, s, half * P:(half + 1) * P], ident[:])
                    last.then_inc(p_turned, 1)
                    if u + 2 < U:
                        score(u + 2)
                    pe.wait_ge(pT_ok, u + 1)
                    if n:
                        pe.matmul(ps[0:HD, 4 + 2 * b, :], v[:, h, n - 1, :], pT[:, b, 0, :], start=True, stop=False)
                    pe.matmul(ps[0:HD, 4 + 2 * b, :], v[:, h, n, :], pT[:, b, 1, :], start=(n == 0),
                              stop=True).then_inc(pv_ok, 1)


def merge(nc, hh, hl, oa, ob, mt, w_dram):
    with Phase(nc, "mrg") as ph:
        raw = [ph.sb(f"raw{u}", [P, 2, KD, P]) for u in range(2)]
        wh = [ph.sb(f"wh{u}", [P, 2, KD, P], F32R) for u in range(2)]
        wl = [ph.sb(f"wl{u}", [P, 2, KD, P], F32R) for u in range(2)]
        sg = [ph.sb(f"sg{u}", [P, T]) for u in range(2)]
        pr = [ph.sb(f"pr{u}", [P, T]) for u in range(2)]
        mv = ph.sb("mv", [P, T])
        ps = ph.psum()
        raw_in, w_hi, w_lo, gemm, sig_ok, prod, sum_ok, mt_hi, mt_lo = (
            [ph.sem(f"{n}{u}") for u in range(2)] for n in
            ("raw_in", "w_hi", "w_lo", "gemm", "sig_ok", "prod", "sum_ok", "mt_hi", "mt_lo"))
        sum_ok, mt_hi, mt_lo = sum_ok[0], mt_hi[0], mt_lo[0]
        with nc.Block() as block:
            @block.sync
            def _(sp):
                def step(j):
                    for u in range(2):
                        after(sp, w_hi[u], j)
                        after(sp, w_lo[u], j)
                        sp.dma_start(raw[u][:], w_dram[j, u]).then_inc(raw_in[u], 16)
                steps(sp, KD, step)

            @block.scalar
            def _(act):
                def split(j, u):
                    act.wait_ge(raw_in[u], 16 * (j + 1))
                    after(act, gemm[u], 2 * j)
                    act.activation(wh[u][:], raw[u][:], ACT.Copy).then_inc(w_hi[u], 1)

                def step(j):
                    for u in range(2):
                        act.wait_ge(gemm[u], 2 * j + 1)
                        after(act, prod[u], j)
                        act.activation(sg[u][:], ps[:, 2 * u, :], ACT.Sigmoid).then_inc(sig_ok[u], 1)
                        if j is not KD - 1:
                            split(j + 1, u)
                    act.wait_ge(sum_ok, j + 1)
                    act.activation(mt[0][:, j, :], mv[:], ACT.Copy).then_inc(mt_hi, 1)

                split(0, 0)
                split(0, 1)
                steps(act, KD, step)

            @block.vector
            def _(dve):
                def split(j, u):
                    dve.wait_ge(w_hi[u], j + 1)
                    dve.tensor_tensor(wl[u][:], raw[u][:], wh[u][:].bitcast(F32), ALU.subtract).then_inc(w_lo[u], 1)

                def step(j):
                    for u in range(2):
                        dve.wait_ge(sig_ok[u], j + 1)
                        dve.wait_ge(gemm[u], 2 * j + 2)
                        dve.tensor_tensor(pr[u][:], sg[u][:], ps[:, 2 * u + 1, :], ALU.mult).then_inc(prod[u], 1)
                        if j is not KD - 1:
                            split(j + 1, u)
                    dve.wait_ge(prod[0], j + 1)
                    dve.wait_ge(prod[1], j + 1)
                    dve.tensor_tensor(mv[:], pr[0][:], pr[1][:], ALU.add).then_inc(sum_ok, 1)
                    dve.wait_ge(mt_hi, j + 1)
                    dve.tensor_tensor(mt[1][:, j, :], mv[:], mt[0][:, j, :].bitcast(F32), ALU.subtract).then_inc(mt_lo, 1)

                split(0, 0)
                split(0, 1)
                steps(dve, KD, step)

            @block.tensor
            def _(pe):
                def step(j):
                    for u, branch in ((0, oa), (1, ob)):
                        pe.wait_ge(w_hi[u], j + 1)
                        pe.wait_ge(w_lo[u], j + 1)
                        after(pe, prod[u], j)
                        for half, moving in ((0, (hh, hl)), (1, branch)):
                            for k in range(KD):
                                last = mm3(pe, ps[:, 2 * u + half, :], (wh[u][:, half, k, :], wl[u][:, half, k, :]),
                                           (moving[0][:, k, :], moving[1][:, k, :]), k == 0, k == KD - 1)
                            last.then_inc(gemm[u], 1)
                steps(pe, KD, step)


def out_projection(nc, tag, src, kt, w_dram, res_dram, x, store, post_gain=None):
    CB = 256
    NB = D // CB
    with Phase(nc, tag) as ph:
        raw = ph.sb("raw", [P, kt, CB])
        wh = [ph.sb(f"wh{u}", [P, kt, CB], F32R) for u in range(2)]
        wl = [ph.sb(f"wl{u}", [P, kt, CB], F32R) for u in range(2)]
        ss, ms, rt, rs = (ph.sb(n, [P, NT]) for n in ("ss", "ms", "rt", "rs"))
        ps = ph.psum()
        STEP = kt // 4

        def parts(blk):
            return [slice(i, i + STEP) for i in range(0, kt, STEP)] if blk == 0 else [slice(0, kt)]

        first_in = [ph.sem(f"first_in{q}") for q in range(4)]
        first_hi, first_lo, ss_ok, x_even = (ph.sem(n) for n in ("first_hi", "first_lo", "ss_ok", "x_even"))
        names = "res_in gain_in raw_in w_hi w_lo gemm y_ok sq_ok ms_ok root_ok rs_ok scaled gained x_ok stored".split()
        (res_in, gain_in, raw_in, w_hi, w_lo, gemm, y_ok, sq_ok, ms_ok, root_ok, rs_ok, scaled, gained, x_ok,
         stored) = (ph.sem(n) for n in names)
        if post_gain is not None:
            gain = ph.sb("gain", [P, D])
            res = flat(raw[:]).rearrange("p (n d) -> p n d", n=NT)
            junk = ph.sb("junk", [P, NT, CB])
            ssb = ph.sb("ssb", [P, NT, NB])
        with nc.Block() as block:
            @block.sync
            def _(sp):
                for blk in range(NB):
                    if blk:
                        sp.wait_ge(w_hi, blk)
                        sp.wait_ge(w_lo, blk)
                    for q, part in enumerate(parts(blk)):
                        sp.dma_start(raw[:, part, :], w_dram[blk][:, part, :]).then_inc(raw_in if blk else first_in[q], 16)
                    if blk == 0 and post_gain is None:
                        sp.dma_start(x[:], res_dram.rearrange("(n p) d -> p n d", p=P)).then_inc(res_in, 16)
                if post_gain is not None:
                    sp.dma_start(gain[:], post_gain.partition_broadcast(P)).then_inc(gain_in, 16)
                    sp.wait_ge(w_hi, NB)
                    sp.wait_ge(w_lo, NB)
                    sp.dma_start(res, res_dram.rearrange("(n p) d -> p n d", p=P)).then_inc(res_in, 16)
                for n in range(NT):
                    if post_gain is None:
                        sp.wait_ge(x_ok, (NB - 1) * NT + n + 1)
                    else:
                        sp.wait_ge(x_ok if n % 2 else x_even, n // 2 + 1)
                    sp.dma_start(store[n * P:(n + 1) * P, :], x[:, n, :]).then_inc(stored, 16)
                sp.wait_ge(stored, 16 * NT)

            @block.scalar
            def _(act):
                def squares(blk):
                    for n in range(NT):
                        act.wait_ge(y_ok, blk * NT + n + 1)
                        if blk:
                            act.wait_ge(sq_ok, (blk - 1) * NT + n + 1)
                        act.activation(junk[:, n, :], x[:, n, blk * CB:(blk + 1) * CB], ACT.Square,
                                       accum_out=ssb[:, n, blk:blk + 1]).then_inc(sq_ok, 1)

                for blk in range(NB):
                    if blk:
                        act.wait_ge(raw_in, 16 * blk)
                    if blk >= 2:
                        act.wait_ge(gemm, (blk - 1) * NT)
                    for q, part in enumerate(parts(blk)):
                        if blk == 0:
                            act.wait_ge(first_in[q], 16)
                        done = w_hi if part.stop == kt else first_hi
                        act.activation(wh[blk % 2][:, part, :], raw[:, part, :], ACT.Copy).then_inc(done, 1)
                    if post_gain is not None and blk >= 2:
                        squares(blk - 2)
                if post_gain is not None:
                    squares(NB - 2)
                    squares(NB - 1)
                    act.wait_ge(ms_ok, 1)
                    act.activation(rt[:], ms[:], ACT.Sqrt).then_inc(root_ok, 1)

            if post_gain is not None:
                @block.gpsimd
                def _(pool):
                    pool.wait_ge(res_in, 16)
                    for n in range(0, NT, 2):
                        pool.wait_ge(scaled, n + 1)
                        pool.tensor_tensor(x[:, n, :], x[:, n, :], res[:, n, :], ALU.add).then_inc(x_even, 1)

            @block.vector
            def _(dve):
                def split(blk):
                    for q, part in enumerate(parts(blk)):
                        if part.stop == kt:
                            dve.wait_ge(w_hi, blk + 1)
                        else:
                            dve.wait_ge(first_hi, q + 1)
                        done = w_lo if part.stop == kt else first_lo
                        dve.tensor_tensor(wl[blk % 2][:, part, :], raw[:, part, :], wh[blk % 2][:, part, :].bitcast(F32),
                                          ALU.subtract).then_inc(done, 1)

                split(0)
                split(1)
                if post_gain is None:
                    dve.wait_ge(res_in, 16)
                for blk in range(NB):
                    for n in range(NT):
                        dve.wait_ge(gemm, blk * NT + n + 1)
                        cols = slice(blk * CB, (blk + 1) * CB)
                        bank = ps[:, blk % 2 * 4 + n, 0:CB]
                        if post_gain is None:
                            dve.tensor_tensor(x[:, n, cols], bank, x[:, n, cols], ALU.add).then_inc(x_ok, 1)
                        else:
                            dve.tensor_copy(x[:, n, cols], bank).then_inc(y_ok, 1)
                    if blk + 2 < NB:
                        split(blk + 2)
                if post_gain is not None:
                    dve.wait_ge(sq_ok, NB * NT)
                    dve.tensor_reduce(ss[:], ssb[:], AX_X, ALU.add).then_inc(ss_ok, 1)
                    dve.wait_ge(ss_ok, 1)
                    dve.tensor_scalar(ms[:], ss[:], 1.0 / D, EPS, ALU.mult, ALU.add).then_inc(ms_ok, 1)
                    dve.wait_ge(root_ok, 1)
                    dve.reciprocal(rs[:], rt[:]).then_inc(rs_ok, 1)
                    dve.wait_ge(rs_ok, 1)
                    dve.wait_ge(gain_in, 16)
                    for n in range(NT):
                        dve.scalar_tensor_tensor(x[:, n, :], x[:, n, :], rs[:, n:n + 1], gain[:], ALU.mult,
                                                 ALU.mult).then_inc(scaled, 1)
                        if n == 1:
                            dve.wait_ge(res_in, 16)
                        if n % 2:
                            dve.wait_ge(scaled, n + 1)
                            dve.tensor_tensor(x[:, n, :], x[:, n, :], res[:, n, :], ALU.add).then_inc(x_ok, 1)

            @block.tensor
            def _(pe):
                read = y_ok if post_gain is not None else x_ok
                for blk in range(NB):
                    if blk:
                        pe.wait_ge(w_hi, blk + 1)
                        pe.wait_ge(w_lo, blk + 1)
                    if blk >= 2:
                        pe.wait_ge(read, (blk - 1) * NT)
                    for n in range(NT):
                        rows = slice(n * P, (n + 1) * P)
                        for k in range(kt):
                            if blk == 0 and n == 0 and k % STEP == 0:
                                if k + STEP < kt:
                                    pe.wait_ge(first_hi, k // STEP + 1)
                                    pe.wait_ge(first_lo, k // STEP + 1)
                                else:
                                    pe.wait_ge(w_hi, 1)
                                    pe.wait_ge(w_lo, 1)
                            last = mm3(pe, ps[:, blk % 2 * 4 + n, 0:CB], (src[0][:, k, rows], src[1][:, k, rows]),
                                       (wh[blk % 2][:, k, :], wl[blk % 2][:, k, :]), k == 0, k == kt - 1)
                        last.then_inc(gemm, 1)


def route(nc, hh, hl, iT, jT, gT, ident, drams):
    w_dram, keys_dram, iota_dram = drams
    K2 = PEER_K * PEER_K
    LOW = -3.4e38
    with Phase(nc, "rt") as ph:
        raw = ph.sb("raw", [P, KD, 2 * P])
        wh = ph.sb("wh", [P, KD, 2 * P], F32R)
        wl = ph.sb("wl", [P, KD, 2 * P], F32R)
        keys = ph.sb("keys", [P, 2, NKEYS])
        iota = ph.sb("iota", [P, NKEYS])
        qp = ph.sb("qp", [P, 2, T])
        s0 = ph.sb("s0", [P, NT, 2, NKEYS])
        s1 = ph.sb("s1", [P, NT, 2, NKEYS])
        top = ph.sb("top", [P, NT, 2, PEER_K])
        idx = ph.sb("idx", [P, NT, 2, PEER_K], U32)
        idf = ph.sb("idf", [P, NT, 2, PEER_K])
        cand = ph.sb("cand", [P, NT, PEER_K, PEER_K])
        cand1 = ph.sb("cand1", [P, NT, K2])
        best = ph.sb("best", [P, NT, PEER_K])
        pos = ph.sb("pos", [P, NT, PEER_K], U32)
        part = ph.sb("part", [P, 2, NT, PEER_K], U32)
        partf = ph.sb("partf", [P, 2, NT, PEER_K])
        hot = [ph.sb(f"hot{i}", [P, NT, PEER_K, PEER_K]) for i in range(2)]
        sub = ph.sb("sub", [P, NT, PEER_K])
        ex = ph.sb("ex", [P, NT, PEER_K])
        den = ph.sb("den", [P, NT])
        rden = ph.sb("rden", [P, NT])
        nat = [ph.sb(f"nat{i}", [P, NT, P]) for i in range(3)]
        tick = ph.sb("tick", [P, 1])
        ps = ph.psum()
        names = ("small_in raw_in keys_in w_hi w_lo qp_ok qp_sb scored s0_ok m1 x1 r1 m2 x2 idf_ok cand_ok "
                 "cm1 cr1 cm2 cx part_ok partf_ok eq_ok hot_ok pick_ok sub_ok ex_ok den_ok rden_ok gate_ok turned out_ok").split()
        (small_in, raw_in, keys_in, w_hi, w_lo, qp_ok, qp_sb, scored, s0_ok, m1, x1, r1, m2, x2, idf_ok, cand_ok,
         cm1, cr1, cm2, cx, part_ok, partf_ok, eq_ok, hot_ok, pick_ok, sub_ok, ex_ok, den_ok, rden_ok, gate_ok,
         turned, out_ok) = (ph.sem(n) for n in names)
        pairs = [(n, p) for n in range(NT) for p in range(2)]

        grid = [P, NT, PEER_K, PEER_K]

        def bank(n, p):
            return ps[:, 2 + n // 2, (n % 2) * 2 * NKEYS + p * NKEYS:(n % 2) * 2 * NKEYS + (p + 1) * NKEYS]

        with nc.Block() as block:
            @block.sync
            def _(sp):
                sp.dma_start(raw[:], w_dram[0]).then_inc(raw_in, 16)
                sp.dma_start(keys[:], keys_dram[0]).then_inc(keys_in, 16)
                sp.dma_start(iota[:], iota_dram).then_inc(small_in, 16)
                with sp.Fori(0, PEER_H - 1) as h:
                    sp.wait_ge(w_hi, h + 1)
                    sp.wait_ge(w_lo, h + 1)
                    sp.dma_start(raw[:], w_dram[h + 1]).then_inc(raw_in, 16)
                    sp.wait_ge(scored, h + 1)
                    sp.dma_start(keys[:], keys_dram[h + 1]).then_inc(keys_in, 16)

            @block.scalar
            def _(act):
                def split(h):
                    act.wait_ge(raw_in, 16 * (h + 1))
                    act.activation(wh[:], raw[:], ACT.Copy).then_inc(w_hi, 1)

                split(0)

                def step(h):
                    act.wait_ge(qp_ok, h + 1)
                    after(act, scored, h)
                    for p in range(2):
                        last = act.activation(qp[:, p, :], ps[:, p, :], ACT.Copy)
                    last.then_inc(qp_sb, 1)
                    if h is not PEER_H - 1:
                        split(h + 1)
                    act.wait_ge(scored, h + 1)
                    after(act, r1, h)
                    after(act, x1, h)
                    for half in range(2):
                        last = act.activation(s0[:, 2 * half:2 * half + 2, :, :].rearrange("p a b c -> p (a b c)"),
                                              ps[:, 2 + half, :], ACT.Copy)
                    last.then_inc(s0_ok, 1)
                    act.wait_ge(sub_ok, h + 1)
                    act.activation(ex[:], sub[:], ACT.Exp).then_inc(ex_ok, 1)

                steps(act, PEER_H, step)
                for i, dst in enumerate((iT, jT, gT)):
                    act.wait_ge(turned, i + 1)
                    act.activation(dst[:], ps[:, i, :], ACT.Copy).then_inc(out_ok, 1)

            @block.gpsimd
            def _(pool):
                def step(h):
                    if h is not PEER_H - 1:
                        pool.wait_ge(w_hi, h + 2)
                        pool.tensor_tensor(wl[:], raw[:], wh[:].bitcast(F32), ALU.subtract).then_inc(w_lo, 1)
                    pool.wait_ge(m2, h + 1)
                    pool.tensor_tensor(cand[:], top[:, :, 0, :].unsqueeze(3).broadcast_to(grid),
                                       top[:, :, 1, :].unsqueeze(2).broadcast_to(grid), ALU.add).then_inc(cand_ok, 1)
                    pool.wait_ge(eq_ok, h + 1)
                    for p in range(2):
                        last = pool.tensor_tensor(hot[p][:], hot[p][:], idf[:, :, p, :].unsqueeze(2).broadcast_to(grid),
                                                  ALU.mult)
                    last.then_inc(hot_ok, 1)
                steps(pool, PEER_H, step)

            @block.vector
            def _(dve):
                dve.wait_ge(w_hi, 1)
                dve.tensor_tensor(wl[:], raw[:], wh[:].bitcast(F32), ALU.subtract).then_inc(w_lo, 1)
                dve.wait_ge(small_in, 16)

                def pick(h):
                    dve.wait_ge(hot_ok, h + 1)
                    for p in range(2):
                        last = dve.tensor_reduce(nat[p][:, :, bass.ds(h * PEER_K, PEER_K)], hot[p][:], AX_X, ALU.add)
                    last.then_inc(pick_ok, 1)

                def step(h):
                    dve.wait_ge(s0_ok, h + 1)
                    dve.tensor_copy(tick[:], iota[:, 0:1])
                    for n, p in pairs:
                        last = dve.max(top[:, n, p, 0:8], s0[:, n, p, :])
                    last.then_inc(m1, 1)
                    dve.wait_ge(m1, h + 1)
                    dve.tensor_copy(tick[:], iota[:, 0:1])
                    for n, p in pairs:
                        last = dve.max_index(idx[:, n, p, 0:8], top[:, n, p, 0:8], s0[:, n, p, :])
                    last.then_inc(x1, 1)
                    for n, p in pairs:
                        last = dve.match_replace(s1[:, n, p, :], top[:, n, p, 0:8], s0[:, n, p, :], LOW)
                    last.then_inc(r1, 1)
                    dve.wait_ge(r1, h + 1)
                    dve.tensor_copy(tick[:], iota[:, 0:1])
                    for n, p in pairs:
                        last = dve.max(top[:, n, p, 8:16], s1[:, n, p, :])
                    last.then_inc(m2, 1)
                    dve.wait_ge(m2, h + 1)
                    dve.tensor_copy(tick[:], iota[:, 0:1])
                    for n, p in pairs:
                        last = dve.max_index(idx[:, n, p, 8:16], top[:, n, p, 8:16], s1[:, n, p, :])
                    last.then_inc(x2, 1)
                    if not (isinstance(h, int) and h == 0):
                        pick(h - 1)
                    dve.wait_ge(x2, h + 1)
                    dve.tensor_copy(idf[:], idx[:]).then_inc(idf_ok, 1)
                    dve.wait_ge(cand_ok, h + 1)
                    dve.tensor_copy(tick[:], iota[:, 0:1])
                    flat_cand = cand[:].rearrange("p n a b -> p n (a b)")
                    for n in range(NT):
                        last = dve.max(best[:, n, 0:8], flat_cand[:, n, :])
                    last.then_inc(cm1, 1)
                    dve.wait_ge(cm1, h + 1)
                    dve.tensor_copy(tick[:], iota[:, 0:1])
                    for n in range(NT):
                        dve.max_index(pos[:, n, 0:8], best[:, n, 0:8], flat_cand[:, n, :])
                        last = dve.match_replace(cand1[:, n, :], best[:, n, 0:8], flat_cand[:, n, :], LOW)
                    last.then_inc(cr1, 1)
                    dve.wait_ge(cr1, h + 1)
                    dve.tensor_copy(tick[:], iota[:, 0:1])
                    for n in range(NT):
                        last = dve.max(best[:, n, 8:16], cand1[:, n, :])
                    last.then_inc(cm2, 1)
                    dve.wait_ge(cm2, h + 1)
                    after(dve, ex_ok, h)
                    dve.tensor_tensor(sub[:], best[:], best[:, :, 0:1].broadcast_to([P, NT, PEER_K]),
                                      ALU.subtract).then_inc(sub_ok, 1)
                    dve.tensor_copy(tick[:], iota[:, 0:1])
                    for n in range(NT):
                        last = dve.max_index(pos[:, n, 8:16], best[:, n, 8:16], cand1[:, n, :])
                    last.then_inc(cx, 1)
                    dve.wait_ge(cx, h + 1)
                    dve.tensor_scalar(part[:, 0, :, :], pos[:], 4, None, ALU.logical_shift_right)
                    dve.tensor_scalar(part[:, 1, :, :], pos[:], 15, None, ALU.bitwise_and).then_inc(part_ok, 1)
                    dve.wait_ge(part_ok, h + 1)
                    dve.tensor_copy(partf[:], part[:]).then_inc(partf_ok, 1)
                    dve.wait_ge(partf_ok, h + 1)
                    dve.wait_ge(idf_ok, h + 1)
                    for p in range(2):
                        last = dve.tensor_tensor(hot[p][:], partf[:, p, :, :].unsqueeze(3).broadcast_to(grid),
                                                 iota[:, 0:PEER_K].unsqueeze(1).unsqueeze(1).broadcast_to(grid), ALU.is_equal)
                    last.then_inc(eq_ok, 1)
                    dve.wait_ge(ex_ok, h + 1)
                    dve.tensor_reduce(den[:], ex[:], AX_X, ALU.add).then_inc(den_ok, 1)
                    dve.wait_ge(den_ok, h + 1)
                    dve.reciprocal(rden[:], den[:]).then_inc(rden_ok, 1)
                    dve.wait_ge(rden_ok, h + 1)
                    dve.tensor_tensor(nat[2][:, :, bass.ds(h * PEER_K, PEER_K)], ex[:],
                                      rden[:].unsqueeze(2).broadcast_to([P, NT, PEER_K]), ALU.mult).then_inc(gate_ok, 1)

                steps(dve, PEER_H, step)
                pick(PEER_H - 1)

            @block.tensor
            def _(pe):
                def step(h):
                    pe.wait_ge(w_hi, h + 1)
                    pe.wait_ge(w_lo, h + 1)
                    for p in range(2):
                        for k in range(KD):
                            last = mm3(pe, ps[:, p, :], (wh[:, k, p * P:(p + 1) * P], wl[:, k, p * P:(p + 1) * P]),
                                       (hh[:, k, :], hl[:, k, :]), k == 0, k == KD - 1)
                    last.then_inc(qp_ok, 1)
                    pe.wait_ge(qp_sb, h + 1)
                    pe.wait_ge(keys_in, 16 * (h + 1))
                    after(pe, s0_ok, h)
                    for n, p in pairs:
                        last = pe.matmul(bank(n, p), qp[:, p, n * P:(n + 1) * P], keys[:, p, :], start=True, stop=True)
                    last.then_inc(scored, 1)

                steps(pe, PEER_H, step)
                pe.wait_ge(gate_ok, PEER_H)
                pe.wait_ge(pick_ok, PEER_H)
                for i in range(3):
                    for n in range(NT):
                        last = pe.transpose(ps[:, i, n * P:(n + 1) * P], nat[i][:, n, :], ident[:])
                    last.then_inc(turned, 1)


def gate_matrix(nc, iT, jT, gT, iota_dram, g_dram, last_stage, stored, u_raw, u_dram, u_in):
    GT = P
    Q = 4
    POOLED = (1, 2)
    PER = GT // (2 * Q)
    with Phase(nc, "gm") as ph:
        iota = ph.sb("iota", [P, NKEYS])
        first = [ph.sb(f"first{u}", [P, Q, NKEYS]) for u in range(2)]
        second = [ph.sb(f"second{u}", [P, Q, NKEYS]) for u in range(2)]
        turn = ph.sb("turn", [P, 2])
        zero = ph.sb("zero", [P, 2 * Q])
        cols = ph.sb("cols", [P, 2 * Q])
        stage = [ph.sb("stage0", [P, NKEYS, GT]), last_stage]
        ps = ph.psum()
        zero_ok, iota_in, cols_ok = ph.sem("zero_ok"), ph.sem("iota_in"), ph.sem("cols_ok")
        rows_ok, pooled, built, staged = ([ph.sem(f"{n}{u}") for u in range(2)]
                                          for n in ("rows_ok", "pooled", "built", "staged"))
        groups = range(T // GT)

        def group_steps(eng, g, body):
            if g == 0:
                body(0, 0)
            with eng.Fori(0 if g else 1, PER) as q:
                body(g * PER + q, q)

        with nc.Block() as block:
            @block.sync
            def _(sp):
                sp.dma_start(iota[:], iota_dram).then_inc(iota_in, 16)
                sp.dma_start(u_raw[:], u_dram[0]).then_inc(u_in, 16)
                for g in groups:
                    for u in range(2):
                        sp.wait_ge(staged[u], (g + 1) * PER)
                    sp.dma_start(g_dram[g], stage[g % 2][:]).then_inc(stored[g % 2], 16)
                sp.wait_ge(stored[0], 16 * len(groups) // 2)

            @block.gpsimd
            def _(pool):
                pool.memset(zero[:], 0.0).then_inc(zero_ok, 1)
                pool.wait_ge(zero_ok, 1)
                pool.wait_ge(iota_in, 16)

                def body(it, q):
                    after(pool, pooled[1], it)
                    pool.tensor_tensor(cols[:], jT[:, bass.ds(it * (2 * Q), 2 * Q)], zero[:], ALU.add).then_inc(cols_ok, 1)
                    pool.wait_ge(cols_ok, it + 1)
                    for u in range(2):
                        after(pool, built[u], it)
                        pool.tensor_tensor(turn[:, u:u + 1], zero[:, 0:1], zero[:, 0:1], ALU.add)
                        for m in range(POOLED[u]):
                            last = pool.tensor_scalar(second[u][:, m, :], iota[:], cols[:, u * Q + m:u * Q + m + 1], None,
                                                      ALU.is_equal)
                        last.then_inc(pooled[u], 1)

                for g in groups:
                    group_steps(pool, g, body)

            @block.vector
            def _(dve):
                dve.wait_ge(iota_in, 16)

                def body(it, q):
                    for u in range(2):
                        after(dve, built[u], it)
                        for m in range(Q):
                            t = it * (2 * Q) + (u * Q + m)
                            last = dve.tensor_scalar(first[u][:, m, :], iota[:], iT[:, bass.ds(t, 1)],
                                                     gT[:, bass.ds(t, 1)], ALU.is_equal, ALU.mult)
                            if m >= POOLED[u]:
                                last = dve.tensor_scalar(second[u][:, m, :], iota[:], jT[:, bass.ds(t, 1)], None,
                                                         ALU.is_equal)
                        last.then_inc(rows_ok[u], 1)

                for g in groups:
                    group_steps(dve, g, body)

            @block.tensor
            def _(pe):
                def body(it, q):
                    for u in range(2):
                        pe.wait_ge(pooled[u], it + 1)
                        pe.wait_ge(rows_ok[u], it + 1)
                        after(pe, staged[u], it)
                        for m in range(Q):
                            last = pe.matmul(ps[:, u, m * P:(m + 1) * P], second[u][:, m, :], first[u][:, m, :],
                                             start=True, stop=True)
                        last.then_inc(built[u], 1)

                for g in groups:
                    group_steps(pe, g, body)

            @block.scalar
            def _(act):
                for g in groups:
                    if g >= 2:
                        act.wait_ge(stored[g % 2], 16 * (g // 2))

                    def body(it, q):
                        for u in range(2):
                            act.wait_ge(built[u], it + 1)
                            act.activation(stage[g % 2][:, :, bass.ds(q * (2 * Q) + u * Q, Q)],
                                           ps[:, u, :].rearrange("p (m i) -> p i m", m=Q), ACT.Copy).then_inc(staged[u], 1)
                    group_steps(act, g, body)


def experts(nc, hh, hl, x, u_dram, v_dram, g_dram, load, store, last_stage, gates_stored, u_raw, u_in):
    with Phase(nc, "ex") as ph:
        uh = ph.sb("uh", [P, KD, EB * P], F32R)
        ul = ph.sb("ul", [P, KD, EB * P], F32R)
        vh = ph.sb("vh", [P, EB, D], F32R)
        vl = ph.sb("vl", [P, EB, D], F32R)
        region = flat(last_stage[:])
        v_raw = region[:, 0:EB * D].rearrange("p (e d) -> p e d", e=EB)
        act_h, w, gate0, gate1 = (region[:, EB * D + i * EB * T:EB * D + (i + 1) * EB * T] for i in range(4))
        act_h, w = (r.rearrange("p (e t) -> p e t", e=EB) for r in (act_h, w))
        gate = [r.rearrange("p (g e t) -> p g e t", g=T // P, e=EB) for r in (gate0, gate1)]
        GATES = 16 * (T // P) // 2
        whi = ph.sb("whi", [P, EB, T], F32R)
        wlo = ph.sb("wlo", [P, EB, T], F32R)
        ps = ph.psum()
        names = "x_in v_in u_hi u_lo v_hi v_lo hid gelu_ok w_ok w_hi w_lo outp added stored".split()
        (x_in, v_in, u_hi, u_lo, v_hi, v_lo, hid, gelu_ok, w_ok, w_hi, w_lo, outp, added, stored) = (ph.sem(n) for n in names)
        g_in = [ph.sem(f"g_in{i}") for i in range(2)]
        PAIRS = NEB // 2

        def is_last(i, r):
            return i is PAIRS - 1 and r == 1

        with nc.Block() as block:
            @block.sync
            def _(sp):
                def step(i):
                    for r in range(2):
                        b = i * 2 + r
                        after(sp, u_hi, b)
                        after(sp, u_lo, b)
                        if not (isinstance(b, int) and b == 0):
                            sp.dma_start(u_raw[:], u_dram[b]).then_inc(u_in, 16)
                        if isinstance(i, int) and i == 0:
                            if r == 0:
                                sp.wait_ge(gates_stored, GATES)
                        else:
                            sp.wait_ge(w_ok, (b - 1) * EB)
                        sp.dma_start(gate[r], g_dram[:, :, bass.ds(b * EB, EB), :].rearrange("g j i t -> j g (i t)")
                                     ).then_inc(g_in[r], 16)
                        after(sp, v_hi, b)
                        after(sp, v_lo, b)
                        sp.dma_start(v_raw, v_dram[b]).then_inc(v_in, 16)
                        if isinstance(b, int) and b == 0:
                            sp.dma_start(x, load.rearrange("(n p) d -> p n d", p=P)).then_inc(x_in, 16)
                steps(sp, PAIRS, step)
                for n in range(NT):
                    sp.wait_ge(added, (NEB - 1) * 8 + 2 * n + 2)
                    sp.dma_start(store[n * P:(n + 1) * P, :], x[:, n, :]).then_inc(stored, 16)
                sp.wait_ge(stored, 16 * NT)

            @block.scalar
            def _(act):
                def split_u(b):
                    act.wait_ge(u_in, 16 * (b + 1))
                    act.activation(uh[:], u_raw[:], ACT.Copy).then_inc(u_hi, 1)

                def split_v(b):
                    act.wait_ge(v_in, 16 * (b + 1))
                    act.activation(vh[:], v_raw, ACT.Copy).then_inc(v_hi, 1)

                split_u(0)

                def step(i):
                    for r in range(2):
                        b = i * 2 + r
                        if isinstance(b, int) and b == 0:
                            act.wait_ge(gates_stored, GATES)
                        after(act, w_ok, b * EB)
                        for e in range(EB + 1):
                            if e < EB:
                                act.wait_ge(hid, b * EB + e + 1)
                                act.activation(act_h[:, e, :], ps[:, 4 * r + e, :], ACT.Gelu).then_inc(gelu_ok, 1)
                            if e:
                                act.wait_ge(w_ok, b * EB + e)
                                if e == 1:
                                    after(act, outp, b * 8)
                                act.activation(whi[:, e - 1, :], w[:, e - 1, :], ACT.Copy).then_inc(w_hi, 1)
                        if isinstance(b, int) and b == 0:
                            split_v(0)
                        if not is_last(i, r):
                            split_u(b + 1)
                            act.wait_ge(outp, b * 8 + 8)
                            split_v(b + 1)
                steps(act, PAIRS, step)

            @block.vector
            def _(dve):
                def split_u(b):
                    dve.wait_ge(u_hi, b + 1)
                    dve.tensor_tensor(ul[:], u_raw[:], uh[:].bitcast(F32), ALU.subtract).then_inc(u_lo, 1)

                def split_v(b):
                    dve.wait_ge(v_hi, b + 1)
                    dve.tensor_tensor(vl[:], v_raw, vh[:].bitcast(F32), ALU.subtract).then_inc(v_lo, 1)

                split_u(0)

                def step(i):
                    for r in range(2):
                        b = i * 2 + r
                        dve.wait_ge(g_in[r], 16 * (i + 1))
                        after(dve, w_hi, b * EB)
                        for e in range(EB):
                            dve.wait_ge(gelu_ok, b * EB + e + 1)
                            dve.tensor_tensor(w[:, e, :].rearrange("p (a b) -> p a b", a=T // P),
                                              act_h[:, e, :].rearrange("p (a b) -> p a b", a=T // P),
                                              gate[r][:, :, e, :], ALU.mult).then_inc(w_ok, 1)
                            dve.wait_ge(w_hi, b * EB + e + 1)
                            dve.tensor_tensor(wlo[:, e, :], w[:, e, :], whi[:, e, :].bitcast(F32),
                                              ALU.subtract).then_inc(w_lo, 1)
                        if isinstance(b, int) and b == 0:
                            split_v(0)
                            dve.wait_ge(x_in, 16)
                        if not is_last(i, r):
                            split_u(b + 1)
                        for o in range(8):
                            dve.wait_ge(outp, b * 8 + o + 1)
                            n, half = o // 2, o % 2
                            after(dve, added, b * 8)
                            dve.tensor_tensor(x[:, n, half * 512:(half + 1) * 512],
                                              ps[:, (4 * (1 - r) + o) % 8, :],
                                              x[:, n, half * 512:(half + 1) * 512], ALU.add).then_inc(added, 1)
                        if not is_last(i, r):
                            split_v(b + 1)
                steps(dve, PAIRS, step)

            @block.tensor
            def _(pe):
                def step(i):
                    for r in range(2):
                        b = i * 2 + r
                        pe.wait_ge(u_hi, b + 1)
                        pe.wait_ge(u_lo, b + 1)
                        for e in range(EB):
                            if e == 0:
                                if isinstance(b, int):
                                    after(pe, added, max(b * 8 - 4, 0))
                                else:
                                    pe.wait_ge(added, b * 8 - 4)
                            cols = slice(e * P, (e + 1) * P)
                            for k in range(KD):
                                last = mm3(pe, ps[:, 4 * r + e, :], (uh[:, k, cols], ul[:, k, cols]),
                                           (hh[:, k, :], hl[:, k, :]), k == 0, k == KD - 1)
                            last.then_inc(hid, 1)
                        pe.wait_ge(v_hi, b + 1)
                        pe.wait_ge(v_lo, b + 1)
                        after(pe, added, b * 8)
                        for turn in range(2):
                            if turn == 1:
                                pe.wait_ge(gelu_ok, b * EB + EB)
                            for first, some in ((True, range(EB - 1)), (False, range(EB - 1, EB))):
                                for o in range(4 * turn, 4 * turn + 4):
                                    n, half = o // 2, o % 2
                                    for e in some:
                                        if turn == 0 and o == 0:
                                            pe.wait_ge(w_lo, b * EB + e + 1)
                                        rows = slice(n * P, (n + 1) * P)
                                        cols = slice(half * 512, (half + 1) * 512)
                                        last = mm3(pe, ps[:, (4 * (1 - r) + o) % 8, :], (whi[:, e, rows], wlo[:, e, rows]),
                                                   (vh[:, e, cols], vl[:, e, cols]), e == 0, e == EB - 1)
                                    if not first:
                                        last.then_inc(outp, 1)
                steps(pe, PAIRS, step)


def gdn(nc, hh, hl, ot, ident, g_dram, sd_dram, drams):
    w_dram, b_dram, a_dram, conv_dram, alog_dram, dt_dram, gain_dram, reset_dram, masks_dram = drams
    KH, VH, NL = GDN_KH, GDN_VH, 6
    with Phase(nc, "gdn") as ph:
        raw = ph.sb("raw", [P, KD, 2 * P])
        wa = (ph.sb("wah", [P, KD, 2 * P], F32R), ph.sb("wal", [P, KD, 2 * P], F32R))
        wb = (ph.sb("wbh", [P, KD, 2 * P], F32R), ph.sb("wbl", [P, KD, 2 * P], F32R))
        cin = ph.sb("cin", [P, 4 * (T + 3)])
        cin4 = cin[:].rearrange("p (a b) -> p a b", a=4)
        cs = ph.sb("cs", [P, 4, T])
        conv = ph.sb("conv", [P, KH, 4, 4])
        gain = ph.sb("gain", [P, P])
        masks = ph.sb("masks", [P, NL + 2, P])
        cols = ph.sb("cols", [P, 4, NT, VH])
        cc = ph.sb("cc", [P, 4, NT, 2])
        be = ph.sb("be", [P, NT, 2])
        knq = ph.sb("knq", [P, 2, NT, P])
        kn, qn = knq[:, 0, :, :], knq[:, 1, :, :]
        knT = ph.sb("knT", [P, NT, P])
        qnT = ph.sb("qnT", [P, NT, P])
        kbg = ph.sb("kbg", [P, NT, 2, P])
        kdec = ph.sb("kdec", [P, NT, 2, P])
        vb = ph.sb("vb", [P, NT, 2, P])
        qd = ph.sb("qd", [P, NT, 2, P])
        qdT = ph.sb("qdT", [P, 2, NT, P])
        gz = ph.sb("gz", [P, 2 * T])
        dd = ph.sb("dd", [P, NT, 2, P])
        am = ph.sb("am", [P, NT, 2, P])
        qkt = ph.sb("qkt", [P, NT, 2, P])
        sdec = ph.sb("sdec", [P, 2, NCH])
        S = ph.sb("S", [P, 4, 2, P])
        ss, ms, rt, rs = (ph.sb(n, [P, 2, NT]) for n in ("ss", "ms", "rt", "rs"))
        os_, om, ort, ors = (ph.sb(n, [P, NT, 2]) for n in ("os", "om", "ort", "ors"))
        small = ph.sb("small", [VH, 4])
        ps = ph.psum()
        U = cin[:, 0:8 * P].rearrange("p (n a w) -> p n a w", n=NT, a=2)
        Tm = cin[:, 8 * P:16 * P].rearrange("p (n a w) -> p n a w", n=NT, a=2)
        Y = flat(cs[:])[:, 0:8 * P].rearrange("p (n a w) -> p n a w", n=NT, a=2)
        As = flat(cs[:])[:, 8 * P:16 * P].rearrange("p (n a w) -> p n a w", n=NT, a=2)
        vn, u, og = qd, dd, am
        wT = knq[:].rearrange("p a n w -> p (a n w)").rearrange("p (n a w) -> p n a w", n=NT, a=2)
        grow = gz[:].rearrange("p (a n w) -> p n a w", a=2, n=NT)
        zg = gz[:].rearrange("p (n b) -> p n b", n=NT)
        rows = [flat(cs[:])[0:VH, i * T:(i + 1) * T] for i in range(4)]
        rows += [kbg[:].rearrange("p a b c -> p (a b c)")[0:VH, i * T:(i + 1) * T] for i in range(2)]
        yrow, erow, grow_, beta, egrow, ekrow = rows
        reset = vb[:].rearrange("p a b c -> p (a b c)")[0:VH, 0:T]
        dlrow = vb[:].rearrange("p a b c -> p (a b c)")[0:VH, T:2 * T]
        sdrow = kdec[:].rearrange("p a b c -> p (a b c)")[0:VH, 0:NCH]

        names = ("small_in g_in raw_in a_hi a_lo b_hi b_lo zeroed pre_w pre_lo pre_mm row_v row_a row_t cols_ok stored "
                 "qk_ok v_ok z_ok cin_ok cc_ok be_ok tap silu_ok natural sq_ok ms_ok root_ok rs_ok kq_ok prods kq_turned kqT_ok "
                 "kk_ok kb_ok qd_turned qdT_ok dd_ok lim exp_ok masked prod2 a_ok t_ok t_turned u_ok as1_ok "
                 "u_mm u_sb w_sb vp_ok vn_ok ds_ok S_ok o_ok og_ok osq_ok om_ok oroot_ok ors_ok z_sb zg_ok normed "
                 "o_turned hi_ok lo_ok tz").split()
        s = {n: ph.sem(n) for n in names}
        (small_in, g_in, raw_in, a_hi, a_lo, b_hi, b_lo, zeroed, pre_w, pre_lo, pre_mm, row_v, row_a, row_t, cols_ok,
         stored, qk_ok, v_ok, z_ok, cin_ok, cc_ok, be_ok, tap, silu_ok, natural, sq_ok, ms_ok, root_ok, rs_ok, kq_ok,
         prods, kq_turned, kqT_ok, kk_ok, kb_ok, qd_turned, qdT_ok, dd_ok, lim, exp_ok, masked, prod2, a_ok, t_ok, t_turned,
         u_ok, as1_ok, u_mm, u_sb, w_sb, vp_ok, vn_ok, ds_ok, S_ok, o_ok, og_ok, osq_ok,
         om_ok, oroot_ok, ors_ok, z_sb, zg_ok, normed, o_turned, hi_ok, lo_ok, tz) = (s[n] for n in names)
        as_ok, y_mm, y_ok, u_mm_lv, t_mm_lv, u_up, t_up = (
            [ph.sem(f"{n}{half}") for half in range(2)]
            for n in ("as_ok", "y_mm", "y_ok", "u_mm_lv", "t_mm_lv", "u_up", "t_up"))
        full = [P, NT, 2, P]
        last_h = KH - 1

        def per(v):
            return v.unsqueeze(3).broadcast_to(full)

        def both(v):
            return v.unsqueeze(2).broadcast_to(full)

        def every(i):
            return masks[:, i, :].unsqueeze(1).unsqueeze(1).broadcast_to(full)

        def two(bank):
            return ps[:, bank:bank + 2, :].rearrange("p x (n a w) -> p (x n) a w", n=2, a=2)

        def cell(bank, n, a):
            return ps[:, bank + n // 2, ((n % 2) * 2 + a) * P:((n % 2) * 2 + a + 1) * P]

        def halved(ap, half):
            return ap[:, 2 * half:2 * half + 2, :, :]

        def some(half):
            return problems[4 * half:4 * half + 4]

        problems = [(n, a) for n in range(NT) for a in range(2)]

        with nc.Block() as block:
            @block.sync
            def _(sp):
                sp.dma_start(raw[:, :, 0:VH], b_dram).then_inc(small_in, 16)
                sp.dma_start(raw[:, :, P:P + VH], a_dram).then_inc(small_in, 16)
                sp.dma_start(small[:, 0:1], alog_dram).then_inc(small_in, 16)
                sp.dma_start(small[:, 1:2], dt_dram).then_inc(small_in, 16)
                sp.dma_start(conv[:], conv_dram).then_inc(small_in, 16)
                sp.dma_start(gain[:], gain_dram.partition_broadcast(P)).then_inc(small_in, 16)
                sp.dma_start(masks[:], masks_dram).then_inc(small_in, 16)
                sp.dma_start(reset, reset_dram[0:VH, :]).then_inc(small_in, 16)
                sp.wait_ge(pre_lo, 2)
                sp.dma_start(raw[:], w_dram[0, 0]).then_inc(raw_in, 16)
                sp.wait_ge(row_v, 6)
                sp.dma_start(g_dram, grow_).then_inc(stored, 16)
                sp.wait_ge(row_a, 7)
                sp.dma_start(sd_dram, sdrow).then_inc(stored, 16)
                sp.wait_ge(stored, 32)

                def values_and_gates(h):
                    sp.wait_ge(a_hi, 2 * h + 1)
                    sp.wait_ge(a_lo, 2 * h + 1)
                    sp.dma_start(raw[:], w_dram[h, 1]).then_inc(raw_in, 16)
                    sp.wait_ge(b_hi, h + 1)
                    sp.wait_ge(b_lo, h + 1)
                    sp.dma_start(raw[:], w_dram[h, 2]).then_inc(raw_in, 16)

                values_and_gates(0)

                def step(h):
                    after(sp, normed, h)
                    sp.dma_start(gz[:].rearrange("p (a b) -> p a b", a=2),
                                 g_dram[bass.ds(h * 2, 2), :].partition_broadcast(P)).then_inc(g_in, 16)
                    after(sp, S_ok, h * (NCH - 1))
                    sp.dma_start(sdec[:], sd_dram[bass.ds(h * 2, 2), :].partition_broadcast(P)).then_inc(g_in, 16)
                    if h is not last_h:
                        sp.wait_ge(a_hi, 2 * h + 2)
                        sp.wait_ge(a_lo, 2 * h + 2)
                        sp.dma_start(raw[:], w_dram[h + 1, 0]).then_inc(raw_in, 16)
                        values_and_gates(h + 1)
                steps(sp, KH, step)

            @block.gpsimd
            def _(pool):
                for w in (wa[0], wa[1], wb[0], wb[1]):
                    pool.memset(w[:].bitcast(F32)[:, :, 0:P], 0.0).then_inc(zeroed, 1)
                pool.wait_ge(small_in, 16 * 8)

                def low(w, hi_ok, lo_done, count):
                    pool.wait_ge(hi_ok, count)
                    pool.tensor_tensor(w[1][:], raw[:], w[0][:].bitcast(F32), ALU.subtract).then_inc(lo_done, 1)

                low(wa, a_hi, a_lo, 1)
                low(wb, b_hi, b_lo, 1)
                low(wa, a_hi, a_lo, 2)

                def step(h):
                    pool.wait_ge(kq_ok, 2 * h + 1)
                    pool.wait_ge(be_ok, h + 1)
                    pool.tensor_tensor(kbg[:], both(kn), per(be[:]), ALU.mult).then_inc(kb_ok, 1)
                    pool.tensor_tensor(kdec[:], both(kn), per(cc[:, 3, :, :]), ALU.mult).then_inc(kb_ok, 1)
                    pool.wait_ge(z_sb, h + 1)
                    pool.tensor_tensor(gz[:].rearrange("p (n w) -> p n w", w=P), gz[:].rearrange("p (n w) -> p n w", w=P),
                                       gain[:].unsqueeze(1).broadcast_to([P, 2 * NT, P]), ALU.mult).then_inc(zg_ok, 1)
                    if h is not last_h:
                        low(wa, a_hi, a_lo, 2 * h + 3)
                        low(wb, b_hi, b_lo, h + 2)
                        low(wa, a_hi, a_lo, 2 * h + 4)
                steps(pool, KH, step)

            @block.scalar
            def _(act):
                act.wait_ge(small_in, 16 * 8)
                act.wait_ge(zeroed, 4)
                act.activation(wa[0][:, :, 0:VH], raw[:, :, 0:VH], ACT.Copy).then_inc(pre_w, 1)
                act.activation(wb[0][:, :, 0:VH], raw[:, :, P:P + VH], ACT.Copy).then_inc(pre_w, 1)
                act.activation(small[:, 2:3], small[:, 0:1], ACT.Exp).then_inc(row_a, 1)
                act.wait_ge(pre_mm, 1)
                act.activation(beta, ps[0:VH, 6, :], ACT.Sigmoid).then_inc(row_a, 1)
                act.wait_ge(row_v, 2)
                act.activation(erow, erow, ACT.Exp).then_inc(row_a, 1)
                act.wait_ge(row_v, 3)
                act.activation(erow, erow, ACT.Ln).then_inc(row_a, 1)
                act.wait_ge(row_v, 7)
                act.activation(egrow, grow_, ACT.Exp).then_inc(row_a, 1)
                act.activation(ekrow, dlrow, ACT.Exp).then_inc(row_a, 1)
                act.activation(sdrow, grow_.rearrange("p (c w) -> p c w", c=NCH)[:, :, C - 1], ACT.Exp).then_inc(row_a, 1)
                act.wait_ge(row_t, 1)
                act.activation(cols[:].rearrange("p a b c -> p (a b c)"), ps[:, 5, 0:4 * NT * VH], ACT.Copy).then_inc(cols_ok, 1)

                def split_qk(h):
                    act.wait_ge(raw_in, 48 * h + 16)
                    act.activation(wa[0][:], raw[:], ACT.Copy).then_inc(a_hi, 1)

                def split_v(h):
                    act.wait_ge(raw_in, 48 * h + 32)
                    act.activation(wb[0][:], raw[:], ACT.Copy).then_inc(b_hi, 1)

                def split_z(h):
                    act.wait_ge(qk_ok, h + 1)
                    act.wait_ge(raw_in, 48 * h + 48)
                    act.activation(wa[0][:], raw[:], ACT.Copy).then_inc(a_hi, 1)

                act.wait_ge(pre_mm, 2)
                split_qk(0)
                split_v(0)
                split_z(0)

                def conv_in(h, p):
                    act.wait_ge((qk_ok, v_ok)[p], h + 1)
                    act.activation(cin4[:, 2 * p:2 * p + 2, 3:T + 3], ps[:, 2 * p:2 * p + 2, :], ACT.Copy).then_inc(cin_ok, 1)

                def silu(h):
                    for p in range(2):
                        act.wait_ge(tap, 10 * h + 5 * p + 5)
                        act.activation(flat(cs[:, 2 * p:2 * p + 2, :]), flat(cs[:, 2 * p:2 * p + 2, :]),
                                       ACT.Silu).then_inc(silu_ok, 1)

                conv_in(0, 0)
                conv_in(0, 1)
                silu(0)

                def step(h):
                    act.wait_ge(natural, 2 * h + 1)
                    after(act, u_mm, 2 * h)
                    for j in range(2):
                        for n in range(NT):
                            last = act.activation(kbg[:, n, j, :], ps[:, j, n * P:(n + 1) * P], ACT.Square,
                                                  accum_out=ss[:, j, n:n + 1])
                    last.then_inc(sq_ok, 1)
                    act.wait_ge(ms_ok, h + 1)
                    act.activation(rt[:], ms[:], ACT.Sqrt).then_inc(root_ok, 1)
                    act.wait_ge(lim, 2 * h + 2)
                    act.activation(am[:].rearrange("p a b c -> p (a b c)"), am[:].rearrange("p a b c -> p (a b c)"),
                                   ACT.Exp).then_inc(exp_ok, 1)
                    act.activation(qkt[:].rearrange("p a b c -> p (a b c)"), qkt[:].rearrange("p a b c -> p (a b c)"),
                                   ACT.Exp, scale=-1.0).then_inc(exp_ok, 1)
                    for j, dst in enumerate((knT, qnT)):
                        act.wait_ge(kq_turned, 2 * h + j + 1)
                        act.activation(flat(dst[:]), ps[:, 6 + j, :], ACT.Copy).then_inc(kqT_ok, 1)
                    act.wait_ge(qd_turned, h + 1)
                    for a in range(2):
                        last = act.activation(flat(qdT[:, a, :, :]), ps[:, a, :], ACT.Copy)
                    last.then_inc(qdT_ok, 1)
                    act.wait_ge(dd_ok, h + 1)
                    act.wait_ge(z_ok, h + 1)
                    for half in range(2):
                        last = act.activation(gz[:, half * T:(half + 1) * T], ps[:, 4 + half, :], ACT.Silu)
                    last.then_inc(z_sb, 1)
                    act.wait_ge(t_turned, h + 1)
                    for half in range(2):
                        act.activation(halved(U, half), halved(two(2), half), ACT.Copy).then_inc(u_ok, 1)
                    for lv in range(1, NL):
                        for half in range(2):
                            act.wait_ge(y_mm[half], h * (NL - 1) + lv)
                            act.activation(halved(Y, half), halved(two(0), half), ACT.Copy).then_inc(y_ok[half], 1)
                    if h is not last_h:
                        split_qk(h + 1)
                    act.wait_ge(u_mm, 2 * h + 1)
                    act.activation(u[:], two(0), ACT.Copy).then_inc(u_sb, 1)
                    act.wait_ge(u_mm, 2 * h + 2)
                    act.activation(wT, two(2), ACT.Copy).then_inc(w_sb, 1)
                    for n in range(NT):
                        act.wait_ge(o_ok, h * NT + n + 1)
                        for c in range(2):
                            part = slice(c * C, (c + 1) * C)
                            last = act.activation(og[part, n, :, :], ps[part, 6 + n % 2, c * 2 * P:(c + 1) * 2 * P].rearrange(
                                "p (a w) -> p a w", a=2), ACT.Copy)
                        last.then_inc(og_ok, 1)
                        if h is not last_h:
                            if n == 0:
                                split_v(h + 1)
                            if n == 1:
                                conv_in(h + 1, 0)
                            if n == 2:
                                split_z(h + 1)
                            if n == 3:
                                conv_in(h + 1, 1)
                    act.wait_ge(og_ok, h * NT + NT)
                    for n, a in problems:
                        last = act.activation(kdec[:, n, a, :], og[:, n, a, :], ACT.Square, accum_out=os_[:, n, a:a + 1])
                    last.then_inc(osq_ok, 1)
                    act.wait_ge(om_ok, h + 1)
                    act.activation(ort[:], om[:], ACT.Sqrt).then_inc(oroot_ok, 1)
                    if h is not last_h:
                        silu(h + 1)
                    act.wait_ge(o_turned, h + 1)
                    act.activation(ot[0][:, bass.ds(2 * h, 2), :], ps[:, 6:8, :], ACT.Copy).then_inc(hi_ok, 1)

                steps(act, KH, step)

            @block.vector
            def _(dve):
                dve.wait_ge(pre_w, 2)
                dve.tensor_tensor(wa[1][:, :, 0:VH], raw[:, :, 0:VH], wa[0][:, :, 0:VH].bitcast(F32), ALU.subtract).then_inc(pre_lo, 1)
                dve.tensor_tensor(wb[1][:, :, 0:VH], raw[:, :, P:P + VH], wb[0][:, :, 0:VH].bitcast(F32), ALU.subtract).then_inc(pre_lo, 1)
                dve.wait_ge(pre_mm, 2)
                dve.tensor_scalar(yrow, ps[0:VH, 7, :], small[:, 1:2], None, ALU.add).then_inc(tz, 1)
                dve.wait_ge(tz, 1)
                dve.tensor_scalar(erow, yrow, 0.0, 2.0, ALU.min, ALU.mult).then_inc(row_v, 1)
                dve.wait_ge(row_v, 1)
                dve.tensor_tensor(erow, erow, yrow, ALU.subtract).then_inc(row_v, 1)
                dve.wait_ge(row_a, 3)
                dve.tensor_scalar(erow, erow, 1.0, None, ALU.add).then_inc(row_v, 1)
                dve.wait_ge(row_a, 4)
                dve.scalar_tensor_tensor(yrow, yrow, 0.0, erow, ALU.max, ALU.add).then_inc(row_v, 1)
                dve.wait_ge(row_v, 4)
                dve.tensor_scalar(yrow, yrow, small[:, 2:3], -1.0, ALU.mult, ALU.mult).then_inc(row_v, 1)
                dve.wait_ge(row_v, 5)
                dve.tensor_tensor_scan(grow_, reset, yrow, 0.0, ALU.mult, ALU.add).then_inc(row_v, 1)
                dve.wait_ge(row_v, 6)
                g3 = grow_.rearrange("p (c w) -> p c w", c=NCH)
                dve.tensor_tensor(dlrow.rearrange("p (c w) -> p c w", c=NCH), g3[:, :, C - 1:C].broadcast_to([VH, NCH, C]),
                                  g3, ALU.subtract).then_inc(row_v, 1)
                dve.wait_ge(cols_ok, 1)

                def convolve(h, p):
                    base = 10 * h + 5 * p
                    dve.wait_ge(cin_ok, 2 * h + p + 1)
                    dve.memset(cin4[:, 2 * p:2 * p + 2, 0:3], 0.0).then_inc(tap, 1)
                    for j in range(4):
                        dve.wait_ge(tap, base + j + 1)
                        for g in range(2 * p, 2 * p + 2):
                            wj = conv[:, h, g, j:j + 1]
                            if j == 0:
                                last = dve.tensor_scalar(cs[:, g, :], cin4[:, g, 0:T], wj, None, ALU.mult)
                            else:
                                last = dve.scalar_tensor_tensor(cs[:, g, :], cin4[:, g, j:j + T], wj, cs[:, g, :],
                                                                ALU.mult, ALU.add)
                        last.then_inc(tap, 1)
                        yield

                for p in range(2):
                    for _ in convolve(0, p):
                        pass

                def step(h):
                    after(dve, kb_ok, 2 * h)
                    dve.tensor_copy(cc[:], cols[:, :, :, bass.ds(2 * h, 2)]).then_inc(cc_ok, 1)
                    dve.wait_ge(cc_ok, h + 1)
                    g_c, beta_c, eg_c, ek_c = (cc[:, i, :, :] for i in range(4))
                    dve.tensor_tensor(be[:], beta_c, eg_c, ALU.mult).then_inc(be_ok, 1)
                    dve.wait_ge(g_in, 32 * h + 32)
                    dve.tensor_tensor(dd[:], per(g_c), grow, ALU.subtract).then_inc(dd_ok, 1)
                    dve.wait_ge(dd_ok, h + 1)
                    after(dve, normed, h)
                    dve.tensor_scalar(am[:], dd[:], 0.0, None, ALU.min).then_inc(lim, 1)
                    dve.tensor_scalar(qkt[:], dd[:], 0.0, None, ALU.max).then_inc(lim, 1)
                    dve.wait_ge(sq_ok, h + 1)
                    dve.tensor_scalar(ms[:], ss[:], 1.0, EPS, ALU.mult, ALU.add).then_inc(ms_ok, 1)
                    dve.wait_ge(root_ok, h + 1)
                    dve.reciprocal(rs[:], rt[:]).then_inc(rs_ok, 1)
                    dve.wait_ge(rs_ok, h + 1)
                    shape = [P, NT, P]
                    dve.tensor_tensor(kn, ps[:, 1, :].rearrange("p (n w) -> p n w", n=NT),
                                      rs[:, 1, :].unsqueeze(2).broadcast_to(shape), ALU.mult).then_inc(kq_ok, 1)
                    dve.scalar_tensor_tensor(qn, ps[:, 0, :].rearrange("p (n w) -> p n w", n=NT), P ** -0.5,
                                             rs[:, 0, :].unsqueeze(2).broadcast_to(shape), ALU.mult, ALU.mult).then_inc(kq_ok, 1)
                    dve.wait_ge(kq_ok, 2 * h + 2)
                    dve.tensor_tensor(qd[:], both(qn), per(eg_c), ALU.mult).then_inc(prods, 1)
                    dve.wait_ge(natural, 2 * h + 2)
                    dve.tensor_tensor(vb[:], ps[:, 2:4, :].rearrange("p a (n w) -> p n a w", n=NT), per(beta_c),
                                      ALU.mult).then_inc(prods, 1)
                    dve.wait_ge(exp_ok, 2 * h + 2)
                    dve.tensor_tensor(am[:], am[:], every(0), ALU.mult).then_inc(masked, 1)
                    dve.wait_ge(masked, 2 * h + 1)
                    dve.tensor_tensor(am[:], am[:], per(beta_c), ALU.mult).then_inc(prod2, 1)
                    dve.wait_ge(kk_ok, h + 1)
                    dve.wait_ge(prod2, h + 1)
                    dve.tensor_tensor(am[:], am[:], both(ps[:, 6, :].rearrange("p (n w) -> p n w", n=NT)),
                                      ALU.mult).then_inc(a_ok, 1)
                    dve.wait_ge(a_ok, 2 * h + 1)
                    dve.tensor_tensor(As, am[:], every(2), ALU.mult).then_inc(as1_ok, 1)
                    dve.wait_ge(as1_ok, h + 1)
                    dve.tensor_tensor(Tm, ident[:].unsqueeze(1).unsqueeze(1).broadcast_to(full), As,
                                      ALU.subtract).then_inc(t_ok, 1)
                    dve.tensor_tensor(qkt[:], qkt[:], every(1), ALU.mult).then_inc(masked, 1)
                    dve.wait_ge(masked, 2 * h + 2)
                    dve.tensor_tensor(qkt[:], qkt[:], both(ps[:, 7, :].rearrange("p (n w) -> p n w", n=NT)),
                                      ALU.mult).then_inc(a_ok, 1)
                    dve.wait_ge(t_ok, h + 1)
                    dve.wait_ge(u_ok, 2 * h + 2)
                    for lv in range(1, NL):
                        base = h * (NL - 1) + lv
                        for half in range(2):
                            if lv > 1:
                                dve.wait_ge(y_mm[half], base - 1)
                            dve.tensor_tensor(halved(As, half), halved(am[:], half), halved(every(2 + lv), half),
                                              ALU.mult).then_inc(as_ok[half], 1)
                        for half in range(2):
                            dve.wait_ge(u_mm_lv[half], base)
                            dve.tensor_tensor(halved(U, half), halved(U, half), halved(two(2), half),
                                              ALU.subtract).then_inc(u_up[half], 1)
                        for half in range(2):
                            if lv < NL - 1:
                                dve.wait_ge(t_mm_lv[half], h * (NL - 2) + lv)
                                dve.tensor_tensor(halved(Tm, half), halved(Tm, half), halved(two(6), half),
                                                  ALU.subtract).then_inc(t_up[half], 1)
                    dve.wait_ge(u_sb, h + 1)
                    NS = NCH - 1
                    ahead = iter(()) if h is last_h else convolve(h + 1, 0)
                    for i in range(NCH):
                        n, part = i // 2, slice((i % 2) * C, (i % 2 + 1) * C)
                        if i >= 5:
                            next(ahead, None)
                        if i == 0:
                            dve.wait_ge(qd_turned, h + 1)
                            dve.tensor_copy(vn[part, n, :, :], u[part, n, :, :]).then_inc(vn_ok, 1)
                        else:
                            dve.wait_ge(vp_ok, h * NS + i)
                            dve.tensor_tensor(vn[part, n, :, :], u[part, n, :, :],
                                              ps[part, 4, 0:2 * P].rearrange("p (a w) -> p a w", a=2),
                                              ALU.subtract).then_inc(vn_ok, 1)
                        if i == NCH - 1:
                            break
                        dve.wait_ge(ds_ok, h * NS + i + 1)
                        if i == 0:
                            dve.tensor_copy(flat(S[:, 1, :, :]), ps[:, 5, 0:2 * P]).then_inc(S_ok, 1)
                        else:
                            dve.wait_ge(S_ok, h * NS + i)
                            if i >= 3:
                                dve.wait_ge(o_ok, h * NT + (i - 1) // 2)
                            for a in range(2):
                                last = dve.scalar_tensor_tensor(S[:, (i + 1) % 4, a, :], S[:, i % 4, a, :],
                                                                sdec[:, a, i:i + 1], ps[:, 5, a * P:(a + 1) * P],
                                                                ALU.mult, ALU.add)
                            last.then_inc(S_ok, 1)
                    for _ in ahead:
                        pass
                    if h is not last_h:
                        for _ in convolve(h + 1, 1):
                            pass
                    dve.wait_ge(osq_ok, h + 1)
                    dve.tensor_scalar(om[:], os_[:], 1.0 / P, EPS, ALU.mult, ALU.add).then_inc(om_ok, 1)
                    dve.wait_ge(oroot_ok, h + 1)
                    dve.reciprocal(ors[:], ort[:]).then_inc(ors_ok, 1)
                    dve.wait_ge(ors_ok, h + 1)
                    dve.tensor_tensor(og[:], og[:], per(ors[:]), ALU.mult).then_inc(tz, 1)
                    dve.wait_ge(tz, h + 2)
                    dve.wait_ge(zg_ok, h + 1)
                    dve.tensor_tensor(og[:], og[:], zg.rearrange("p n (a w) -> p n a w", a=2), ALU.mult).then_inc(normed, 1)
                    dve.wait_ge(hi_ok, h + 1)
                    dve.tensor_tensor(ot[1][:, bass.ds(2 * h, 2), :], ps[:, 6:8, :],
                                      ot[0][:, bass.ds(2 * h, 2), :].bitcast(F32), ALU.subtract).then_inc(lo_ok, 1)

                steps(dve, KH, step)

            @block.tensor
            def _(pe):
                pe.wait_ge(pre_lo, 2)
                for bank, w in ((6, wa), (7, wb)):
                    for k in range(KD):
                        last = mm3(pe, ps[:, bank, :], (w[0][:, k, 0:P], w[1][:, k, 0:P]), (hh[:, k, :], hl[:, k, :]),
                                   k == 0, k == KD - 1)
                    last.then_inc(pre_mm, 1)
                pe.wait_ge(row_a, 7)
                for i, row in enumerate((grow_, beta, egrow, ekrow)):
                    for n in range(NT):
                        last = pe.transpose(ps[:, 5, (i * NT + n) * VH:(i * NT + n + 1) * VH], row[:, n * P:(n + 1) * P],
                                            ident[0:VH, 0:VH])
                last.then_inc(row_t, 1)

                def project(h):
                    for bank, w, col, done in ((0, wa, 0, None), (1, wa, P, qk_ok), (2, wb, 0, None), (3, wb, P, v_ok)):
                        if bank == 0:
                            pe.wait_ge(a_hi, 2 * h + 1)
                            pe.wait_ge(a_lo, 2 * h + 1)
                        if bank == 2:
                            pe.wait_ge(b_hi, h + 1)
                            pe.wait_ge(b_lo, h + 1)
                        for k in range(KD):
                            last = mm3(pe, ps[:, bank, :], (w[0][:, k, col:col + P], w[1][:, k, col:col + P]),
                                       (hh[:, k, :], hl[:, k, :]), k == 0, k == KD - 1)
                            if k == KD - 1 and done is not None:
                                last.then_inc(done, 1)
                            yield

                def gate(h, tiles):
                    pe.wait_ge(a_hi, 2 * h + 2)
                    pe.wait_ge(a_lo, 2 * h + 2)
                    for n in tiles:
                        for k in range(KD):
                            rws = slice(n * P, (n + 1) * P)
                            last = mm3(pe, ps[:, 4 + n // 2, (n % 2) * 2 * P:(n % 2 + 1) * 2 * P],
                                       (hh[:, k, rws], hl[:, k, rws]), (wa[0][:, k, :], wa[1][:, k, :]), k == 0, k == KD - 1)
                        if n == NT - 1:
                            last.then_inc(z_ok, 1)

                def turn(h, p):
                    pe.wait_ge(silu_ok, 2 * h + p + 1)
                    for g in range(2 * p, 2 * p + 2):
                        for n in range(NT):
                            last = pe.transpose(ps[:, g, n * P:(n + 1) * P], cs[:, g, n * P:(n + 1) * P], ident[:])
                    last.then_inc(natural, 1)

                def step(h):
                    turn(h, 0)
                    if isinstance(h, int) and h == 0:
                        pe.wait_ge(cols_ok, 1)
                    gate(h, (2,))
                    turn(h, 1)
                    after(pe, lo_ok, h)
                    for j, src in enumerate((kn, qn)):
                        pe.wait_ge(kq_ok, 2 * h + j + 1)
                        for n in range(NT):
                            last = pe.transpose(ps[:, 6 + j, n * P:(n + 1) * P], src[:, n, :], ident[:])
                        last.then_inc(kq_turned, 1)
                    pe.wait_ge(kqT_ok, 2 * h + 2)
                    for j, src in enumerate((knT, qnT)):
                        for n in range(NT):
                            last = pe.matmul(ps[:, 6 + j, n * P:(n + 1) * P], knT[:, n, :], src[:, n, :], start=True, stop=True)
                    last.then_inc(kk_ok, 1)
                    pe.wait_ge(prods, 2 * h + 2)
                    for n, a in problems:
                        last = pe.transpose(ps[:, a, n * P:(n + 1) * P], qd[:, n, a, :], ident[:])
                    last.then_inc(qd_turned, 1)
                    gate(h, (3,))
                    pe.wait_ge(t_ok, h + 1)
                    for n, a in problems:
                        last = pe.transpose(cell(2, n, a), Tm[:, n, a, :], ident[:])
                    last.then_inc(t_turned, 1)
                    pe.wait_ge(u_ok, 2 * h + 2)
                    pe.wait_ge(qdT_ok, h + 1)
                    for lv in range(1, NL):
                        base = h * (NL - 1) + lv
                        for half in range(2):
                            pe.wait_ge(as_ok[half], base)
                            if lv > 1:
                                pe.wait_ge(u_up[half], base - 1)
                            for n, a in some(half):
                                last = pe.matmul(cell(0, n, a), As[:, n, a, :], U[:, n, a, :], start=True, stop=True)
                            last.then_inc(y_mm[half], 1)
                        for half in range(2):
                            pe.wait_ge(y_ok[half], base)
                            if lv > 1:
                                pe.wait_ge(t_up[half], h * (NL - 2) + lv - 1)
                            for n, a in some(half):
                                last = pe.matmul(cell(2, n, a), Tm[:, n, a, :], Y[:, n, a, :], start=True, stop=True)
                            last.then_inc(u_mm_lv[half], 1)
                        if lv < NL - 1:
                            if lv == 1:
                                pe.wait_ge(a_ok, 2 * h + 2)
                            for half in range(2):
                                for n, a in some(half):
                                    last = pe.matmul(cell(6, n, a), Y[:, n, a, :], Tm[:, n, a, :], start=True, stop=True)
                                last.then_inc(t_mm_lv[half], 1)
                    for half in range(2):
                        pe.wait_ge(u_up[half], h * (NL - 1) + NL - 1)
                    pe.wait_ge(kb_ok, 2 * h + 2)
                    for n, a in problems:
                        last = pe.matmul(cell(0, n, a), U[:, n, a, :], vb[:, n, a, :], start=True, stop=True)
                    last.then_inc(u_mm, 1)
                    for n, a in problems:
                        last = pe.matmul(cell(2, n, a), kbg[:, n, a, :], U[:, n, a, :], start=True, stop=True)
                    last.then_inc(u_mm, 1)
                    pe.wait_ge(z_sb, h + 1)
                    pe.wait_ge(w_sb, h + 1)
                    NS = NCH - 1
                    ahead = iter(()) if h is last_h else project(h + 1)

                    def fill(count):
                        for _ in zip(range(count), ahead):
                            pass

                    for i in range(NCH):
                        n, part = i // 2, slice((i % 2) * C, (i % 2 + 1) * C)
                        fill(2)
                        if i:
                            pe.wait_ge(S_ok, h * NS + i)
                            for a in range(2):
                                last = pe.matmul(ps[:, 4, a * P:(a + 1) * P], wT[:, n, a, :], S[:, i % 4, a, :],
                                                 start=True, stop=True)
                            last.then_inc(vp_ok, 1)
                        fill(2)
                        pe.wait_ge(vn_ok, h * NCH + i + 1)
                        if i < NS:
                            for a in range(2):
                                last = pe.matmul(ps[:, 5, a * P:(a + 1) * P], kdec[part, n, a, :], vn[part, n, a, :],
                                                 start=True, stop=True)
                            last.then_inc(ds_ok, 1)
                        if i % 2:
                            if n >= 2:
                                pe.wait_ge(og_ok, h * NT + n - 1)
                            for c in range(2):
                                for a in range(2):
                                    out = ps[:, 6 + n % 2, (c * 2 + a) * P:(c * 2 + a + 1) * P]
                                    inter = 2 * n + c > 0
                                    last = pe.matmul(out, qkt[:, n, a, :], vn[:, n, a, :], start=True, stop=not inter)
                                    if inter:
                                        last = pe.matmul(out, qdT[:, a, n, :], S[:, (2 * n + c) % 4, a, :], start=False, stop=True)
                            last.then_inc(o_ok, 1)
                    fill(4 * KD)
                    if h is not last_h:
                        gate(h + 1, (0, 1))
                    pe.wait_ge(normed, h + 1)
                    for n, a in problems:
                        last = pe.transpose(ps[:, 6 + a, n * P:(n + 1) * P], og[:, n, a, :], ident[:])
                    last.then_inc(o_turned, 1)

                for _ in project(0):
                    pass
                gate(0, (0, 1))
                steps(pe, KH, step)


def short_conv(nc, hh, hl, ot, drams):
    w_dram, conv_dram = drams
    N = SC_TILES
    with Phase(nc, "sc") as ph:
        raw = [ph.sb(f"raw{i}", [P, KD, 2 * P]) for i in range(2)]
        wh = [ph.sb(f"wh{i}", [P, KD, 2 * P], F32R) for i in range(2)]
        wl = [ph.sb(f"wl{i}", [P, KD, 2 * P], F32R) for i in range(2)]
        conv = ph.sb("conv", [P, N, 3])
        cg = ph.sb("cg", [P, T])
        cu = ph.sb("cu", [P, T + 2])
        acc = [ph.sb(f"acc{i}", [P, T]) for i in range(3)]
        sz = ph.sb("sz", [P, T])
        y = ph.sb("y", [P, T])
        yz = ph.sb("yz", [P, T])
        ps = ph.psum()
        conv_in, zeroed, cg_ok, cu_ok, tap, sz_ok, y_ok, yz_ok, hi_ok, lo_ok = (
            ph.sem(n) for n in ("conv_in", "zeroed", "cg_ok", "cu_ok", "tap", "sz_ok", "y_ok", "yz_ok", "hi_ok", "lo_ok"))
        raw_in, w_hi, w_lo, gemm = ([ph.sem(f"{n}{i}") for i in range(2)] for n in ("raw_in", "w_hi", "w_lo", "gemm"))
        with nc.Block() as block:
            @block.sync
            def _(sp):
                sp.dma_start(conv[:], conv_dram).then_inc(conv_in, 16)

                def step(j):
                    for i in range(2):
                        after(sp, w_hi[i], j)
                        after(sp, w_lo[i], j)
                        sp.dma_start(raw[i][:], w_dram[j, i]).then_inc(raw_in[i], 16)
                steps(sp, N, step)

            @block.scalar
            def _(act):
                def split(j, i):
                    act.wait_ge(raw_in[i], 16 * (j + 1))
                    after(act, gemm[i], 2 * j)
                    act.activation(wh[i][:], raw[i][:], ACT.Copy).then_inc(w_hi[i], 1)

                def step(j):
                    act.wait_ge(gemm[0], 2 * j + 2)
                    after(act, cu_ok, j)
                    act.activation(cg[:], ps[:, 1, :], ACT.Copy).then_inc(cg_ok, 1)
                    if j is not N - 1:
                        split(j + 1, 0)
                    act.wait_ge(gemm[1], 2 * j + 2)
                    after(act, yz_ok, j)
                    act.activation(sz[:], ps[:, 3, :], ACT.Silu).then_inc(sz_ok, 1)
                    if j is not N - 1:
                        split(j + 1, 1)
                    act.wait_ge(yz_ok, j + 1)
                    act.activation(ot[0][:, j, :], yz[:], ACT.Copy).then_inc(hi_ok, 1)

                split(0, 0)
                split(0, 1)
                steps(act, N, step)

            @block.vector
            def _(dve):
                def split(j, i):
                    dve.wait_ge(w_hi[i], j + 1)
                    dve.tensor_tensor(wl[i][:], raw[i][:], wh[i][:].bitcast(F32), ALU.subtract).then_inc(w_lo[i], 1)

                def step(j):
                    dve.wait_ge(cg_ok, j + 1)
                    dve.tensor_tensor(cu[:, 2:T + 2], cg[:], ps[:, 0, :], ALU.mult).then_inc(cu_ok, 1)
                    if j is not N - 1:
                        split(j + 1, 0)
                    dve.wait_ge(cu_ok, j + 1)
                    dve.tensor_scalar(acc[0][:], cu[:, 0:T], conv[:, j, 0:1], None, ALU.mult).then_inc(tap, 1)
                    for i in range(1, 3):
                        dve.wait_ge(tap, 3 * j + i)
                        dve.scalar_tensor_tensor(acc[i][:], cu[:, i:T + i], conv[:, j, i:i + 1], acc[i - 1][:],
                                                 ALU.mult, ALU.add).then_inc(tap, 1)
                    dve.wait_ge(tap, 3 * j + 3)
                    dve.wait_ge(sz_ok, j + 1)
                    dve.tensor_tensor(y[:], acc[2][:], ps[:, 2, :], ALU.mult).then_inc(y_ok, 1)
                    dve.wait_ge(y_ok, j + 1)
                    dve.tensor_tensor(yz[:], y[:], sz[:], ALU.mult).then_inc(yz_ok, 1)
                    if j is not N - 1:
                        split(j + 1, 1)
                    dve.wait_ge(hi_ok, j + 1)
                    dve.tensor_tensor(ot[1][:, j, :], yz[:], ot[0][:, j, :].bitcast(F32), ALU.subtract).then_inc(lo_ok, 1)

                dve.memset(cu[:, 0:2], 0.0).then_inc(zeroed, 1)
                dve.wait_ge(zeroed, 1)
                dve.wait_ge(conv_in, 16)
                split(0, 0)
                split(0, 1)
                steps(dve, N, step)

            @block.tensor
            def _(pe):
                def step(j):
                    for i in range(2):
                        pe.wait_ge(w_hi[i], j + 1)
                        pe.wait_ge(w_lo[i], j + 1)
                        after(pe, (cu_ok, y_ok)[i], j)
                        for half in range(2):
                            for k in range(KD):
                                cols = slice(half * P, (half + 1) * P)
                                last = mm3(pe, ps[:, 2 * i + half, :], (wh[i][:, k, cols], wl[i][:, k, cols]),
                                           (hh[:, k, :], hl[:, k, :]), k == 0, k == KD - 1)
                            last.then_inc(gemm[i], 1)
                steps(pe, N, step)


def second_block(nc, sb, ident, hh, hl, a, x2_dram, grow_dram, sd_dram, x3_dram, out):
    with ExitStack() as o:
        ot = (sb("oth", [P, 2 * KD, T], F32R, o), sb("otl", [P, 2 * KD, T], F32R, o))
        gdn(nc, hh, hl, ot, ident, grow_dram, sd_dram,
            [a[n] for n in ("gdn_w", "gdn_b", "gdn_a", "gdn_conv", "a_log", "dt_bias", "gdn_gain", "reset", "gdn_masks")])
        xo = sb("x3", [P, NT, D], F32, o)
        out_projection(nc, "go", ot, 2 * KD, a["gdn_wo"], x2_dram, xo, x3_dram, a["post_gain0"])
        norm_transposed(nc, "n4", xo, a["pre_gain1"], ident, hh, hl)
        short_conv(nc, hh, hl, ot, (a["sc_w"], a["sc_conv"]))
        out_projection(nc, "so", ot, 2 * KD, a["sc_wo"], x3_dram, xo, out, a["post_gain1"])


def program(nc, a, out):
    x1_dram = nc.dram_tensor("x1_scratch", (T, D), F32, kind="Internal").ap()
    x2_dram = nc.dram_tensor("x2_scratch", (T, D), F32, kind="Internal").ap()
    x3_dram = nc.dram_tensor("x3_scratch", (T, D), F32, kind="Internal").ap()
    grow_dram = nc.dram_tensor("g_scratch", (GDN_VH, T), F32, kind="Internal").ap()
    sd_dram = nc.dram_tensor("sd_scratch", (GDN_VH, NCH), F32, kind="Internal").ap()
    g_dram = nc.dram_tensor("gate_scratch", (T // P, NKEYS, NKEYS, P), F32, kind="Internal").ap()
    with ExitStack() as top:
        def sb(name, shape, dt=F32, ctx=top):
            return ctx.enter_context(nc.sbuf_tensor(name, shape, dt))
        ident = sb("ident", [P, P])
        hh = sb("hh", [P, KD, T], F32R)
        hl = sb("hl", [P, KD, T], F32R)
        ident_in = nc.alloc_semaphore("ident_in")
        with nc.Block() as block:
            @block.sync
            def _(sp):
                sp.dma_start(ident[:], a["ident"]).then_inc(ident_in, 16)
                sp.wait_ge(ident_in, 16)
        with nc.sbuf_tensor("x_in", [P, NT, D], F32) as x:
            norm_transposed(nc, "n1", x, a["mix_gain"], ident, hh, hl, load_from=a["x"])
        with ExitStack() as mix:
            oa = (sb("oah", [P, KD, T], F32R, mix), sb("oal", [P, KD, T], F32R, mix))
            gla(nc, hh, hl, oa, ident, [a[n] for n in ("gla_w", "glr_w", "gk2", "bgk", "gla_gain", "tri", "reset")])
            ob = (sb("obh", [P, KD, T], F32R, mix), sb("obl", [P, KD, T], F32R, mix))
            with ExitStack() as sw:
                qT = sb("qT", [P, SWA_KV, 2, T], F32, sw)
                kT = sb("kT", [P, SWA_KV, T], F32, sw)
                v = sb("v", [P, SWA_KV, NT, HD], F32, sw)
                swa_heads(nc, hh, hl, qT, kT, v, ident, [a[n] for n in ("swa_w", "qg", "kg", "cos", "sin")])
                swa_attend(nc, qT, kT, v, ob, ident, (a["mask"], a["sinks"]))
            mt = (sb("mth", [P, KD, T], F32R, mix), sb("mtl", [P, KD, T], F32R, mix))
            merge(nc, hh, hl, oa, ob, mt, a["mrg_w"])
            with ExitStack() as o:
                xo = sb("xo", [P, NT, D], F32, o)
                out_projection(nc, "wo", mt, KD, a["wo_w"], a["x"], xo, x1_dram)
                norm_transposed(nc, "n2", xo, a["ffn_gain"], ident, hh, hl)
        with ExitStack() as peer:
            gx = peer.enter_context(Phase(nc, "gx"))
            last_stage = gx.sb("last_stage", [P, NKEYS, P])
            x = flat(last_stage[:])[:, NKEYS * P - NT * D:NKEYS * P].rearrange("p (n d) -> p n d", n=NT)
            u_raw, u_in = gx.sb("u_raw", [P, KD, EB * P]), gx.sem("u_in")
            gates_stored = [gx.sem(f"stored{u}") for u in range(2)]
            with ExitStack() as rt:
                iT, jT, gT = (sb(n, [P, T], F32, rt) for n in ("iT", "jT", "gT"))
                route(nc, hh, hl, iT, jT, gT, ident, (a["pq_w"], a["keys"], a["iota"]))
                gate_matrix(nc, iT, jT, gT, a["iota"], g_dram, last_stage, gates_stored,
                            u_raw, a["u_w"], u_in)
            experts(nc, hh, hl, x, a["u_w"], a["v_w"], g_dram, x1_dram, x2_dram, last_stage,
                    gates_stored[1], u_raw, u_in)
            norm_transposed(nc, "n3", x, a["pre_gain0"], ident, hh, hl)
        second_block(nc, sb, ident, hh, hl, a, x2_dram, grow_dram, sd_dram, x3_dram, out)


OUT = ("out", (T, D))


def finish(r):
    return r.reshape(1, T, D)


def columns(v):
    return v.reshape(-1, P).T


def k_major(w, cols):
    return w[:, cols].reshape(-1, P, len(cols)).transpose(1, 0, 2)


def laid_out(i):
    ar = np.arange
    splits = np.cumsum([0, 512, 512, 1024, 1024, 16, 1024, 256, 256, 1024, 1024])
    gq, gk, gv, gr, glr, sq, sk, sv, ga, gb = splits[:10]
    w = i["w_in"][0]
    a = {"x": i["x"][0], "ident": np.eye(P, dtype=np.float32), "mix_gain": columns(i["norm_mix_g"][0])}
    a["gla_w"] = np.stack([k_major(w, np.concatenate([gq + h * 128 + ar(128), gk + h * 128 + ar(128),
                                                      gv + h * 256 + ar(256), gr + h * 256 + ar(256)]))
                           for h in range(GLA_H)])
    a["glr_w"] = k_major(w, glr + ar(GLA_R))
    a["gk2"] = i["w_gk2"][0]
    a["bgk"] = columns(i["b_gk"][0])
    a["gla_gain"] = i["gla_norm_g"][0]
    a["tri"] = np.tile(np.triu(np.ones((C, C), np.uint32)), (2, 1))
    a["reset"] = np.tile((ar(T) % C != 0).astype(np.float32), (P, 1))
    a["swa_w"] = np.stack([k_major(w, np.concatenate([sq + h * 256 + ar(256), sk + h * 64 + ar(64), sv + h * 64 + ar(64)]))
                           for h in range(SWA_KV)])
    a["qg"], a["kg"] = i["q_norm_g"][0], i["k_norm_g"][0]
    pos = ar(T, dtype=np.float32)
    inv_freq = np.float32(500000.0) ** (-ar(0, 16, 2, dtype=np.float32) / np.float32(16))
    ang = pos[:, None] * inv_freq[None, :]
    for n, f in (("cos", np.cos), ("sin", np.sin)):
        a[n] = f(ang).astype(np.float32).reshape(NT, P, ROPE_HALF).transpose(1, 0, 2)
    q, k = ar(P)[:, None] + P, ar(2 * P)[None, :]
    a["mask"] = np.where((q - k >= 0) & (q - k < P), 0.0, NEG).astype(np.float32)
    a["sinks"] = i["attn_sinks"][0].reshape(SWA_KV, GRP)[:, [0, 2, 1, 3]]
    wa, wb = i["w_branch_a"][0], i["w_branch_b"][0]
    a["mrg_w"] = np.stack([np.stack([np.stack([k_major(w, g + j * P + ar(P)), k_major(br, j * P + ar(P))], axis=1)
                                     for g, br in ((ga, wa), (gb, wb))]) for j in range(KD)])
    a["wo_w"] = np.stack([k_major(i["w_out"][0], j * 256 + ar(256)) for j in range(4)])
    a["ffn_gain"] = columns(i["norm_ffn_g"][0])
    a["pq_w"] = np.stack([k_major(i["w_peer_q"][0], h * 256 + ar(256)) for h in range(PEER_H)])
    a["keys"] = i["peer_sub_keys"][0].transpose(0, 3, 1, 2)
    a["iota"] = np.tile(ar(NKEYS, dtype=np.float32), (P, 1))
    a["u_w"] = i["peer_u"][0].reshape(NEB, EB * P, KD, P).transpose(0, 3, 2, 1)
    a["v_w"] = i["peer_v"][0].reshape(NEB, EB, P, D).transpose(0, 2, 1, 3)
    a["pre_gain0"], a["pre_gain1"] = (columns(i["pre_norm_w_2"][l]) for l in range(2))
    a["post_gain0"], a["post_gain1"] = (i["post_norm_w_2"][l] for l in range(2))
    w, c = i["gdn_w_in_2"][0], i["gdn_conv_w_2"][0]
    kw, vw = GDN_KH * P, GDN_VH * P
    a["gdn_w"] = np.stack([np.stack([
        k_major(w, np.concatenate([h * P + ar(P), kw + h * P + ar(P)])),
        k_major(w, 2 * kw + 2 * h * P + ar(2 * P)),
        k_major(w, 2 * kw + vw + 2 * h * P + ar(2 * P))]) for h in range(GDN_KH)])
    a["gdn_b"] = k_major(w, 2 * kw + 2 * vw + ar(GDN_VH))
    a["gdn_a"] = k_major(w, 2 * kw + 2 * vw + GDN_VH + ar(GDN_VH))
    ch = np.stack([np.stack([h * P + ar(P), kw + h * P + ar(P), 2 * kw + 2 * h * P + ar(P),
                             2 * kw + (2 * h + 1) * P + ar(P)]) for h in range(GDN_KH)])
    a["gdn_conv"] = c[:, ch].transpose(3, 1, 2, 0)
    a["a_log"], a["dt_bias"] = i["gdn_A_log_2"][0][:, None], i["gdn_dt_bias_2"][0][:, None]
    a["gdn_gain"] = i["gdn_norm_w_2"][0]
    r, q = ar(P)[:, None], ar(P)[None, :]
    same = r // C == q // C
    lv = [(r // (2 * s) == q // (2 * s)) & (r // s % 2 == 1) & (q // s % 2 == 0) for s in (1, 2, 4, 8, 16, 32)]
    a["gdn_masks"] = np.stack([same & (q < r), same & (r <= q)] + lv, axis=1).astype(np.float32)
    a["gdn_wo"] = np.stack([k_major(i["gdn_w_out_2"][0], j * 256 + ar(256)) for j in range(4)])
    w, sw = i["sc_w_in_2"][0], SC_TILES * P
    a["sc_w"] = np.stack([np.stack([k_major(w, np.concatenate([g * sw + j * P + ar(P) for g in pair]))
                                    for pair in ((0, 2), (1, 3))]) for j in range(SC_TILES)])
    a["sc_conv"] = i["sc_conv_w_2"][0].reshape(3, SC_TILES, P).transpose(2, 1, 0)
    a["sc_wo"] = np.stack([k_major(i["sc_w_out_2"][0], j * 256 + ar(256)) for j in range(4)])
    return {n: np.ascontiguousarray(v) for n, v in a.items()}


def kernel(**inputs):
    import concourse.bacc as bacc
    from concourse.bass_utils import run_bass_kernel_spmd

    nc = bacc.Bacc("TRN2", target_bir_lowering=False, num_devices=1)
    arrays = laid_out({n: np.asarray(v) for n, v in inputs.items()})
    aps = {n: nc.dram_tensor(f"in_{n}", v.shape, mybir.dt.from_np(v.dtype), kind="ExternalInput").ap()
           for n, v in arrays.items()}
    name, shape = OUT
    out = nc.dram_tensor(name, shape, F32, kind="ExternalOutput").ap()
    program(nc, aps, out)
    r = run_bass_kernel_spmd(nc, [{f"in_{n}": v for n, v in arrays.items()}], core_ids=[0])
    return finish(r.results[0][name])
```
